# Optimizing a Trainium2 kernel written in Bass

```python
import jax, jax.numpy as jnp
from jax import lax
import numpy as np

D_MODEL = 1024
BATCH = 1
SEQ = 256
DEPTH = 2
DEC_BATCH = 8
DEC_SEQ = 8
PAST_LEN = 2048
PAGE_SIZE = 128

N_A_LAYERS = DEPTH // 2
N_B_LAYERS = DEPTH - N_A_LAYERS
D_FF = 2816
CONV_W = 31
N_HEADS = 16
HEAD_DIM = D_MODEL // N_HEADS
N_KV = 4
GROUP = N_HEADS // N_KV
CMP_STRIDE = 16
L_CMP = 2 * CMP_STRIDE
CMP_HID = 128
SEL_BLK = 64
N_SELECT = 16
WINDOW = 512
W_BLK = 128
N_BAND = WINDOW // W_BLK + 1
SEL_QBLK = 16
N_KV_ROWS = 6
N_PAGED = 4
EPS = 1e-6
NEG = -1e30
FORCE = 1e9
F32 = jnp.float32

kernel_name = 'yoco_conformer_conv_nsa_step'

def rmsnorm(x, g):
    xf = x.astype(F32)
    y = xf * lax.rsqrt(jnp.mean(xf * xf, axis=-1, keepdims=True) + EPS)
    return (y * g.astype(F32)).astype(x.dtype)

def swiglu(h, w_in, w_out):
    a, b = jnp.split(h @ w_in, 2, axis=-1)
    return (jax.nn.silu(a) * b) @ w_out

def masked_softmax(s, mask):
    s = jnp.where(mask, s, NEG)
    m = jnp.max(s, axis=-1, keepdims=True)
    e = jnp.exp(s - m) * mask
    return e / jnp.maximum(jnp.sum(e, axis=-1, keepdims=True), 1e-30)

def conv_module(h, prev, w_pw1, w_dw, b_dw, ln_g, ln_b, w_pw2):
    a, b = jnp.split(h @ w_pw1, 2, axis=-1)
    v = a * jax.nn.sigmoid(b)
    full = jnp.concatenate([prev.astype(v.dtype), v], axis=1)
    c = lax.conv_general_dilated(full, w_dw[:, None, :].astype(full.dtype), (1,), 'VALID',
                                 dimension_numbers=('NWC', 'WIO', 'NWC'),
                                 feature_group_count=D_MODEL) + b_dw
    cf = c.astype(F32)
    mu = jnp.mean(cf, axis=-1, keepdims=True)
    var = jnp.mean(jnp.square(cf - mu), axis=-1, keepdims=True)
    n = ((cf - mu) * lax.rsqrt(var + EPS) * ln_g.astype(F32) + ln_b.astype(F32)).astype(c.dtype)
    return jax.nn.silu(n) @ w_pw2, full[:, full.shape[1] - (CONV_W - 1):]

def compress(rows, w1, b1, w2, b2, pe):
    B, T = rows.shape[:2]
    n16 = T // CMP_STRIDE
    ch = rows[:, :n16 * CMP_STRIDE].reshape(B, n16, CMP_STRIDE, N_KV, HEAD_DIM)
    first = jnp.einsum('bnsgd,sdh->bngh', ch, w1[:CMP_STRIDE])
    second = jnp.einsum('bnsgd,sdh->bngh', ch, w1[CMP_STRIDE:])
    z = first[:, :-1] + second[:, 1:] + (b1 + jnp.einsum('sd,sdh->h', pe, w1))
    return jax.nn.gelu(z) @ w2 + b2

def build_shared(kc_rows, vc_rows, ks_rows, vs_rows, w_cmp1, b_cmp1, w_cmp2, b_cmp2, pe_cmp):
    kc = compress(kc_rows, w_cmp1[0], b_cmp1[0], w_cmp2[0], b_cmp2[0], pe_cmp[0])
    vc = compress(vc_rows, w_cmp1[1], b_cmp1[1], w_cmp2[1], b_cmp2[1], pe_cmp[1])
    B, T = ks_rows.shape[:2]
    n_sel = -(-T // SEL_BLK)

    def blocks(r):
        r = jnp.pad(r, ((0, 0), (0, n_sel * SEL_BLK - T), (0, 0), (0, 0)))
        return r.reshape(B, n_sel, SEL_BLK, N_KV, HEAD_DIM).transpose(0, 3, 1, 2, 4)

    return {'kc': kc, 'vc': vc, 'kb': blocks(ks_rows), 'vb': blocks(vs_rows)}

def select_attend(q, qpos, idx, kb, vb, slopes):
    B = q.shape[0]
    scale = HEAD_DIM ** -0.5
    bi = jnp.arange(B)[:, None, None, None]
    gi = jnp.arange(N_KV)[None, :, None, None]
    kg = kb[bi, gi, idx]
    vg = vb[bi, gi, idx]
    kpos = idx[..., None] * SEL_BLK + jnp.arange(SEL_BLK)
    dist = (qpos[:, None, None] - kpos)[:, :, None]
    s = (jnp.einsum('bgzqd,bgqkld->bgzqkl', q, kg).astype(F32) * scale
         - slopes[None, :, :, None, None, None] * dist.astype(F32))
    shp = s.shape
    mask = (dist >= 0).reshape(B, N_KV, 1, shp[3], -1)
    p = masked_softmax(s.reshape(shp[0], shp[1], shp[2], shp[3], -1), mask).reshape(shp)
    return jnp.einsum('bgzqkl,bgqkld->bgzqd', p.astype(q.dtype), vg)

def window_banded(q, kw, vw, slopes):
    B, _, _, T, _ = q.shape
    scale = HEAD_DIM ** -0.5
    nb = T // W_BLK
    pad = ((0, 0), (WINDOW, 0), (0, 0), (0, 0))
    kp = jnp.pad(kw, pad).reshape(B, nb + N_BAND - 1, W_BLK, N_KV, HEAD_DIM)
    vp = jnp.pad(vw, pad).reshape(B, nb + N_BAND - 1, W_BLK, N_KV, HEAD_DIM)
    kband = jnp.concatenate([kp[:, i:i + nb] for i in range(N_BAND)], axis=2)
    vband = jnp.concatenate([vp[:, i:i + nb] for i in range(N_BAND)], axis=2)
    qb = q.reshape(B, N_KV, GROUP, nb, W_BLK, HEAD_DIM)
    r = jnp.arange(N_BAND * W_BLK)[None, :]
    dist = jnp.arange(W_BLK)[:, None] - r + WINDOW
    kpos = jnp.arange(nb)[:, None] * W_BLK - WINDOW + r
    mask = (dist >= 0) & (dist < WINDOW) & (kpos[:, None, :] >= 0)
    s = (jnp.einsum('bgzncd,bnkgd->bgznck', qb, kband).astype(F32) * scale
         - slopes[:, :, None, None, None] * dist.astype(F32))
    p = masked_softmax(s, mask)
    o = jnp.einsum('bgznck,bnkgd->bgzncd', p.astype(q.dtype), vband)
    return o.reshape(B, N_KV, GROUP, T, HEAD_DIM)

def window_dense(q, qpos, kw, vw, kpos, slopes):
    scale = HEAD_DIM ** -0.5
    dist = qpos[:, None] - kpos[None, :]
    mask = (dist >= 0) & (dist < WINDOW)
    s = (jnp.einsum('bgzqd,bkgd->bgzqk', q, kw).astype(F32) * scale
         - slopes[:, :, None, None] * dist.astype(F32))
    p = masked_softmax(s, mask)
    return jnp.einsum('bgzqk,bkgd->bgzqd', p.astype(q.dtype), vw)

def nsa_mixer(h, qpos, sh, w_qg, w_o, slopes, prompt):
    B, T = h.shape[:2]
    scale = HEAD_DIM ** -0.5
    proj = h @ w_qg
    q = proj[..., :N_HEADS * HEAD_DIM].reshape(B, T, N_KV, GROUP, HEAD_DIM).transpose(0, 2, 3, 1, 4)
    gates = jax.nn.sigmoid(proj[..., N_HEADS * HEAD_DIM:].astype(F32))
    gates = gates.reshape(B, T, 3, N_KV, GROUP).transpose(2, 0, 3, 4, 1)[..., None]
    kc, vc = sh['kc'], sh['vc']
    n_cmp = kc.shape[1]
    cend = jnp.arange(n_cmp) * CMP_STRIDE + (L_CMP - 1)
    dist_c = qpos[:, None] - cend[None, :]
    s_c = (jnp.einsum('bgzqd,bngd->bgzqn', q, kc).astype(F32) * scale
           - slopes[:, :, None, None] * dist_c.astype(F32))
    p_c = masked_softmax(s_c, dist_c >= 0)
    o_c = jnp.einsum('bgzqn,bngd->bgzqd', p_c.astype(q.dtype), vc)
    kb, vb = sh['kb'], sh['vb']
    n_sel = kb.shape[2]
    cstart = jnp.arange(n_cmp)[:, None] * CMP_STRIDE
    sstart = jnp.arange(n_sel)[None, :] * SEL_BLK
    overlap = jnp.clip(jnp.minimum(cstart + L_CMP, sstart + SEL_BLK) - jnp.maximum(cstart, sstart),
                       0, L_CMP).astype(F32) / L_CMP
    imp = jnp.einsum('bgqn,nj->bgqj', p_c.sum(axis=2), overlap)
    jj = jnp.arange(n_sel)[None, :]
    cur = (qpos // SEL_BLK)[:, None]
    forced = (jj == 0) | (jj == cur) | (jj == cur - 1)
    causal = jj * SEL_BLK <= qpos[:, None]
    score = jnp.where(forced, FORCE, jnp.where(causal, imp, NEG))
    _, idx = lax.top_k(score, min(N_SELECT, n_sel))
    if prompt:
        nC = T // SEL_QBLK
        k = idx.shape[-1]
        qc = q.reshape(B, N_KV, GROUP, nC, SEL_QBLK, HEAD_DIM).transpose(3, 0, 1, 2, 4, 5)
        pc = qpos.reshape(nC, SEL_QBLK)
        ic = idx.reshape(B, N_KV, nC, SEL_QBLK, k).transpose(2, 0, 1, 3, 4)
        o_s = lax.map(lambda a: select_attend(a[0], a[1], a[2], kb, vb, slopes), (qc, pc, ic))
        o_s = o_s.transpose(1, 2, 3, 0, 4, 5).reshape(B, N_KV, GROUP, T, HEAD_DIM)
        o_w = window_banded(q, sh['kw'], sh['vw'], slopes)
    else:
        o_s = select_attend(q, qpos, idx, kb, vb, slopes)
        o_w = window_dense(q, qpos, sh['kw'], sh['vw'], sh['kpos'], slopes)
    o = (gates[0] * o_c + gates[1] * o_s + gates[2] * o_w).astype(h.dtype)
    o = o.transpose(0, 3, 1, 2, 4).reshape(B, T, N_HEADS * HEAD_DIM)
    return o @ w_o

def run_trunk(x, qpos, conv_prev, make_shared, W, slopes, prompt):
    conv_new = []
    shared = None
    extra = None
    for layer in range(DEPTH):
        if layer == N_A_LAYERS:
            shared, extra = make_shared(x)
        g = W['norm_g'][layer]
        x = x + 0.5 * swiglu(rmsnorm(x, g[0]), W['w_ff_in'][layer, 0], W['w_ff_out'][layer, 0])
        if layer < N_A_LAYERS:
            a = layer
            out, st = conv_module(rmsnorm(x, g[1]), conv_prev[a], W['w_pw1'][a], W['w_dw'][a],
                                  W['b_dw'][a], W['ln_g'][a], W['ln_b'][a], W['w_pw2'][a])
            conv_new.append(st)
        else:
            b = layer - N_A_LAYERS
            out = nsa_mixer(rmsnorm(x, g[1]), qpos, shared, W['w_qg'][b], W['w_o'][b], slopes, prompt)
        x = x + out
        x = x + 0.5 * swiglu(rmsnorm(x, g[2]), W['w_ff_in'][layer, 1], W['w_ff_out'][layer, 1])
    return rmsnorm(x, W['g_final']), jnp.stack(conv_new), extra

def setup_inputs(seed: int = 0) -> dict:
    key = jax.random.key(seed)
    ks = jax.random.split(key, 32)
    n_pages = PAST_LEN // PAGE_SIZE
    n_pool = (5 * DEC_BATCH * n_pages) // 4
    wbuf = min(WINDOW, PAST_LEN)

    def nrm(i, shape, scale=1.0):
        return jax.random.normal(ks[i], shape, F32) * scale

    page_table = jax.random.permutation(ks[3], n_pool)[:DEC_BATCH * n_pages]
    page_table = page_table.reshape(DEC_BATCH, n_pages).astype(jnp.int32)
    return {
        'x_prompt': nrm(0, (BATCH, SEQ, D_MODEL)),
        'x_sample': nrm(1, (DEC_BATCH, DEC_SEQ, D_MODEL)),
        'cache_kv': nrm(2, (n_pool, PAGE_SIZE, N_PAGED, N_KV, HEAD_DIM)),
        'page_table': page_table,
        'state_kv_win': nrm(4, (DEC_BATCH, wbuf, N_KV_ROWS - N_PAGED, N_KV, HEAD_DIM)),
        'state_conv': nrm(5, (N_A_LAYERS, DEC_BATCH, CONV_W - 1, D_MODEL), 0.5),
        'norm_g': 1.0 + nrm(6, (DEPTH, 3, D_MODEL), 0.02),
        'w_ff_in': nrm(7, (DEPTH, 2, D_MODEL, 2 * D_FF), D_MODEL ** -0.5),
        'w_ff_out': nrm(8, (DEPTH, 2, D_FF, D_MODEL), D_FF ** -0.5),
        'w_pw1': nrm(9, (N_A_LAYERS, D_MODEL, 2 * D_MODEL), D_MODEL ** -0.5),
        'w_dw': nrm(10, (N_A_LAYERS, CONV_W, D_MODEL), CONV_W ** -0.5),
        'b_dw': nrm(11, (N_A_LAYERS, D_MODEL), 0.01),
        'ln_g': 1.0 + nrm(12, (N_A_LAYERS, D_MODEL), 0.02),
        'ln_b': nrm(13, (N_A_LAYERS, D_MODEL), 0.01),
        'w_pw2': nrm(14, (N_A_LAYERS, D_MODEL, D_MODEL), D_MODEL ** -0.5),
        'g_kv': 1.0 + nrm(15, (D_MODEL,), 0.02),
        'w_kv': nrm(16, (D_MODEL, N_KV_ROWS * N_KV * HEAD_DIM), D_MODEL ** -0.5),
        'w_cmp1': nrm(17, (2, L_CMP, HEAD_DIM, CMP_HID), (L_CMP * HEAD_DIM) ** -0.5),
        'b_cmp1': nrm(18, (2, CMP_HID), 0.01),
        'w_cmp2': nrm(19, (2, CMP_HID, HEAD_DIM), CMP_HID ** -0.5),
        'b_cmp2': nrm(20, (2, HEAD_DIM), 0.01),
        'pe_cmp': nrm(21, (2, L_CMP, HEAD_DIM), 0.1),
        'w_qg': nrm(22, (N_B_LAYERS, D_MODEL, N_HEADS * HEAD_DIM + 3 * N_HEADS), D_MODEL ** -0.5),
        'w_o': nrm(23, (N_B_LAYERS, N_HEADS * HEAD_DIM, D_MODEL), (N_HEADS * HEAD_DIM) ** -0.5),
        'g_final': 1.0 + nrm(24, (D_MODEL,), 0.02),
    }

def reference(x_prompt, x_sample, cache_kv, page_table, state_kv_win, state_conv,
              norm_g, w_ff_in, w_ff_out, w_pw1, w_dw, b_dw, ln_g, ln_b, w_pw2,
              g_kv, w_kv, w_cmp1, b_cmp1, w_cmp2, b_cmp2, pe_cmp, w_qg, w_o, g_final):
    W = {'norm_g': norm_g, 'w_ff_in': w_ff_in, 'w_ff_out': w_ff_out, 'w_pw1': w_pw1,
         'w_dw': w_dw, 'b_dw': b_dw, 'ln_g': ln_g, 'ln_b': ln_b, 'w_pw2': w_pw2,
         'w_qg': w_qg, 'w_o': w_o, 'g_final': g_final}
    slopes = jnp.exp2(-8.0 * (jnp.arange(N_HEADS, dtype=F32) + 1.0) / N_HEADS).reshape(N_KV, GROUP)

    def kv_rows(x):
        B, T = x.shape[:2]
        return (rmsnorm(x, g_kv) @ w_kv).reshape(B, T, N_KV_ROWS, N_KV, HEAD_DIM)

    def shared_prompt(x):
        rows = kv_rows(x)
        T = rows.shape[1]
        sh = build_shared(rows[:, :, 0], rows[:, :, 1], rows[:, :, 2], rows[:, :, 3],
                          w_cmp1, b_cmp1, w_cmp2, b_cmp2, pe_cmp)
        sh['kw'] = rows[:, :, 4]
        sh['vw'] = rows[:, :, 5]
        keep = min(WINDOW, T)
        return sh, (rows[:, :, :N_PAGED], rows[:, T - keep:, N_PAGED:])

    qpos_p = jnp.arange(x_prompt.shape[1])
    conv0 = jnp.zeros((N_A_LAYERS, x_prompt.shape[0], CONV_W - 1, D_MODEL), x_prompt.dtype)
    y_prompt, conv_prompt, ext_p = run_trunk(x_prompt, qpos_p, conv0, shared_prompt, W, slopes, True)
    kv_prompt, win_prompt = ext_p

    past_len = page_table.shape[1] * PAGE_SIZE

    def shared_sample(x):
        rows = kv_rows(x)
        Bd, Tn = rows.shape[:2]

        def full(c):
            past = cache_kv[page_table, :, c].reshape(Bd, past_len, N_KV, HEAD_DIM).astype(rows.dtype)
            return jnp.concatenate([past, rows[:, :, c]], axis=1)

        sh = build_shared(full(0), full(1), full(2), full(3),
                          w_cmp1, b_cmp1, w_cmp2, b_cmp2, pe_cmp)
        win = jnp.concatenate([state_kv_win.astype(rows.dtype), rows[:, :, N_PAGED:]], axis=1)
        wbuf = state_kv_win.shape[1]
        sh['kw'] = win[:, :, 0]
        sh['vw'] = win[:, :, 1]
        sh['kpos'] = past_len - wbuf + jnp.arange(wbuf + Tn)
        keep = min(WINDOW, past_len + Tn)
        return sh, (rows[:, :, :N_PAGED], win[:, win.shape[1] - keep:])

    qpos_s = past_len + jnp.arange(x_sample.shape[1])
    y_sample, conv_sample, ext_s = run_trunk(x_sample, qpos_s, state_conv, shared_sample, W, slopes, False)
    kv_sample, win_sample = ext_s

    return (y_prompt, y_sample, kv_prompt, kv_sample, win_prompt, win_sample, conv_prompt, conv_sample)


_drawn_inputs = setup_inputs


def setup_inputs(seed=0):
    import zlib

    import numpy as np

    out = dict(_drawn_inputs(seed))
    spreads = {}
    factors = {'b_dw': 4.247,
     'ln_g': 4.234,
     'ln_b': 8.0,
     'g_kv': 8.276,
     'b_cmp1': 59.328,
     'b_cmp2': 35.039,
     'g_final': 8.031,
     'pe_cmp': 6.192}
    for name, (base, spread) in spreads.items():
        noise = np.random.default_rng([zlib.crc32(name.encode()), seed]).standard_normal(out[name].shape)
        drawn = base * np.exp(spread * noise) if base else spread * noise
        out[name] = __import__('jax').numpy.asarray(drawn.astype(out[name].dtype))
    for name, factor in factors.items():
        out[name] = (out[name] * factor).astype(out[name].dtype)
    return out
```

```python
from contextlib import ExitStack

import numpy as np

import concourse.bass as bass
from concourse import mybir
from concourse.alu_op_type import AluOpType as ALU

ACT = mybir.ActivationFunctionType
F32 = mybir.dt.float32
I32 = mybir.dt.int32
AX_X = mybir.AxisListType.X

P = 128
D = 1024
KT = D // P
SEQ = 256
NB = 8
NQ = 8
TS = NB * NQ
T = SEQ + TS
FF = 2816
FT = FF // P
TAPS = 31
HIST = TAPS - 1
NKV = 4
NZ = 4
NH = NKV * NZ
HD = 64
PAGE = 128
NPAGE = 16
PAST = NPAGE * PAGE
NPOOL = 160
CS = 16
NCH = PAST // CS
NCP = SEQ // CS
SB = 64
NSEL = 33
WIN = 512
WR = WIN // P
EPS = 1e-6
NEG = -1e30
FORCE = 1e9
FAR = 1e33
TINY = 1e-30
QSCALE = HD ** -0.5

PROMPT_W = HIST + SEQ
SAMPLE_W = HIST + NQ
FULL_W = PROMPT_W + NB * SAMPLE_W
TOK_TILES = ((0, P), (P, P), (SEQ, TS))

V_NORM, V_KV, V_FINAL, V_BDW, V_LNG, V_LNB = 0, 48, 56, 64, 72, 80
V_B1, V_B2, V_PE, V_ROWS = 88, 90, 91, 123

S_SEL, S_NEW, S_WIN, S_WNEW, S_CMP = 0, PAST, PAST + TS, PAST + TS + WIN, PAST + 2 * TS + WIN
S_COLS = S_CMP + P
CREDIT = 2


def host_constants():
    f = np.float32
    p = np.arange(P)
    slope = np.exp2(f(-8.0) * (np.arange(NH, dtype=f) + f(1)) / f(NH)).astype(f)
    g, z, q = p // 32, p // 8 % 4, p % 8
    sl = slope[g * NZ + z][:, None]
    qpos = (PAST + q)[:, None]
    n = np.arange(P)[None]
    cmp_bias = -(sl * (qpos - (n * CS + 31)).astype(f))
    cmp_bias[:, P - 1] = NEG
    sel_bias = -(sl * (qpos - np.arange(PAST)[None]).astype(f))
    r, pp = np.divmod(np.arange(WIN), P)
    dist = qpos - (PAST - WIN + pp * WR + r)[None]
    win_bias = np.where(dist < WIN, -(sl * dist.astype(f)), f(NEG))
    k = np.arange(120)[None] - 56
    dist = q[:, None] - k
    new_bias = np.where((k >= 0) & (k < NQ) & (dist >= 0), -(sl * dist.astype(f)), f(NEG))
    cs, ss = np.arange(P)[:, None] * CS, np.arange(NSEL)[None] * SB
    overlap = np.clip(np.minimum(cs + 32, ss + SB) - np.maximum(cs, ss), 0, 32).astype(f) / f(32)
    overlap[P - 1] = 0
    t = np.arange(SEQ).reshape(2, P)
    dist = t[:, :, None] - np.arange(SEQ)
    dist_full = np.where(dist >= 0, dist, FAR).transpose(1, 0, 2)
    dist = t[:, :, None] - (np.arange(NCP) * CS + 31)
    live = (dist >= 0) & (np.arange(NCP) < NCP - 1)
    dist_cmp = np.where(live, dist, FAR).transpose(1, 0, 2)
    live_cmp = live.transpose(1, 0, 2)
    parts = [
        ("ident", np.eye(P)),
        ("zsum", (g[:, None] == g[None]) & (q[:, None] == q[None])),
        ("mean", np.full((P, P), 1 / D)),
        ("overlap", overlap),
        ("head_rows", np.arange(P)[:, None] == (p // 8)[None]),
        ("own_query", q[:, None] == np.arange(NQ)[None]),
        ("token_row", (p % 8)[:, None] * 32 + np.arange(CS)[None] * 2),
        ("neg_slope", np.broadcast_to(-slope, (P, NH))),
        ("cmp_bias", cmp_bias), ("new_bias", new_bias), ("win_bias", win_bias),
        ("dist_full", dist_full.reshape(P, -1)), ("dist_cmp", dist_cmp.reshape(P, -1)),
        ("live_cmp", live_cmp.reshape(P, -1)), ("sel_bias", sel_bias),
    ]
    where, at = {}, 0
    for name, a in parts:
        where[name] = (at, a.shape[1])
        at += a.shape[1]
    return np.concatenate([a.astype(f) for _, a in parts], axis=1), where


class Seen:

    def __init__(self):
        self.n = {}

    def __getitem__(self, sem):
        return self.n.get(sem.name, 0)

    def add(self, sem, k=1):
        self.n[sem.name] = self[sem] + k
        return self[sem]

    def wait(self, eng, sem, k=1):
        eng.wait_ge(sem, self.add(sem, k))


def program(nc, ins, outs, where):
    with ExitStack() as ctx:
        def sb(name, *shape, dt=F32):
            return ctx.enter_context(nc.sbuf_tensor(name, list(shape), dt))

        def sem(name):
            return ctx.enter_context(nc.semaphore(name))

        const = sb("const", P, where["sel_bias"][0])
        xT = sb("xT", P, KT, T)
        hT = sb("hT", P, KT, T)
        sq = sb("sq", P, KT, T)
        G = sb("G", P, FT * T)
        W = sb("W", P, 2, FT * P)
        stage = sb("stage", P, 2, 4096)
        C1 = sb("C1", P, 2, 2048)
        R = sb("R", P, 4104)
        kcT = sb("kcT", P, NB, 2, P)
        vc = sb("vc", P, NB, 256)
        kcTp = sb("kcTp", P, 2, NCP)
        vcp = sb("vcp", NCP, 256)
        rows = sb("rows", P, 2, 6, 256)
        rowsS = sb("rowsS", TS, 6, 256)
        kT = sb("kT", P, 2, 2, T)
        w2 = sb("w2", P, 2, HD)
        b2v = sb("b2v", 1, 256)
        ones = sb("ones", 1, P)
        wg = sb("wg", P, KT, 48)
        vecs = sb("vecs", P, V_ROWS)
        wdw = sb("wdw", P, TAPS * KT)
        cst = sb("cst", P, 2)
        eps = sb("eps", P, 1)
        stat = sb("stat", P, 3, T)
        tmp = sb("tmp", P, 2, T)
        ptab = sb("ptab", P, NB, dt=I32)
        ptabf = sb("ptabf", P, NB)
        ptrow = sb("ptrow", 1, P, dt=I32)
        cidx = sb("cidx", P, NB * CS, dt=I32)
        cslot = sb("cslot", P, CS, dt=I32)
        gateP = sb("gateP", P, 2, 48)
        gateS = sb("gateS", P, 3, NB)
        gsig = sb("gsig", NH, 3 * TS)
        small = sb("small", P, 2, 16)
        imp = sb("imp", P, 4, NSEL)
        top8 = sb("top8", P, 2, 8)
        PSA = ctx.enter_context(nc.psum_tensor("PSA", [P, 8, 512], F32))
        PS = [PSA[:, i, :] for i in range(8)]

        def cn(name, n=P):
            a, w = where[name]
            return const[0:n, a:a + w]

        ident, meanm = cn("ident"), cn("mean")
        dist_full = cn("dist_full").rearrange("p (q k) -> p q k", q=2)
        dist_cmp = cn("dist_cmp").rearrange("p (q k) -> p q k", q=2)
        live_cmp = cn("live_cmp").rearrange("p (q k) -> p q k", q=2)
        xin = G[:, 0:3 * D].rearrange("p (t d) -> p t d", t=3)
        gT = G[:, :].rearrange("p (f t) -> p f t", f=FT)
        full = G[:, 0:KT * FULL_W].rearrange("p (k c) -> p k c", k=KT)
        fullS = G[:, 0:KT * FULL_W].rearrange("p (k c) -> p k c", k=KT)[:, :, PROMPT_W:] \
            .rearrange("p k (b r) -> p k b r", b=NB)
        convS = G[0:TS, KT * FULL_W:KT * FULL_W + D]
        convP = G[0:HIST, KT * FULL_W + D:KT * FULL_W + 2 * D]
        rowsf = rows[:, :, :, :].rearrange("p t c d -> p (t c d)")
        hist = rowsf[0:120, 0:2 * D].rearrange("p (h d) -> p h d", h=2)
        vr = rowsf[:, 2 * D:2 * D + 3 * P]
        Wgu = [W[:, u, 0:2048].rearrange("p (k h n) -> p k h n", k=KT, h=2) for u in range(2)]
        Wdn = [W[:, u, :].rearrange("p (k n) -> p k n", k=FT) for u in range(2)]
        W256 = [W[:, u, 0:2048].rearrange("p (k n) -> p k n", k=KT) for u in range(2)]
        selb = W[:, 1, 0:PAST]
        w1 = C1[:, :, :].rearrange("p c (j h) -> p c j h", h=P)
        STG = [stage[:, u, :].rearrange("p (s c) -> p s c", s=8) for u in range(2)]
        RT = R[:, 0:2056].rearrange("p (j c n) -> p j c n", j=2, c=2)
        hgel = R[:, 2056:3080].rearrange("p (c n) -> p c n", c=2)
        RL = R[:, 3080:4104].rearrange("p (c n) -> p c n", c=2)
        vnew = stat[:, :, :].rearrange("p a t -> p (a t)")[:, 0:KT * TS].rearrange("p (k t) -> p k t", k=KT)
        qT = sq
        oT = hT
        KTb = R[:, 0:4096].rearrange("p (g n) -> p g n", g=2)
        S = G[:, 0:S_COLS]
        PT = G[:, S_COLS:S_COLS + 23 * P]
        KTw = G[:, S_COLS + 23 * P:S_COLS + 23 * P + 2 * WIN].rearrange("p (g n) -> p g n", g=2)
        qbd = G[:, S_COLS + 23 * P + 2 * WIN:S_COLS + 23 * P + 2 * WIN + 256].rearrange("p (g n) -> p g n", g=2)
        osb = tmp[:, 0, 0:256]
        ips = tmp[:, 1, 0:P]
        kpg = stage[:, 0, :].rearrange("p (k c) -> p k c", k=NPAGE)
        vpg = stage[:, 1, :].rearrange("p (k c) -> p k c", k=NPAGE)
        wst = [C1[:, u, :].rearrange("p (r c) -> p r c", r=WR) for u in range(2)]
        SP_ = G[:, 0:2 * 528].rearrange("p (v n) -> p v n", v=2)
        PTp = G[:, 1056:1056 + 2 * 640].rearrange("p (v c n) -> p v c n", v=2, c=5)
        qsl = G[:, 2336:2336 + 512].rearrange("p (g n) -> p g n", g=2)
        oP = G[:, 2848:2848 + 2048].rearrange("p (t n) -> p t n", t=2)
        yout = G[:, 0:3 * D].rearrange("p (t d) -> p t d", t=3)

        names = """passed kv_stored conv_stored consts_loaded vecs_loaded x_loaded misc_loaded hist_loaded slab_used evac_done act_glu
            turned turned_out sq_ready ssum_ready mean_ready std_ready rstd_ready h_ready setup_done
            conv_step conv_init hist_out cen_ready idx_ready slot_ready rt_turned rt_ready rl_ready vnew_ready z_ready gelu_ready
            kv_ready kv_out conv_turned conv_rows stored kT_turned kT_out prow_loaded q_ready
            gate_logits gate_sig gate_spread gate_out gate_mul dve_step
            qsl_ready p_scores p_biased p_max p_exp p_scaled p_turned p_PT p_out o_evac oP_turned oP_out
            win_stored attn_in
            kt_turned kt_out0 kt_out1 s_scores s_biased c_max c_exp c_scaled imp_sum imp_sumout imp_ready
            s_max s_exp s_scaled pt_turned pt_out o_ready o_copied o_turned o_out qbd_ready
            selb_loaded ptrow_loaded y_turned y_out pool_step""".split()
        m = {n: sem(n) for n in names}
        slab_loaded = [sem("slab_loaded0"), sem("slab_loaded1")]
        gathered = [sem("gathered0"), sem("gathered1")]
        half_used = [sem("half_used0"), sem("half_used1")]
        K_loaded, V_loaded, K_used, V_used = map(sem, ("K_loaded", "V_loaded", "K_used", "V_used"))
        win_loaded = [sem("win_loaded0"), sem("win_loaded1")]
        win_used = [sem("win_used0"), sem("win_used1")]

        cache = ins["cache_kv"]

        def sp_program(sp):
            slab = [0]

            def slabs(n, load):
                base = slab[0]
                with sp.Fori(0, n // 2) as i:
                    for u in range(2):
                        sp.wait_ge(m["slab_used"], i * 2 + (base + u + 1))
                        load(i, u)
                slab[0] += n

            def ffn(layer, j):
                wi = ins["w_ff_in"][layer, j].rearrange("(k p) (h n) -> p k h n", p=P, h=2)
                wo = ins["w_ff_out"][layer, j].rearrange("(k p) n -> p k n", p=P)

                def up(i, u):
                    for h in range(2):
                        sp.dma_start(Wgu[u][:, :, h, :], wi[:, :, h, bass.ds(i * 256 + u * P, P)]) \
                          .then_inc(slab_loaded[u], 16)

                def down(i, u):
                    sp.dma_start(Wdn[u], wo[:, :, bass.ds(i * 256 + u * P, P)]).then_inc(slab_loaded[u], 16)
                slabs(FT, up)
                slabs(KT, down)

            sp.dma_start(const[:, :], ins["const"][:, 0:const.shape[1]]).then_inc(m["consts_loaded"], 16)
            sp.dma_start(xin[:, 0:2, :], ins["x_prompt"][0].rearrange("(t p) d -> p t d", p=P)) \
              .then_inc(m["x_loaded"], 16)
            sp.dma_start(xin[0:TS, 2, :], ins["x_sample"].rearrange("b t d -> (b t) d")).then_inc(m["x_loaded"], 16)

            def vload(row, n, src):
                sp.dma_start(vr[row:row + n, 0:P], src).then_inc(m["vecs_loaded"], 16)
            vload(V_NORM, 48, ins["norm_g"].rearrange("l j (k p) -> (l j k) p", p=P))
            vload(V_KV, 8, ins["g_kv"].rearrange("(k p) -> k p", p=P))
            vload(V_FINAL, 8, ins["g_final"].rearrange("(k p) -> k p", p=P))
            for r, name in ((V_BDW, "b_dw"), (V_LNG, "ln_g"), (V_LNB, "ln_b")):
                vload(r, 8, ins[name][0].rearrange("(k p) -> k p", p=P))
            vload(V_B1, 2, ins["b_cmp1"])
            for h in range(2):
                sp.dma_start(vr[V_B2:V_B2 + 1, h * HD:h * HD + HD], ins["b_cmp2"][0:1, :]).then_inc(m["vecs_loaded"], 16)
            vload(V_PE, 32, ins["pe_cmp"].rearrange("c (j s) d -> (c j) (s d)", s=2))
            wd = ins["w_dw"][0].rearrange("w (k p) -> (w k) p", p=P)
            for h in range(2):
                sp.dma_start(vr[0:124, P * (h + 1):P * (h + 2)], wd[124 * h:124 * h + 124]) \
                  .then_inc(m["vecs_loaded"], 16)
            pt = ins["page_table"]
            with nc.allow_non_contiguous_dma(reason="a table of 128 numbers"):
                for r in range(PAGE // CS):
                    sp.dma_start(ptab[r:P:PAGE // CS, :], pt.rearrange("b k -> k b")).then_inc(m["ptrow_loaded"], 16)
            sp.dma_start(ptrow[:, :], pt.rearrange("(a b) k -> a (b k)", a=1)).then_inc(m["ptrow_loaded"], 16)
            for h in range(2):
                sp.dma_start(hist[:, h, :], ins["state_conv"][0].rearrange("(h b) r d -> h (b r) d", h=2)[h]) \
                  .then_inc(m["hist_loaded"], 16)
            for c in range(2):
                sp.dma_start(w1[:, c, :, :], ins["w_cmp1"][c].rearrange("(j s) d h -> (s d) j h", s=2)) \
                  .then_inc(m["misc_loaded"], 16)
                sp.dma_start(w2[:, c, :], ins["w_cmp2"][c]).then_inc(m["misc_loaded"], 16)
            for g in range(NKV):
                sp.dma_start(b2v[0:1, g * HD:g * HD + HD], ins["b_cmp2"][1:2, :]).then_inc(m["misc_loaded"], 16)
            sp.dma_start(wg[:, :, :], ins["w_qg"][0][:, D:].rearrange("(k p) n -> p k n", p=P)) \
              .then_inc(m["misc_loaded"], 16)
            ffn(0, 0)
            wp = ins["w_pw1"][0].rearrange("(k p) (h n) -> p k h n", p=P, h=2)

            def pw1(i, u):
                for h in range(2):
                    sp.dma_start(Wgu[u][:, :, h, :], wp[:, :, h, bass.ds(i * 256 + u * P, P)]) \
                      .then_inc(slab_loaded[u], 16)
            slabs(KT, pw1)

            def wide(src):
                def load(i, u):
                    sp.dma_start(W256[u], src[:, :, bass.ds(i * 512 + u * 256, 256)]).then_inc(slab_loaded[u], 16)
                return load
            slabs(4, wide(ins["w_pw2"][0].rearrange("(k p) n -> p k n", p=P)))
            ffn(0, 1)
            slabs(6, wide(ins["w_kv"].rearrange("(k p) n -> p k n", p=P)))
            sp.wait_ge(m["kv_stored"], 16)
            for u in range(2):
                src = outs[2][0].rearrange("(n s) c g d -> n s (c g d)", s=CS)[:, 8 * u:8 * u + 8, 0:512]
                sp.wait_ge(half_used[u], CREDIT_H + NB)
                sp.dma_start(STG[u][0:NCP], src).then_inc(m["prow_loaded"], 16)
            ffn(1, 0)
            wq = ins["w_qg"][0].rearrange("(k p) n -> p k n", p=P)

            def queries(i, u):
                for h in range(2):
                    for g in range(2):
                        sp.dma_start(W256[u][:, :, h * P + g * HD:h * P + g * HD + HD],
                                     wq[:, :, bass.ds(i * 512 + (g * 256 + (2 * u + h) * HD), HD)]) \
                          .then_inc(slab_loaded[u], 16)
            slabs(4, queries)
            sp.wait_ge(m["slab_used"], slab[0] + CREDIT)
            sp.dma_start(selb, ins["const"][:, const.shape[1]:]).then_inc(m["selb_loaded"], 16)
            sp.wait_ge(m["kv_out"], 2 * (NB + 1))
            sp.wait_ge(m["ptrow_loaded"], 16 * 9)
            with sp.Fori(0, NB // 2) as i:
                for u in range(2):
                    b = i * 2 + u
                    sp.wait_ge(win_used[u], i + 1)
                    sp.dma_start(C1[:, u, :], ins["state_kv_win"].rearrange("b (p r) c g d -> b p (r c g d)", r=WR)
                                 [bass.ds(b, 1)].rearrange("a p c -> p (a c)")).then_inc(win_loaded[u], 16)
                    for c, page, used, loaded in ((2, kpg, K_used, K_loaded), (3, vpg, V_used, V_loaded)):
                        sp.wait_ge(used, b + 1)
                        sp.sem_inc(m["passed"], 1)
                        for k in range(NPAGE):
                            n = sp.value_load(ptrow[0:1, bass.ds(b * NPAGE + k, 1)], min_val=0, max_val=NPOOL - 1)
                            src = cache[bass.ds(n, 1), :, c, :, :].rearrange("a t g d -> t (a g d)")
                            sp.dma_start(page[:, k, :], src).then_inc(loaded, 16)
            sp.wait_ge(m["o_out"], 2 * NB)
            wo = ins["w_o"][0].rearrange("(q g z d) n -> q g d z n", q=2, g=2, z=NZ)

            def out_proj(i, u):
                for q in range(2):
                    for g in range(2):
                        sp.dma_start(W256[u][g * HD:g * HD + HD, q * NZ:q * NZ + NZ, :],
                                     wo[q, g, :, :, bass.ds(i * 512 + u * 256, 256)]).then_inc(slab_loaded[u], 16)
            slabs(4, out_proj)
            ffn(1, 1)

        CREDIT_H = 1

        def pool_program(pool):
            pool.memset(eps[:, :], EPS).then_inc(m["pool_step"], 1)
            pool.memset(ones[:, :], 1.0).then_inc(m["pool_step"], 1)
            pool.memset(R[:, :], 0.0).then_inc(m["pool_step"], 1)
            pool.dma_start(outs[5].rearrange("b t c g d -> b (t c g d)")[:, 0:(WIN - NQ) * 512],
                           ins["state_kv_win"].rearrange("b t c g d -> b (t c g d)")[:, NQ * 512:]) \
                .then_inc(m["stored"], 16)
            pool.dma_start(outs[7][0, :, 0:HIST - NQ, :], ins["state_conv"][0, :, NQ:, :]).then_inc(m["stored"], 16)
            pool.wait_ge(m["idx_ready"], 1)
            pairs = cache.rearrange("n t (h c) g d -> (n t h) (c g d)", h=2)
            with pool.Fori(0, NB) as b:
                for u in range(2):
                    pool.wait_ge(half_used[u], b + 1)
                    pool.tensor_copy(cslot[:, 8 * u:8 * u + 8], cidx[:, bass.ds(b * CS + 8 * u, 8)]) \
                        .then_inc(m["slot_ready"], 1)
                    pool.wait_ge(m["slot_ready"], b * 2 + (u + 1))
                    pool.sem_inc(m["passed"], 1)
                    for s in range(8):
                        pool.indirect_dma_start(
                            out=STG[u][:, s, :], out_offset=None, in_=pairs,
                            in_offset=bass.IndirectOffsetOnAxis(ap=cslot[:, 8 * u + s:8 * u + s + 1], axis=0)) \
                            .then_inc(gathered[u], 16)
            pool.wait_ge(m["conv_rows"], 4)
            pool.dma_start(outs[6][0, 0], convP).then_inc(m["conv_stored"], 16)
            for b in range(NB):
                pool.dma_start(outs[7][0, b, HIST - NQ:, :], convS[b * NQ:b * NQ + NQ, :]) \
                    .then_inc(m["conv_stored"], 16)
            pool.wait_ge(m["evac_done"], SLAB_KV + CREDIT)
            flat = [outs[2][0].rearrange("(t p) c g d -> p t (c g d)", p=P),
                    outs[4][0].rearrange("(t p) c g d -> p t (c g d)", p=P)]
            for o, (c, n), done in zip(flat, ((0, 4), (4, 2)), (m["kv_stored"], m["stored"])):
                pool.dma_start(o, rows[:, :, c:c + n, :].rearrange("p t c d -> p t (c d)")).then_inc(done, 16)
            pool.dma_start(outs[3].rearrange("b t c g d -> (b t) (c g d)"),
                           rowsS[:, 0:4, :].rearrange("p c d -> p (c d)")).then_inc(m["stored"], 16)
            for b in range(NB):
                pool.dma_start(outs[5].rearrange("b t c g d -> b t (c g d)")[b, WIN - NQ:, :],
                               rowsS[b * NQ:b * NQ + NQ, 4:6, :].rearrange("p c d -> p (c d)")) \
                    .then_inc(m["stored"], 16)
            pool.wait_ge(m["y_out"], 6)
            pool.dma_start(outs[0][0].rearrange("(t p) d -> p t d", p=P), yout[:, 0:2, :]).then_inc(m["stored"], 16)
            pool.dma_start(outs[1].rearrange("b t d -> (b t) d"), yout[0:TS, 2, :]).then_inc(m["stored"], 16)
            pool.wait_ge(m["kv_stored"], 16)
            pool.wait_ge(m["conv_stored"], 16 * (NB + 1))
            pool.wait_ge(m["stored"], 16 * (2 + 2 + NB + 2))

        def pe_program(pe):
            seen = Seen()
            slab = [0]
            for s, n in ((m["slab_used"], CREDIT), (K_used, 1), (V_used, 1), (win_used[0], 1), (win_used[1], 1)):
                pe.sem_inc(s, n)

            def slabs(n, per_slot, work):
                base, b0 = slab[0], [seen[s] for s in slab_loaded]
                with pe.Fori(0, n // 2) as i:
                    for u in range(2):
                        pe.wait_ge(slab_loaded[u], i * (16 * per_slot) + (b0[u] + 16 * per_slot))
                        pe.wait_ge(m["evac_done"], i * 2 + (base + u + 1))
                        work(i, u).then_inc(m["slab_used"], 1)
                for u in range(2):
                    seen.add(slab_loaded[u], 16 * per_slot * n // 2)
                slab[0] += n

            def gated(i, u):
                for h in range(2):
                    for k in range(KT):
                        mm = pe.matmul(PS[2 * u + h][:, 0:T], Wgu[u][:, k, h, :], hT[:, k, :],
                                       start=k == 0, stop=k == KT - 1)
                return mm

            def down(i, u):
                for k in range(FT):
                    mm = pe.matmul(PS[2 * u][:, 0:T], Wdn[u][:, k, :], gT[:, k, :], start=k == 0, stop=k == FT - 1)
                return mm

            def pair(i, u):
                for h in range(2):
                    for k in range(KT):
                        mm = pe.matmul(PS[2 * u + h][:, 0:T], W256[u][:, k, h * P:h * P + P], hT[:, k, :],
                                       start=k == 0, stop=k == KT - 1)
                return mm

            def kv(i, u):
                for t, (at, n) in enumerate(TOK_TILES):
                    out = PS[2 * u][:, t * 256:t * 256 + 256] if t < 2 else PS[2 * u + 1][0:n, 0:256]
                    for k in range(KT):
                        mm = pe.matmul(out, hT[:, k, at:at + n], W256[u][:, k, :], start=k == 0, stop=k == KT - 1)
                return mm

            def channel_mean():
                seen.wait(pe, m["ssum_ready"])
                pe.matmul(PS[4][:, 0:T], meanm, stat[:, 0, :], start=True, stop=True).then_inc(m["mean_ready"], 1)

            def norm():
                channel_mean()
                seen.wait(pe, m["h_ready"])

            def ffn():
                norm()
                slabs(FT, 2, gated)
                pe.wait_ge(m["evac_done"], slab[0] + CREDIT)
                slabs(KT, 1, down)

            def compress(n, b):
                def first_layer(t):
                    j, c = t // 2, t % 2
                    pe.wait_ge(m["rt_ready"], b * 16 + (t + 1 + CREDIT))
                    z = PS[(7, 4)[c]]
                    pe.matmul(z[:, 0:4 * n], w1[:, c, j, :], RT[:, j % 2, c, 0:4 * n], start=j == 0, stop=False)
                    mm = pe.matmul(z[:, 0:4 * n], w1[:, c, 8 + j, :], RT[:, j % 2, c, 1:4 * n + 1],
                                   start=False, stop=j == 7)
                    if t >= 14:
                        mm.then_inc(m["z_ready"], 1)

                for t in range(16):
                    j, c = t // 2, t % 2
                    pe.wait_ge(m["rt_ready"], b * 16 + (t + 1))
                    pe.wait_ge(m["rl_ready"], b * 16 + (t + 1))
                    for g in range(NKV):
                        tr = pe.transpose(PS[5 + c][:, g * n:g * n + n], RL[0:n, c, g * P:g * P + P],
                                          ident[0:n, 0:n])
                    tr.then_inc(m["rt_turned"], 1)
                    if t:
                        first_layer(t - 1)
                first_layer(15)
                pe.wait_ge(m["gelu_ready"], b * 2 + 1)
                h4 = hgel[:, 0, 0:4 * n].rearrange("p (q g n) -> p g q n", q=2, g=2)
                for g in range(2):
                    mm = pe.matmul(PS[0][g * HD:g * HD + HD, 0:2 * n], w2[:, 0, :], h4[:, g, :, :], start=True, stop=True)
                mm.then_inc(m["kv_ready"], 1)
                pe.wait_ge(m["gelu_ready"], b * 2 + 2)
                for g in range(NKV):
                    pe.matmul(PS[1][0:n, g * HD:g * HD + HD], ones[0:1, 0:n], b2v[0:1, g * HD:g * HD + HD],
                              start=True, stop=False)
                    mm = pe.matmul(PS[1][0:n, g * HD:g * HD + HD], hgel[:, 1, g * n:g * n + n], w2[:, 1, :],
                                   start=False, stop=True)
                mm.then_inc(m["kv_ready"], 1)

            pe.wait_ge(m["consts_loaded"], 16)
            pe.wait_ge(m["x_loaded"], 32)
            for k in range(KT):
                for t, (at, n) in enumerate(TOK_TILES):
                    mm = pe.transpose(PS[k][:, at:at + n], xin[0:n, t, k * P:k * P + P], ident[0:n, 0:n])
                mm.then_inc(m["turned"], 1)
            pe.wait_ge(m["vecs_loaded"], 16 * 12)
            pe.wait_ge(m["turned_out"], 1)
            pe.transpose(PS[0][:, 0:V_ROWS], vr[0:V_ROWS, 0:P], ident[0:V_ROWS, 0:V_ROWS]).then_inc(m["turned"], 1)
            for h in range(2):
                pe.wait_ge(m["turned_out"], h + 2)
                pe.transpose(PS[h + 1][:, 0:124], vr[0:124, P * (h + 1):P * (h + 2)], ident[0:124, 0:124]) \
                    .then_inc(m["turned"], 1)
            pe.wait_ge(m["misc_loaded"], 16 * 9)
            pe.wait_ge(m["turned_out"], 9)
            for c in range(2):
                for j in range(16):
                    mm = pe.matmul(PS[3][:, c:c + 1], w1[:, c, j, :], vecs[:, V_PE + 16 * c + j:V_PE + 16 * c + j + 1],
                                   start=j == 0, stop=j == 15)
            mm.then_inc(m["turned"], 1)
            ffn()
            pe.wait_ge(m["hist_loaded"], 32)
            pe.wait_ge(m["evac_done"], slab[0] + CREDIT)
            for h in range(2):
                for a in range(2):
                    for k in range(4):
                        kk = 4 * a + k
                        mm = pe.transpose(PS[4 + 2 * h + a][:, k * 120:k * 120 + 120],
                                          hist[:, h, kk * P:kk * P + P], ident[0:120, 0:120])
                    mm.then_inc(m["turned"], 1)
            pe.wait_ge(m["hist_out"], 4)
            norm()
            slabs(KT, 2, gated)
            pe.wait_ge(m["vnew_ready"], 1)
            for k in range(KT):
                b, c = k // 4, (k % 4) * P
                pe.transpose(PS[b][0:TS, c:c + P], vnew[:, k, :], ident)
                mm = pe.transpose(PS[2 + b][0:HIST, c:c + P], full[:, k, PROMPT_W - HIST:PROMPT_W], ident)
            mm.then_inc(m["conv_turned"], 1)
            pe.wait_ge(m["conv_rows"], 4)
            with pe.Fori(0, NB) as b:
                compress(P, b)
            channel_mean()
            channel_mean()
            seen.wait(pe, m["h_ready"])
            slabs(4, 1, pair)
            ffn()
            norm()
            slabs(6, 1, kv)
            pe.wait_ge(m["evac_done"], slab[0] + CREDIT)
            for br in range(2):
                for q in range(2):
                    for t, (at, n) in enumerate(TOK_TILES):
                        src = rows[:, t, 2 + 2 * br, q * P:q * P + P] if t < 2 else rowsS[:, 2 + 2 * br, q * P:q * P + P]
                        mm = pe.transpose(PS[4 + 2 * br + q][:, at:at + n], src, ident[0:n, 0:n])
                    mm.then_inc(m["kT_turned"], 1)
            pe.wait_ge(m["kT_out"], 4)
            ffn()
            pe.wait_ge(m["evac_done"], slab[0] + CREDIT)
            compress(NCP, NB)
            pe.wait_ge(m["kv_out"], 2 * (NB + 1))
            norm()
            slabs(4, 4, pair)
            for t in range(2):
                for k in range(KT):
                    mm = pe.matmul(PS[5][:, t * 48:t * 48 + 48], hT[:, k, t * P:t * P + P], wg[:, k, :],
                                   start=k == 0, stop=k == KT - 1)
            mm.then_inc(m["gate_logits"], 1)
            for r in range(3):
                for k in range(KT):
                    mm = pe.matmul(PS[6][0:NH, r * TS:r * TS + TS], wg[:, k, r * NH:r * NH + NH], hT[:, k, SEQ:],
                                   start=k == 0, stop=k == KT - 1)
            mm.then_inc(m["gate_logits"], 1)
            pe.wait_ge(m["gate_sig"], 2)
            pe.matmul(PS[7][:, 0:3 * TS], cn("head_rows", NH), gsig[:, :], start=True, stop=True) \
                .then_inc(m["gate_spread"], 1)
            pe.wait_ge(m["evac_done"], slab[0] + CREDIT)
            pe.wait_ge(m["gate_out"], 1)

            for q in range(2):
                with pe.Fori(0, NZ) as z:
                    unit = z * 4 + 16 * q

                    def scores(w):
                        g, t = w // 2, w % 2
                        n = P * (t + 1)
                        lhs = qsl[:, g, t * P:t * P + P]
                        X, Y = PS[2 * (w % 2)], PS[2 * (w % 2) + 1]
                        pe.matmul(X[:, 0:n], lhs, kT[:, 0, q, 0:n], start=True, stop=True)
                        pe.matmul(X[:, 256:256 + NCP], lhs, kcTp[:, q, :], start=True, stop=True)
                        pe.matmul(Y[:, 0:n], lhs, kT[:, 1, q, 0:n], start=True, stop=True) \
                            .then_inc(m["p_scores"], 1)

                    def turn(w):
                        v, t = w % 2, w % 2
                        pe.wait_ge(m["p_scaled"], unit + (w + 1))
                        for c in range(2 * (t + 1)):
                            br, k = c // (t + 1), c % (t + 1)
                            pe.transpose(PS[4][:, c * P:c * P + P], SP_[:, v, br * 256 + k * P:br * 256 + k * P + P], ident)
                        pe.transpose(PS[5][0:NCP, 0:P], SP_[:, v, 512:528], ident).then_inc(m["p_turned"], 1)

                    def values(w):
                        g, t, v = w // 2, w % 2, w % 2
                        grp = 2 * q + g
                        pe.wait_ge(m["p_PT"], unit + (w + 1))
                        out = PS[6 + t][:, bass.ds(z * P + g * HD, HD)]
                        for c in range(2 * (t + 1)):
                            br, k = c // (t + 1), c % (t + 1)
                            pe.matmul(out, PTp[:, v, c, :], rows[:, k, 3 + 2 * br, grp * HD:grp * HD + HD],
                                      start=c == 0, stop=False)
                        pe.matmul(out, PTp[0:NCP, v, 4, :], vcp[:, grp * HD:grp * HD + HD], start=False, stop=True) \
                            .then_inc(m["p_out"], 1)

                    pe.wait_ge(m["qsl_ready"], z + (4 * q + 1))
                    scores(0)
                    for w in range(4):
                        if w < 3:
                            scores(w + 1)
                        turn(w)
                        values(w)
                pe.wait_ge(m["o_evac"], 2 * q + 2)
            for c in range(8):
                for t in range(2):
                    mm = pe.transpose(PS[c // 2][:, (c % 2) * 256 + t * P:(c % 2) * 256 + t * P + P],
                                      oP[:, t, c * P:c * P + P], ident)
                if c % 2:
                    mm.then_inc(m["oP_turned"], 1)
            pe.wait_ge(m["oP_out"], 4)
            pe.wait_ge(m["attn_in"], 1)

            with pe.Fori(0, NB // 2) as i:
                for u in range(2):
                    b = i * 2 + u

                    def chunk(c, mms):
                        pe.wait_ge(m["s_biased"], b * 6 + (c + 1))
                        bank = PS[2 + c % 2]
                        for at, n, keys in mms:
                            for q in range(2):
                                mm = pe.matmul(bank[:, at:at + n], qbd[:, q, :], keys(q), start=q == 0, stop=q == 1)
                        mm.then_inc(m["s_scores"], 1)
                        return mm

                    def turn_keys(r, tiles):
                        pe.wait_ge((m["kt_out0"], m["kt_out1"])[r % 2], b * 5 + (r // 2 + 1))
                        for c, t in enumerate(tiles):
                            mm = pe.transpose(PS[r % 2][:, c * P:c * P + P], t, ident)
                        mm.then_inc(m["kt_turned"], 1)

                    def turn_probs(g, tiles):
                        pe.wait_ge(m["pt_out"], b * 6 + (g + 1))
                        pe.sem_inc(m["passed"], 1)
                        for c, (at, n) in enumerate(tiles):
                            mm = pe.transpose(PS[5 + g % 2][0:n, c * P:c * P + P], S[:, at:at + n], ident)
                        mm.then_inc(m["pt_turned"], 1)

                    def value(c, n, v, first=False, last=False):
                        return pe.matmul(PS[7][:, 0:256], PT[0:n, c * P:c * P + P], v, start=first, stop=last)

                    pe.wait_ge(m["qbd_ready"], b + 1)
                    chunk(0, [(0, TS, lambda q: kT[:, 0, q, SEQ:]), (TS, TS, lambda q: kT[:, 1, q, SEQ:]),
                              (2 * TS, P, lambda q: kcT[:, bass.ds(b, 1), q, :].rearrange("p a n -> p (a n)"))])
                    pe.wait_ge(K_loaded, b * 256 + 256)
                    for r in range(8):
                        turn_keys(r, [kpg[:, 4 * (r % 4) + c, (r // 4) * P:(r // 4) * P + P] for c in range(4)])
                    pe.wait_ge(win_loaded[u], i * 16 + 16)
                    for q in range(2):
                        turn_keys(8 + q, [wst[u][:, c, q * P:q * P + P] for c in range(4)])
                    pe.wait_ge(m["c_scaled"], b + 1)
                    pe.matmul(PS[4][:, 0:P], S[:, S_CMP:S_COLS], cn("zsum"), start=True, stop=True) \
                        .then_inc(m["imp_sum"], 1)
                    for o in range(2):
                        pe.wait_ge((m["kt_out0"], m["kt_out1"])[o], b * 5 + 6)
                    chunk(1, [(0, 512, lambda q: KTb[:, q, 0:512])])
                    pe.wait_ge(m["imp_sumout"], b + 1)
                    pe.matmul(PS[4][:, P:P + NSEL], ips, cn("overlap"), start=True, stop=True) \
                        .then_inc(m["imp_ready"], 1)
                    for c in range(1, 4):
                        chunk(c + 1, [(0, 512, lambda q: KTb[:, q, c * 512:c * 512 + 512])])
                    chunk(5, [(0, WIN, lambda q: KTw[:, q, :])])
                    pe.wait_ge(m["s_scaled"], b + 1)
                    groups = [[(S_NEW, TS), (S_WNEW, TS), (S_CMP, P)], [(S_WIN + c * P, P) for c in range(4)]] + \
                        [[(S_SEL + (4 * g + c) * P, P) for c in range(4)] for g in range(4)]
                    turn_probs(0, groups[0])
                    pe.wait_ge(V_loaded, b * 256 + 256)
                    pe.wait_ge(m["o_copied"], b + 1)
                    for g in range(6):
                        if g < 5:
                            turn_probs(g + 1, groups[g + 1])
                        pe.wait_ge(m["pt_out"], b * 6 + (g + 1 + CREDIT))
                        if g == 0:
                            value(0, TS, rowsS[:, 3, :], first=True)
                            value(1, TS, rowsS[:, 5, :]).then_inc(K_used, 1)
                            value(2, P, vc[:, bass.ds(b, 1), :].rearrange("p a n -> p (a n)"))
                        elif g == 1:
                            for c in range(4):
                                value(3 + c, P, wst[u][:, c, 256:512])
                        else:
                            for c in range(4):
                                k = 4 * (g - 2) + c
                                mm = value(7 + k, P, vpg[:, k, :], last=k == NPAGE - 1)
                                if k == 0:
                                    mm.then_inc(win_used[u], 1)
                    mm.then_inc(m["o_ready"], 1)
                    pe.wait_ge(m["o_copied"], b + 2)
                    pe.transpose(PS[4][:, 256:384], osb[:, 0:P], ident).then_inc(V_used, 1)
                    pe.transpose(PS[4][:, 384:512], osb[:, P:256], ident).then_inc(m["o_turned"], 1)
            pe.wait_ge(m["o_out"], 2 * NB)
            slabs(4, 4, pair)
            ffn()
            norm()
            for g in range(6):
                t, h = g // 2, g % 2
                at, n = TOK_TILES[t]
                for k in range(4):
                    mm = pe.transpose(PS[g][0:n, k * P:k * P + P], hT[:, 4 * h + k, at:at + n], ident)
                mm.then_inc(m["y_turned"], 1)

        def act_program(act):
            seen = Seen()
            slab = [0]

            def norm_parts(first_wait, src, square=True):
                first_wait()
                act.activation(sq[:, :, :], src[:, :, :], ACT.Square).then_inc(m["sq_ready"], 1)
                seen.wait(act, m["mean_ready"])
                act.activation(stat[:, 1, :], PS[4][:, 0:T], ACT.Sqrt, bias=eps[:, 0:1]).then_inc(m["std_ready"], 1)

            def norm():
                norm_parts(lambda: act.wait_ge(m["evac_done"], slab[0] + CREDIT), xT)

            def glu(n, half, func):
                base = slab[0]
                with act.Fori(0, n // 2) as i:
                    for u in range(2):
                        act.wait_ge(m["slab_used"], i * 2 + (base + u + 1 + CREDIT))
                        act.activation(tmp[:, u, :], PS[2 * u + half][:, 0:T], func).then_inc(m["act_glu"], 1)
                slab[0] += n

            def ffn():
                norm()
                glu(FT, 0, ACT.Silu)
                slab[0] += KT

            def compress(n, b, kout, vout, loaded):
                def relay(t):
                    j, c = t // 2, t % 2
                    if t % 8 == 0:
                        loaded(t // 8)
                    src = STG[j // 4][0:n, 2 * (j % 4):2 * (j % 4) + 2, c * 256:c * 256 + 256]
                    s = act.activation(RL[0:n, c, :].rearrange("p (g s d) -> p s g d", g=NKV, s=2),
                                       src.rearrange("p s (g d) -> p s g d", g=NKV), ACT.Copy)
                    s.then_inc(m["rl_ready"], 1)

                relay(0)
                relay(1)
                for t in range(16):
                    j, c = t // 2, t % 2
                    act.wait_ge(m["rt_turned"], b * 16 + (t + 1))
                    act.activation(RT[:, j % 2, c, 0:4 * n], PS[5 + c][:, 0:4 * n], ACT.Copy) \
                        .then_inc(m["rt_ready"], 1)
                    if t < 14:
                        relay(t + 2)
                    if t in (6, 14):
                        act.wait_ge(m["rl_ready"], b * 16 + (8 + 8 * (t // 14)))
                        act.sem_inc(half_used[t // 14], 1)
                for c in range(2):
                    act.wait_ge(m["z_ready"], b * 2 + (c + 1))
                    act.activation(hgel[:, c, 0:4 * n], PS[(7, 4)[c]][:, 0:4 * n], ACT.Gelu_apprx_tanh,
                                   bias=cst[:, c:c + 1]).then_inc(m["gelu_ready"], 1)
                act.wait_ge(m["kv_ready"], b * 2 + 1)
                act.activation(kout, PS[0][:, 0:2 * n].rearrange("p (q n) -> p q n", q=2), ACT.Identity,
                               bias=vecs[:, V_B2:V_B2 + 1]).then_inc(m["kv_out"], 1)
                act.wait_ge(m["kv_ready"], b * 2 + 2)
                act.activation(vout, PS[1][0:n, 0:256], ACT.Copy).then_inc(m["kv_out"], 1)

            act.sem_inc(m["rt_ready"], CREDIT)
            for u in range(2):
                act.sem_inc(half_used[u], CREDIT_H)
            act.wait_ge(m["pool_step"], 3)
            act.wait_ge(m["turned_out"], 12)
            norm_parts(lambda: None, xT)
            glu(FT, 0, ACT.Silu)
            slab[0] += KT
            norm()
            glu(KT, 1, ACT.Sigmoid)
            act.wait_ge(m["conv_turned"], 1)
            for h in range(2):
                act.activation(convS[:, 512 * h:512 * h + 512], PS[h][0:TS, :], ACT.Copy).then_inc(m["conv_rows"], 1)
                act.activation(convP[:, 512 * h:512 * h + 512], PS[2 + h][0:HIST, :], ACT.Copy) \
                    .then_inc(m["conv_rows"], 1)
            with act.Fori(0, NB) as b:
                compress(P, b, kcT[:, bass.ds(b, 1), :, :].rearrange("p a q n -> p (a q) n"),
                         vc[:, bass.ds(b, 1), :].rearrange("p a n -> p (a n)"),
                         lambda u: act.wait_ge(gathered[u], b * 128 + 128))
            seen.wait(act, m["mean_ready"])
            norm_parts(lambda: seen.wait(act, m["cen_ready"]), hT)
            seen.wait(act, m["cen_ready"])
            for k in range(KT):
                s = act.activation(hT[:, k, :], hT[:, k, :], ACT.Silu, scale=vecs[:, V_LNG + k:V_LNG + k + 1],
                                   bias=vecs[:, V_LNB + k:V_LNB + k + 1])
            s.then_inc(m["h_ready"], 1)
            slab[0] += 4
            ffn()
            norm()
            slab[0] += 6
            for i in range(4):
                act.wait_ge(m["kT_turned"], i + 1)
                act.activation(kT[:, i // 2, i % 2, :], PS[4 + i][:, 0:T], ACT.Copy).then_inc(m["kT_out"], 1)
            ffn()
            compress(NCP, NB, kcTp[:, :, :], vcp[:, :], lambda u: act.wait_ge(m["prow_loaded"], 32))
            norm()
            slab[0] += 4
            act.wait_ge(m["gate_logits"], 1)
            act.activation(gateP[:, :, :], PS[5][:, 0:96].rearrange("p (t n) -> p t n", t=2), ACT.Sigmoid) \
                .then_inc(m["gate_sig"], 1)
            act.wait_ge(m["gate_logits"], 2)
            act.activation(gsig[:, :], PS[6][0:NH, 0:3 * TS], ACT.Sigmoid).then_inc(m["gate_sig"], 1)

            for q in range(2):
                with act.Fori(0, NZ) as z:
                    unit = z * 4 + 16 * q

                    def exps(w):
                        v, n = w % 2, P * (w % 2 + 1)
                        act.wait_ge(m["p_max"], unit + (w + 1))
                        for r in range(3):
                            x = SP_[:, v, 512:528] if r == 0 else SP_[:, v, 256 * (r - 1):256 * (r - 1) + n]
                            e = act.activation(x, x, ACT.Exp, bias=small[:, v, r:r + 1],
                                               accum_out=small[:, v, 4 + r:5 + r] if r else None)
                        e.then_inc(m["p_exp"], 1)

                    def probs(w):
                        v, t = w % 2, w % 2
                        act.wait_ge(m["p_turned"], unit + (w + 1))
                        act.activation(PTp[:, v, 0:2 * (t + 1), :].rearrange("p c n -> p (c n)"),
                                       PS[4][:, 0:256 * (t + 1)], ACT.Copy)
                        act.activation(PTp[0:NCP, v, 4, :], PS[5][0:NCP, 0:P], ACT.Copy).then_inc(m["p_PT"], 1)

                    exps(0)
                    for w in range(4):
                        if w < 3:
                            exps(w + 1)
                        probs(w)

            for s, n in ((m["kt_out0"], 1), (m["pt_out"], CREDIT), (m["o_copied"], 1)):
                act.sem_inc(s, n)
            with act.Fori(0, NB) as b:
                act.wait_ge(m["c_max"], b + 1)
                act.activation(S[:, S_CMP:S_COLS], S[:, S_CMP:S_COLS], ACT.Exp, bias=small[:, 0, 0:1],
                               accum_out=small[:, 0, 4:5]).then_inc(m["c_exp"], 1)

                def keys(r):
                    act.wait_ge(m["kt_turned"], b * 10 + (r + 1))
                    dst = KTb[:, r // 4, (r % 4) * 512:(r % 4) * 512 + 512] if r < 8 else KTw[:, r - 8, :]
                    act.activation(dst, PS[r % 2][:, :], ACT.Copy).then_inc(m["kt_out0"], 1)
                for r in range(0, 10, 2):
                    keys(r)
                act.wait_ge(m["imp_sum"], b + 1)
                act.activation(ips, PS[4][:, 0:P], ACT.Copy).then_inc(m["imp_sumout"], 1)
                act.wait_ge(m["s_max"], b * 2 + 1)
                act.activation(S[:, S_WIN:S_CMP], S[:, S_WIN:S_CMP], ACT.Exp, bias=small[:, 0, 2:3],
                               accum_out=small[:, 0, 6:7]).then_inc(m["s_exp"], 1)
                act.wait_ge(m["s_max"], b * 2 + 2)
                act.activation(S[:, 0:S_WIN], S[:, 0:S_WIN], ACT.Exp, bias=small[:, 0, 1:2],
                               accum_out=small[:, 0, 5:6]).then_inc(m["s_exp"], 1)
                for g in range(6):
                    act.wait_ge(m["pt_turned"], b * 6 + (g + 1))
                    if g == 0:
                        act.activation(PT[0:TS, 0:256], PS[5][0:TS, 0:256], ACT.Copy)
                        act.activation(PT[:, 256:384], PS[5][:, 256:384], ACT.Copy).then_inc(m["pt_out"], 1)
                    else:
                        at = (3 + 4 * (g - 1)) * P
                        act.activation(PT[:, at:at + 512], PS[5 + g % 2][:, :], ACT.Copy).then_inc(m["pt_out"], 1)
                act.wait_ge(m["o_ready"], b + 1)
                act.activation(osb, PS[7][:, 0:256], ACT.Copy).then_inc(m["o_copied"], 1)
            slab[0] += 4
            ffn()
            norm()

        def dve_program(dve):
            seen = Seen()
            slab = [0]
            steps = [0, 0]

            def did(ins):
                steps[1] += 1
                return ins.then_inc(m["dve_step"], 1)

            def settle():
                dve.wait_ge(m["dve_step"], steps[0] + steps[1])

            def evac(n, work):
                base = slab[0]
                with dve.Fori(0, n // 2) as i:
                    for u in range(2):
                        dve.wait_ge(m["slab_used"], i * 2 + (base + u + 1 + CREDIT))
                        work(i, u, base).then_inc(m["evac_done"], 1)
                slab[0] += n

            glus = [0]

            def gate_rows(i, u, base):
                dve.wait_ge(m["act_glu"], i * 2 + (glus[0] + u + 1))
                return dve.tensor_tensor(gT[:, bass.ds(i * 2 + u, 1), :].rearrange("p a t -> p (a t)"),
                                         PS[2 * u + 1][:, 0:T], tmp[:, u, :], ALU.mult)

            def residual_half(i, u, base):
                x = xT[:, bass.ds(i * 2 + u, 1), :].rearrange("p a t -> p (a t)")
                return dve.scalar_tensor_tensor(x, PS[2 * u][:, 0:T], 0.5, x, ALU.mult, ALU.add)

            def residual_pair(i, u, base):
                x = xT[:, bass.ds(i * 4 + 2 * u, 2), :]
                return dve.tensor_tensor(x, PSA[:, 2 * u:2 * u + 2, 0:T], x, ALU.add)

            def column_sums():
                dve.tensor_reduce(stat[:, 0, :], sq[:, :, :].rearrange("p k t -> p t k"), AX_X, ALU.add) \
                    .then_inc(m["ssum_ready"], 1)

            def norm(g, dst):
                seen.wait(dve, m["sq_ready"])
                column_sums()
                seen.add(m["mean_ready"])
                seen.wait(dve, m["std_ready"])
                did(dve.reciprocal(stat[:, 2, :], stat[:, 1, :]))
                settle()
                for k in range(KT):
                    s = dve.scalar_tensor_tensor(dst[:, k, :], xT[:, k, :], vecs[:, g + k:g + k + 1], stat[:, 2, :],
                                                 ALU.mult, ALU.mult)
                s.then_inc(m["h_ready"], 1)

            def ffn(g):
                norm(g, hT)
                evac(FT, gate_rows)
                glus[0] += FT
                evac(KT, residual_half)

            for s, n in ((m["evac_done"], CREDIT),):
                dve.sem_inc(s, n)
            for k in range(KT):
                dve.wait_ge(m["turned"], k + 1)
                dve.tensor_copy(xT[:, k, :], PS[k][:, 0:T]).then_inc(m["turned_out"], 1)
            for i, (dst, n) in enumerate(((vecs[:, :], V_ROWS), (wdw[:, 0:124], 124), (wdw[:, 124:248], 124))):
                dve.wait_ge(m["turned"], KT + 1 + i)
                dve.tensor_copy(dst, PS[i][:, 0:n]).then_inc(m["turned_out"], 1)
            dve.wait_ge(m["turned"], KT + 4)
            dve.wait_ge(m["turned_out"], 11)
            dve.tensor_tensor(cst[:, :], PS[3][:, 0:2], vecs[:, V_B1:V_B1 + 2], ALU.add).then_inc(m["turned_out"], 1)
            dve.wait_ge(m["ptrow_loaded"], 16 * 9)
            dve.wait_ge(m["consts_loaded"], 16)
            did(dve.tensor_scalar(ptabf[:, :], ptab[:, :], float(2 * PAGE), None, ALU.mult))
            settle()
            for b in range(NB):
                s = dve.tensor_scalar(cidx[:, b * CS:b * CS + CS], cn("token_row"), ptabf[:, b:b + 1], None, ALU.add)
            s.then_inc(m["idx_ready"], 1)
            ffn(V_NORM)
            did(dve.memset(full[:, :, 0:HIST], 0.0))
            for h in range(2):
                for a in range(2):
                    dve.wait_ge(m["turned"], KT + 5 + 2 * h + a)
                    dve.tensor_copy(fullS[:, 4 * a:4 * a + 4, 4 * h:4 * h + 4, 0:HIST],
                                    PS[4 + 2 * h + a][:, 0:480].rearrange("p (k b r) -> p k b r", k=4, b=4)) \
                        .then_inc(m["hist_out"], 1)
            norm(V_NORM + 8, hT)

            def conv_rows_in(i, u, base):
                dve.wait_ge(m["act_glu"], i * 2 + (glus[0] + u + 1))
                k = bass.ds(i * 2 + u, 1)
                dve.tensor_tensor(full[:, k, HIST:PROMPT_W].rearrange("p a t -> p (a t)"),
                                  PS[2 * u][:, 0:SEQ], tmp[:, u, 0:SEQ], ALU.mult)
                return dve.tensor_tensor(fullS[:, k, :, HIST:].rearrange("p a b r -> p (a b) r"),
                                         PS[2 * u][:, SEQ:T].rearrange("p (b r) -> p b r", b=NB),
                                         tmp[:, u, SEQ:].rearrange("p (b r) -> p b r", b=NB), ALU.mult)
            evac(KT, conv_rows_in)
            glus[0] += KT
            dve.wait_ge(m["evac_done"], slab[0] + CREDIT)
            dve.wait_ge(m["hist_out"], 4)
            dve.tensor_copy(vnew.rearrange("p k (b r) -> p k b r", b=NB), fullS[:, :, :, HIST:]) \
                .then_inc(m["vnew_ready"], 1)
            def conv_tiles(k):
                return (hT[:, k, 0:SEQ], lambda tap: full[:, k, bass.ds(tap, SEQ)],
                        hT[:, k, SEQ:].rearrange("p (b r) -> p b r", b=NB),
                        lambda tap: fullS[:, k, :, bass.ds(tap, NQ)])
            for k in range(KT):
                o1, i1, o2, i2 = conv_tiles(k)
                for o, x in ((o1, i1(0)), (o2, i2(0))):
                    dve.tensor_scalar(o, x, wdw[:, k:k + 1], vecs[:, V_BDW + k:V_BDW + k + 1], ALU.mult, ALU.add) \
                        .then_inc(m["conv_step"], 1)
            with dve.Fori(0, TAPS - 1) as j:
                for k in range(KT):
                    o1, i1, o2, i2 = conv_tiles(k)
                    for h, (o, x) in enumerate(((o1, i1), (o2, i2))):
                        dve.wait_ge(m["conv_step"], j * 16 + (2 * k + h + 1))
                        dve.scalar_tensor_tensor(o, x(j + 1), wdw[:, bass.ds(j * KT + (KT + k), 1)], o,
                                                 ALU.mult, ALU.add).then_inc(m["conv_step"], 1)
            dve.wait_ge(m["conv_step"], 16 * TAPS)
            dve.wait_ge(m["conv_turned"], 1)
            dve.tensor_reduce(stat[:, 0, :], hT[:, :, :].rearrange("p k t -> p t k"), AX_X, ALU.add) \
                .then_inc(m["ssum_ready"], 1)
            seen.wait(dve, m["mean_ready"])
            mu = PSA[:, 4:5, 0:T].broadcast_to([P, KT, T])
            dve.tensor_tensor(hT[:, :, :], hT[:, :, :], mu, ALU.subtract).then_inc(m["cen_ready"], 1)
            seen.wait(dve, m["sq_ready"])
            column_sums()
            seen.wait(dve, m["std_ready"])
            did(dve.reciprocal(stat[:, 2, :], stat[:, 1, :]))
            settle()
            dve.tensor_tensor(hT[:, :, :], hT[:, :, :], stat[:, 2:3, :].broadcast_to([P, KT, T]), ALU.mult) \
                .then_inc(m["cen_ready"], 1)
            seen.add(m["mean_ready"])
            seen.add(m["h_ready"])
            evac(4, residual_pair)
            dve.wait_ge(m["conv_stored"], 16 * (NB + 1))
            ffn(V_NORM + 16)
            norm(V_KV, hT)

            def kv_rows(i, u, base):
                c = bass.ds(i * 2 + u, 1)
                dve.tensor_copy(rows[:, :, c, :].rearrange("p t a n -> p (t a) n"),
                                PS[2 * u][:, :].rearrange("p (t n) -> p t n", t=2))
                return dve.tensor_copy(rowsS[:, c, :].rearrange("p a n -> p (a n)"), PS[2 * u + 1][0:TS, 0:256])
            evac(6, kv_rows)
            ffn(V_NORM + 24)
            norm(V_NORM + 32, hT)

            def queries(i, u, base):
                return dve.tensor_scalar(qT[:, bass.ds(i * 4 + 2 * u, 2), :], PSA[:, 2 * u:2 * u + 2, 0:T], QSCALE, None,
                                         ALU.mult)
            evac(4, queries)
            dve.wait_ge(m["evac_done"], slab[0] + CREDIT)
            dve.wait_ge(m["gate_spread"], 1)
            gm = tmp[:, 1, 0:3 * TS].rearrange("p (n q) -> p n q", q=NQ)
            own = cn("own_query").rearrange("p (a q) -> p a q", a=1).broadcast_to([P, 3 * NB, NQ])
            did(dve.tensor_tensor(gm, PS[7][:, 0:3 * TS].rearrange("p (n q) -> p n q", q=NQ), own, ALU.mult))
            settle()
            dve.tensor_reduce(gateS[:, :, :], gm, AX_X, ALU.add).then_inc(m["gate_out"], 1)
            did(dve.memset(qsl[:, :, :], 0.0))
            settle()

            PSTEPS = 20
            pbase = steps[1]
            for q in range(2):
                with dve.Fori(0, NZ) as z:
                    unit = z * 4 + 16 * q
                    steps[0], steps[1] = z * PSTEPS, pbase + q * NZ * PSTEPS
                    start = steps[1]
                    for g in range(2):
                        s = dve.tensor_copy(qsl[g * HD:g * HD + HD, g, :],
                                            qT[g * HD:g * HD + HD, bass.ds(z + q * NZ, 1), 0:SEQ].rearrange("p a t -> p (a t)"))
                    s.then_inc(m["qsl_ready"], 1)

                    def biased(w):
                        g, t, v = w // 2, w % 2, w % 2
                        n = P * (t + 1)
                        head = bass.ds(z + (2 * q + g) * NZ, 1)
                        slope = cn("neg_slope")[:, head]
                        dve.wait_ge(m["p_scores"], unit + (w + 1))
                        full_ = SP_[:, v, 0:512].rearrange("p (r n) -> p r n", r=2)[:, :, 0:n]
                        dve.scalar_tensor_tensor(full_, dist_full[:, t:t + 1, 0:n].broadcast_to([P, 2, n]), slope,
                                                 PSA[:, 2 * v:2 * v + 2, 0:n], ALU.mult, ALU.add)
                        did(dve.scalar_tensor_tensor(SP_[:, v, 512:528], dist_cmp[:, t, :], slope,
                                                     PS[2 * v][:, 256:256 + NCP], ALU.mult, ALU.add))
                        settle()
                        dve.tensor_reduce(small[:, v, 1:3], full_, AX_X, ALU.max, negate=True)
                        dve.tensor_reduce(small[:, v, 0:1], SP_[:, v, 512:528], AX_X, ALU.max, negate=True) \
                            .then_inc(m["p_max"], 1)

                    def scaled(w):
                        g, t, v = w // 2, w % 2, w % 2
                        n = P * (t + 1)
                        sums = small[:, v, 4:7]
                        dve.wait_ge(m["p_exp"], unit + (w + 1))
                        did(dve.scalar_tensor_tensor(SP_[:, v, 512:528], SP_[:, v, 512:528], 1.0, live_cmp[:, t, :],
                                                     ALU.mult, ALU.mult, accum_out=small[:, v, 4:5]))
                        settle()
                        did(dve.tensor_scalar(small[:, v, 8:11], sums, TINY, None, ALU.max))
                        settle()
                        did(dve.reciprocal(small[:, v, 8:11], small[:, v, 8:11]))
                        settle()
                        gates = gateP[:, t, :].rearrange("p (r h) -> p r h", r=3)[:, :, bass.ds(z + (2 * q + g) * NZ, 1)] \
                            .rearrange("p r a -> p (r a)")
                        did(dve.tensor_tensor(small[:, v, 12:15], small[:, v, 8:11], gates, ALU.mult))
                        settle()
                        for r in range(3):
                            x = SP_[:, v, 512:528] if r == 0 else SP_[:, v, 256 * (r - 1):256 * (r - 1) + n]
                            s = dve.tensor_scalar(x, x, small[:, v, 12 + r:13 + r], None, ALU.mult)
                        s.then_inc(m["p_scaled"], 1)

                    biased(0)
                    for w in range(4):
                        if w < 3:
                            biased(w + 1)
                        scaled(w)
                    assert steps[1] - start == PSTEPS, steps[1] - start
                for t in range(2):
                    dve.wait_ge(m["p_out"], 16 * (q + 1))
                    dve.tensor_copy(oP[:, t, 512 * q:512 * q + 512], PS[6 + t][:, :]).then_inc(m["o_evac"], 1)
            for c in range(4):
                dve.wait_ge(m["oP_turned"], c + 1)
                dve.tensor_copy(oT[:, 2 * c:2 * c + 2, 0:SEQ], PS[c][:, :].rearrange("p (k t) -> p k t", k=2)) \
                    .then_inc(m["oP_out"], 1)

            steps[0], steps[1] = 0, pbase + 2 * NZ * PSTEPS
            did(dve.memset(qbd[:, :, :], 0.0))
            did(dve.memset(imp[:, 0, :], FORCE))
            settle()
            dve.sem_inc(m["s_biased"], CREDIT)
            dve.sem_inc(m["kt_out1"], 1)
            dve.wait_ge(m["oP_turned"], 4)
            dve.drain().then_inc(m["attn_in"], 1)
            dve.wait_ge(m["selb_loaded"], 16)
            SSTEPS = 13
            sbase = steps[1]
            with dve.Fori(0, NB) as b:
                steps[0], steps[1] = b * SSTEPS, sbase
                for q in range(2):
                    for g in range(2):
                        grp = 2 * q + g
                        s = dve.tensor_copy(
                            qbd[g * HD:g * HD + HD, q, grp * 32:grp * 32 + 32].rearrange("p (z r) -> p z r", z=NZ),
                            qT[g * HD:g * HD + HD, q * NZ:q * NZ + NZ, bass.ds(b * NQ + SEQ, NQ)])
                s.then_inc(m["qbd_ready"], 1)
                newb = cn("new_bias")[:, bass.ds(b * -NQ + 56, TS)]
                dve.wait_ge(m["s_scores"], b * 6 + 1)
                dve.tensor_tensor(S[:, S_NEW:S_WIN], PS[2][:, 0:TS], newb, ALU.add)
                dve.tensor_tensor(S[:, S_WNEW:S_CMP], PS[2][:, TS:2 * TS], newb, ALU.add)
                dve.tensor_tensor(S[:, S_CMP:S_COLS], PS[2][:, 2 * TS:2 * TS + P], cn("cmp_bias"), ALU.add) \
                    .then_inc(m["s_biased"], 1)
                dve.wait_ge(m["s_biased"], b * 6 + 1 + CREDIT)
                dve.tensor_reduce(small[:, 0, 0:1], S[:, S_CMP:S_COLS], AX_X, ALU.max, negate=True) \
                    .then_inc(m["c_max"], 1)

                def keys(r):
                    dve.wait_ge(m["kt_turned"], b * 10 + (r + 1))
                    dst = KTb[:, r // 4, (r % 4) * 512:(r % 4) * 512 + 512] if r < 8 else KTw[:, r - 8, :]
                    dve.tensor_copy(dst, PS[r % 2][:, :]).then_inc(m["kt_out1"], 1)

                def normalise(src, col):
                    did(dve.tensor_scalar(small[:, 0, 8 + col:8 + col + src], small[:, 0, 4 + col:4 + col + src], TINY,
                                          None, ALU.max))
                    settle()
                    did(dve.reciprocal(small[:, 0, 8 + col:8 + col + src], small[:, 0, 8 + col:8 + col + src]))
                    settle()

                keys(1)
                dve.wait_ge(m["c_exp"], b + 1)
                normalise(1, 0)
                dve.tensor_scalar(S[:, S_CMP:S_COLS], S[:, S_CMP:S_COLS], small[:, 0, 8:9], None, ALU.mult) \
                    .then_inc(m["c_scaled"], 1)
                for r in range(3, 10, 2):
                    keys(r)
                dve.wait_ge(m["imp_sum"], b + 1)
                dve.wait_ge(m["c_scaled"], b + 1)
                did(dve.tensor_scalar(S[:, S_CMP:S_COLS], S[:, S_CMP:S_COLS], gateS[:, 0, bass.ds(b, 1)], None,
                                      ALU.mult))

                def chunk(c):
                    dve.wait_ge(m["s_scores"], b * 6 + (c + 1))
                    at = 512 * (c - 1)
                    dst, bias = (S[:, at:at + 512], selb[:, at:at + 512]) if c < 5 else \
                        (S[:, S_WIN:S_WNEW], cn("win_bias"))
                    dve.tensor_tensor(dst, PS[2 + c % 2][:, :], bias, ALU.add).then_inc(m["s_biased"], 1)
                chunk(1)
                dve.wait_ge(m["imp_ready"], b + 1)
                did(dve.tensor_copy(imp[:, 0, 1:NSEL - 2], PS[4][:, P + 1:P + NSEL - 2]))
                settle()
                dve.sem_inc(m["passed"], 1)
                did(dve.max(out=top8[:, 0, :], in_=imp[:, 0, :]))
                settle()
                dve.sem_inc(m["passed"], 1)
                did(dve.match_replace(out=imp[:, 1, :], in_to_replace=top8[:, 0, :], in_values=imp[:, 0, :],
                                      imm_value=NEG))
                settle()
                dve.sem_inc(m["passed"], 1)
                did(dve.max(out=top8[:, 1, :], in_=imp[:, 1, :]))
                settle()
                dve.sem_inc(m["passed"], 1)
                did(dve.match_replace(out=imp[:, 2, :], in_to_replace=top8[:, 1, :], in_values=imp[:, 1, :],
                                      imm_value=NEG))
                settle()
                did(dve.tensor_scalar(imp[:, 3, :], imp[:, 2, :], NEG / 2, NEG, ALU.is_gt, ALU.mult))
                for c in range(2, 6):
                    chunk(c)
                dve.wait_ge(m["s_biased"], b * 6 + 6 + CREDIT)
                dve.tensor_reduce(small[:, 0, 2:3], S[:, S_WIN:S_CMP], AX_X, ALU.max, negate=True) \
                    .then_inc(m["s_max"], 1)
                settle()
                sblk = S[:, 0:PAST].rearrange("p (j l) -> p j l", l=SB)
                drop = imp[:, 3, 0:NSEL - 1].rearrange("p (j a) -> p j a", a=1).broadcast_to([P, NSEL - 1, SB])
                did(dve.tensor_tensor(sblk, sblk, drop, ALU.add))
                settle()
                dve.tensor_reduce(small[:, 0, 1:2], S[:, 0:S_WIN], AX_X, ALU.max, negate=True) \
                    .then_inc(m["s_max"], 1)
                dve.wait_ge(m["s_exp"], b * 2 + 2)
                normalise(2, 1)
                did(dve.tensor_tensor(small[:, 0, 12:14], small[:, 0, 9:11], gateS[:, 1:3, bass.ds(b, 1)]
                                      .rearrange("p r a -> p (r a)"), ALU.mult))
                settle()
                dve.tensor_scalar(S[:, S_WIN:S_CMP], S[:, S_WIN:S_CMP], small[:, 0, 13:14], None, ALU.mult)
                dve.tensor_scalar(S[:, 0:S_WIN], S[:, 0:S_WIN], small[:, 0, 12:13], None, ALU.mult) \
                    .then_inc(m["s_scaled"], 1)
                dve.wait_ge(m["o_turned"], b + 1)
                ob = PS[4][:, 256:512]
                for q in range(2):
                    for g in range(2):
                        grp = 2 * q + g
                        s = dve.tensor_copy(
                            oT[g * HD:g * HD + HD, q * NZ:q * NZ + NZ, bass.ds(b * NQ + SEQ, NQ)],
                            ob[g * HD:g * HD + HD, q * P + grp * 32:q * P + grp * 32 + 32].rearrange("p (z r) -> p z r", z=NZ))
                        if q:
                            s.then_inc(m["o_out"], 1)
                assert steps[1] - sbase == SSTEPS
            evac(4, residual_pair)
            ffn(V_NORM + 40)
            norm(V_FINAL, hT)
            for g in range(6):
                t, h = g // 2, g % 2
                at, n = TOK_TILES[t]
                dve.wait_ge(m["y_turned"], g + 1)
                dve.tensor_copy(yout[0:n, t, h * 512:h * 512 + 512], PS[g][0:n, :]).then_inc(m["y_out"], 1)

        SLAB_KV = 2 * (FT + KT) + KT + 4 + 6

        with nc.Block() as block:
            @block.sync
            def _(sp):
                sp_program(sp)

            @block.gpsimd
            def _(pool):
                pool_program(pool)

            @block.scalar
            def _(act):
                act_program(act)

            @block.vector
            def _(dve):
                dve_program(dve)

            @block.tensor
            def _(pe):
                pe_program(pe)


_OUTS = [((1, SEQ, D), "y_prompt"), ((NB, NQ, D), "y_sample"), ((1, SEQ, 4, NKV, HD), "kv_prompt"),
         ((NB, NQ, 4, NKV, HD), "kv_sample"), ((1, SEQ, 2, NKV, HD), "win_prompt"),
         ((NB, WIN, 2, NKV, HD), "win_sample"), ((1, 1, HIST, D), "conv_prompt"), ((1, NB, HIST, D), "conv_sample")]


def kernel(**inputs):
    import concourse.bacc as bacc
    from concourse.bass_utils import run_bass_kernel_spmd

    nc = bacc.Bacc("TRN2", target_bir_lowering=False, num_devices=1)
    table, where = host_constants()
    arrays, ins = {}, {}
    for name, a in {**inputs, "const": table}.items():
        a = np.ascontiguousarray(a)
        arrays[f"in_{name}"] = a
        ins[name] = nc.dram_tensor(f"in_{name}", a.shape, mybir.dt.from_np(a.dtype), kind="ExternalInput").ap()
    outs = [nc.dram_tensor(f"out_{name}", list(shape), F32, kind="ExternalOutput").ap() for shape, name in _OUTS]
    program(nc, ins, outs, where)
    r = run_bass_kernel_spmd(nc, [arrays], core_ids=[0])
    return tuple(r.results[0][f"out_{name}"] for _, name in _OUTS)
```

```python
from contextlib import ExitStack

import numpy as np

import concourse.bass as bass
from concourse import mybir
from concourse.alu_op_type import AluOpType as ALU

ACT = mybir.ActivationFunctionType
F32 = mybir.dt.float32
F32R = mybir.dt.float32r
I32 = mybir.dt.int32
AX_X = mybir.AxisListType.X

P = 128
D = 1024
KT = D // P
SEQ = 256
NB = 8
NQ = 8
TS = NB * NQ
T = SEQ + TS
FF = 2816
FT = FF // P
TAPS = 31
HIST = TAPS - 1
NKV = 4
NZ = 4
NH = NKV * NZ
HD = 64
PAGE = 128
NPAGE = 16
PAST = NPAGE * PAGE
NPOOL = 160
CS = 16
NCH = PAST // CS
NCP = SEQ // CS
SB = 64
NSEL = 33
WIN = 512
WR = WIN // P
EPS = 1e-6
NEG = -1e30
FORCE = 1e9
FAR = 1e33
TINY = 1e-30
QSCALE = HD ** -0.5

PROMPT_W = HIST + SEQ
SAMPLE_W = HIST + NQ
FULL_W = PROMPT_W + NB * SAMPLE_W
TOK_TILES = ((0, P), (P, P), (SEQ, TS))

V_NORM, V_KV, V_FINAL, V_BDW, V_LNG, V_LNB = 0, 48, 56, 64, 72, 80
V_B1, V_B2, V_PE, V_ROWS = 88, 90, 91, 123

S_SEL, S_NEW, S_WIN, S_WNEW, S_CMP = 0, PAST, PAST + TS, PAST + TS + WIN, PAST + 2 * TS + WIN
S_COLS = S_CMP + P
CREDIT = 2


def host_constants():
    f = np.float32
    p = np.arange(P)
    slope = np.exp2(f(-8.0) * (np.arange(NH, dtype=f) + f(1)) / f(NH)).astype(f)
    g, z, q = p // 32, p // 8 % 4, p % 8
    sl = slope[g * NZ + z][:, None]
    qpos = (PAST + q)[:, None]
    n = np.arange(P)[None]
    cmp_bias = -(sl * (qpos - (n * CS + 31)).astype(f))
    cmp_bias[:, P - 1] = NEG
    sel_bias = -(sl * (qpos - np.arange(PAST)[None]).astype(f))
    r, pp = np.divmod(np.arange(WIN), P)
    dist = qpos - (PAST - WIN + pp * WR + r)[None]
    win_bias = np.where(dist < WIN, -(sl * dist.astype(f)), f(NEG))
    k = np.arange(120)[None] - 56
    dist = q[:, None] - k
    new_bias = np.where((k >= 0) & (k < NQ) & (dist >= 0), -(sl * dist.astype(f)), f(NEG))
    cs, ss = np.arange(P)[:, None] * CS, np.arange(NSEL)[None] * SB
    overlap = np.clip(np.minimum(cs + 32, ss + SB) - np.maximum(cs, ss), 0, 32).astype(f) / f(32)
    overlap[P - 1] = 0
    t = np.arange(SEQ).reshape(2, P)
    dist = t[:, :, None] - np.arange(SEQ)
    dist_full = np.where(dist >= 0, dist, FAR).transpose(1, 0, 2)
    dist = t[:, :, None] - (np.arange(NCP) * CS + 31)
    live = (dist >= 0) & (np.arange(NCP) < NCP - 1)
    dist_cmp = np.where(live, dist, FAR).transpose(1, 0, 2)
    live_cmp = live.transpose(1, 0, 2)
    parts = [
        ("ident", np.eye(P)), ("mean", np.full((P, P), 1 / D)),
        ("zsum", (g[:, None] == g[None]) & (q[:, None] == q[None])),
        ("overlap", overlap),
        ("head_rows", np.arange(P)[:, None] == (p // 8)[None]),
        ("own_query", q[:, None] == np.arange(NQ)[None]),
        ("token_row", (p % 8)[:, None] * 32 + np.arange(CS)[None] * 2),
        ("neg_slope", np.broadcast_to(-slope, (P, NH))),
        ("cmp_bias", cmp_bias), ("new_bias", new_bias), ("win_bias", win_bias),
        ("dist_full", dist_full.reshape(P, -1)), ("dist_cmp", dist_cmp.reshape(P, -1)),
        ("live_cmp", live_cmp.reshape(P, -1)), ("sel_bias", sel_bias),
    ]
    where, at = {}, 0
    for name, a in parts:
        where[name] = (at, a.shape[1])
        at += a.shape[1]
    return np.concatenate([a.astype(f) for _, a in parts], axis=1), where


class Phase:

    def __init__(self, n, dmas, cols, before):
        self.n, self.dmas, self.cols = n, dmas, cols
        self.base = before.end if before else 0
        self.loaded0 = before.loaded0 + 16 * before.dmas * before.n // 2 if before else 0
        self.end = self.base + n

    def upto(self, i, u, ahead=0):
        return i * 2 + (self.base + 2 * ahead + u + 1)

    def loaded(self, i, ahead=0):
        return i * (16 * self.dmas) + (self.loaded0 + 16 * self.dmas * (ahead + 1))


def slab_phases():
    up, down = (FT, 2, 2 * D), (2 * KT, 1, FT // 2 * P)
    wide = 2 * D
    order = [("up00", up), ("down00", down), ("pw1", (KT, 2, wide)), ("pw2", (4, 1, wide)), ("up01", up),
             ("down01", down), ("kv", (6, 1, wide)), ("up10", up), ("down10", down), ("q", (4, 4, wide)),
             ("o", (4, 4, wide)), ("up11", up), ("down11", down)]
    phases, last = {}, None
    for name, shape in order:
        last = phases[name] = Phase(*shape, last)
    return phases


class Seen:

    def __init__(self):
        self.n = {}

    def __getitem__(self, sem):
        return self.n.get(sem.name, 0)

    def add(self, sem, k=1):
        self.n[sem.name] = self[sem] + k
        return self[sem]

    def wait(self, eng, sem, k=1):
        eng.wait_ge(sem, self.add(sem, k))


def program(nc, ins, outs, where):
    with ExitStack() as ctx:
        def sb(name, *shape, dt=F32):
            return ctx.enter_context(nc.sbuf_tensor(name, list(shape), dt))

        def both(name, n):
            with nc.sbuf_tensor(name + "_f32", [P, n], F32) as f:
                pass
            return f, sb(name + "_f32r", P, n, dt=F32R)

        def sem(name):
            return ctx.enter_context(nc.semaphore(name))

        const = sb("const", P, where["sel_bias"][0])
        xT = sb("xT", P, KT, T)
        W = sb("W", P, 2, 2 * D)
        SF, SR = both("S", 8 * D)
        HF, HR = both("H", 2 * KT * T)
        GF, GR = both("G", 14968)
        kcT = sb("kcT", P, NB, 2, P)
        vc = sb("vc", P, NB, 256)
        kcTp = sb("kcTp", P, 2, NCP)
        vcp = sb("vcp", NCP, 256)
        rows = sb("rows", P, 2, 6, 256)
        rowsS = sb("rowsS", TS, 6, 256)
        kT = sb("kT", P, 2, 2, T)
        w2 = sb("w2", P, 2, HD)
        b2v = sb("b2v", 1, 256)
        ones = sb("ones", 1, P)
        wg = sb("wg", P, KT, 48)
        wgh, wgl = sb("wgh", P, KT, 48, dt=F32R), sb("wgl", P, KT, 48, dt=F32R)
        vecs = sb("vecs", P, V_ROWS)
        wdw = sb("wdw", P, TAPS * KT)
        cst, cst_part = sb("cst", P, 2), sb("cst_part", P, 2)
        eps = sb("eps", P, 1)
        warm = sb("warm", P, 32)
        stat = sb("stat", P, 3, T)
        tmp = sb("tmp", P, 4, T)
        ptab = sb("ptab", P, NB, dt=I32)
        ptabf = sb("ptabf", P, NB)
        ptrow = sb("ptrow", 1, P, dt=I32)
        cidx = sb("cidx", P, NB * CS, dt=I32)
        cslot = sb("cslot", P, CS, dt=I32)
        gateP = sb("gateP", P, 2, 48)
        gateS = sb("gateS", P, 3, NB)
        gsig = sb("gsig", NH, 3 * TS)
        small = sb("small", P, 4, 16)
        imp = sb("imp", P, 4, NSEL)
        top8 = sb("top8", P, 2, 8)
        PSA = ctx.enter_context(nc.psum_tensor("PSA", [P, 8, 512], F32))
        PS = [PSA[:, i, :] for i in range(8)]

        def cn(name, n=P):
            a, w = where[name]
            return const[0:n, a:a + w]

        ident, meanm = cn("ident"), cn("mean")
        dist_full = cn("dist_full").rearrange("p (q k) -> p q k", q=2)
        dist_cmp = cn("dist_cmp").rearrange("p (q k) -> p q k", q=2)
        live_cmp = cn("live_cmp").rearrange("p (q k) -> p q k", q=2)
        def area(a, at, *shape):
            n = int(np.prod(shape))
            names = "abcd"[:len(shape)]
            return a[:, at:at + n].rearrange(f"p ({' '.join(names)}) -> p {' '.join(names)}",
                                             **dict(zip(names, shape))) if len(shape) > 1 else a[:, at:at + n]

        def slab_views(*shape):
            n = int(np.prod(shape))
            names = "abc"[:len(shape)]
            pat = f"p ({' '.join(names)}) -> p {' '.join(names)}"
            kw = dict(zip(names, shape))
            return [[a[:, 0:n].rearrange(pat, **kw) for a in (W[:, u, :], SR[:, u * 2 * D:u * 2 * D + 2 * D],
                                                              SR[:, (u + 2) * 2 * D:(u + 3) * 2 * D])] for u in range(2)]
        flat_slab = [[W[:, u, :], SR[:, u * 2 * D:u * 2 * D + 2 * D], SR[:, (u + 2) * 2 * D:(u + 3) * 2 * D]]
                     for u in range(2)]
        Wgu = slab_views(KT, 2, P)
        Wdn = slab_views(FT // 2, P)
        W256 = slab_views(KT, 256)
        RAW, HI, LO = range(3)
        hR = [area(HR, p * KT * T, KT, T) for p in range(2)]
        gR = [area(GR, p * FT * T, FT, T) for p in range(2)]
        oT = area(HF, KT * T, KT, T)
        csum = oT
        xin = area(GF, 0, 3, D)
        full = area(GF, 0, KT, FULL_W)
        fullS = full[:, :, PROMPT_W:].rearrange("p k (b r) -> p k b r", b=NB)
        rowsf = rows[:, :, :, :].rearrange("p t c d -> p (t c d)")
        convS = rowsf[0:TS, 0:D]
        convP = rowsf[0:HIST, D:2 * D]
        hist = rowsf[0:120, 0:2 * D].rearrange("p (h d) -> p h d", h=2)
        vr = rowsf[:, 2 * D:2 * D + 3 * P]
        STG = [area(GF, 4720 + u * 4096, 8, 512) for u in range(2)]
        w1 = W[:, :, :].rearrange("p c (j h) -> p c j h", h=P)
        w1s = [area(SR, part * 4096, 2, 16, P) for part in range(2)]
        RTs = area(HR, 0, 2, 2, 514), area(GR, 12912, 2, 2, 514)
        RTp = area(HF, 0, 2, 2, 66)
        hgel = area(W[:, 1, :], 0, 2, 512)
        RL = area(W[:, 1, :], 1024, 2, 512)
        vnew = stat[:, :, :].rearrange("p a t -> p (a t)")[:, 0:KT * TS].rearrange("p (k t) -> p k t", k=KT)
        pages = [area(GF, u * 4096, NPAGE, 256) for u in range(2)]
        kpg, vpg = pages
        STGp = [area(GF, u * 4096, 8, 512) for u in range(2)]
        qT = area(GF, 8192, KT, T)
        w1p = area(GF, 8192 + KT * T, 2, 16, P)
        PT = area(GF, 8192 + KT * T, 23 * P)
        qbd = area(GF, 8192 + KT * T + 23 * P, 2, P)
        selb = area(HF, 0, PAST)
        KTb = area(SF, 0, 2, PAST)
        S = area(SF, 4096, S_COLS)
        KTw = area(SF, 4096 + S_COLS, 2, WIN)
        osb = tmp[:, 0, 0:256]
        ips = tmp[:, 1, 0:P]
        wst = [W[:, u, :].rearrange("p (r c) -> p r c", r=WR) for u in range(2)]
        oP = area(SF, 0, 2, 1024)
        SP_ = area(SF, 4104, 4, 528)
        PTp = area(SF, 4104 + 4 * 528, 2, 5, P)
        qsl = area(SF, 4104 + 4 * 528 + 1280, 2, 256)
        yout = area(SF, 0, 3, D)
        PH = slab_phases()

        names = """hi_ready lo_ready x_step gate_step h_raw h_hi w1_loaded w1p_loaded w1_high w1_low rt_high wg_hi cst_ready passed kv_stored conv_stored consts_loaded vecs_loaded x_loaded misc_loaded hist_loaded slab_used evac_done act_glu
            turned turned_out sq_ready ssum_ready mean_ready std_ready rstd_ready h_ready setup_done
            conv_step ln_step hist_out cen_ready idx_ready slot_ready rt_turned rt_ready rl_ready vnew_ready z_ready gelu_ready
            kv_ready kv_out conv_turned conv_rows stored kT_turned kT_out prow_loaded q_ready
            gate_logits gate_sig gate_spread gate_out gate_mul dve_step
            qsl_ready p_scores p_biased p_max p_exp p_scaled p_turned p_PT p_out o_evac oP_turned oP_out
            win_stored attn_in
            kt_turned kt_out0 kt_out1 s_scores s_biased c_max c_exp c_scaled imp_sum imp_sumout imp_ready
            s_max s_exp s_scaled pt_turned pt_out o_ready o_copied o_turned o_out qbd_ready
            selb_loaded ptrow_loaded y_turned y_out pool_step""".split()
        m = {n: sem(n) for n in names}
        slab_loaded = [sem("slab_loaded0"), sem("slab_loaded1")]
        gathered = [sem("gathered0"), sem("gathered1")]
        half_used = [sem("half_used0"), sem("half_used1")]
        K_loaded, V_loaded, K_used, V_used = map(sem, ("K_loaded", "V_loaded", "K_used", "V_used"))
        win_loaded = [sem("win_loaded0"), sem("win_loaded1")]
        win_used = [sem("win_used0"), sem("win_used1")]

        SQ = 2 * KT
        OUTS_DOWN00 = FT + KT
        OUTS_KV = 2 * (FT + KT) + KT + 4 + 6
        OUTS_DOWN10 = OUTS_KV + FT + KT

        cache = ins["cache_kv"]

        def load_pages(eng, b, c, page, used, loaded):
            eng.wait_ge(used, b + 1)
            eng.sem_inc(m["passed"], 1)
            for k in range(NPAGE):
                n = eng.value_load(ptrow[0:1, bass.ds(b * NPAGE + k, 1)], min_val=0, max_val=NPOOL - 1)
                src = cache[bass.ds(n, 1), :, c, :, :].rearrange("a t g d -> t (a g d)")
                eng.dma_start(page[:, k, :], src).then_inc(loaded, 16)

        def sp_program(sp):
            def slabs(name, load, first=None):
                ph = PH[name]
                if first:
                    for u in range(2):
                        for sem_, n in first[u]:
                            sp.wait_ge(sem_, n)
                        load(0, u)
                with sp.Fori(1 if first else 0, ph.n // 2) as i:
                    for u in range(2):
                        sp.wait_ge(m["lo_ready"], ph.upto(i, u))
                        load(i, u)

            def ffn_up(layer, j):
                wi = ins["w_ff_in"][layer, j].rearrange("(k p) (h n) -> p k h n", p=P, h=2)

                def up(i, u):
                    for h in range(2):
                        sp.dma_start(Wgu[u][RAW][:, :, h, :], wi[:, :, h, bass.ds(i * 256 + u * P, P)]) \
                          .then_inc(slab_loaded[u], 16)

                slabs(f"up{layer}{j}", up)

            def ffn_down(layer, j):
                wo = ins["w_ff_out"][layer, j].rearrange("(k p) n -> p k n", p=P)

                def down(i, u):
                    sp.dma_start(Wdn[u][RAW], wo[:, u * (FT // 2):(u + 1) * (FT // 2), bass.ds(i * P, P)]) \
                      .then_inc(slab_loaded[u], 16)
                slabs(f"down{layer}{j}", down)

            def ffn(layer, j):
                ffn_up(layer, j)
                ffn_down(layer, j)

            first, rest = slice(0, 2 * P), slice(2 * P, const.shape[1])
            sp.dma_start(const[:, first], ins["const"][:, first]).then_inc(m["consts_loaded"], 16)
            sp.dma_start(xin[:, 0:2, :], ins["x_prompt"][0].rearrange("(t p) d -> p t d", p=P)) \
              .then_inc(m["x_loaded"], 16)
            sp.dma_start(xin[0:TS, 2, :], ins["x_sample"].rearrange("b t d -> (b t) d")).then_inc(m["x_loaded"], 16)

            def vload(row, n, src):
                sp.dma_start(vr[row:row + n, 0:P], src).then_inc(m["vecs_loaded"], 16)
            vload(V_NORM, 48, ins["norm_g"].rearrange("l j (k p) -> (l j k) p", p=P))
            vload(V_KV, 8, ins["g_kv"].rearrange("(k p) -> k p", p=P))
            vload(V_FINAL, 8, ins["g_final"].rearrange("(k p) -> k p", p=P))
            for r, name in ((V_BDW, "b_dw"), (V_LNG, "ln_g"), (V_LNB, "ln_b")):
                vload(r, 8, ins[name][0].rearrange("(k p) -> k p", p=P))
            vload(V_B1, 2, ins["b_cmp1"])
            for h in range(2):
                sp.dma_start(vr[V_B2:V_B2 + 1, h * HD:h * HD + HD], ins["b_cmp2"][0:1, :]).then_inc(m["vecs_loaded"], 16)
            vload(V_PE, 32, ins["pe_cmp"].rearrange("c (j s) d -> (c j) (s d)", s=2))
            wd = ins["w_dw"][0].rearrange("w (k p) -> (w k) p", p=P)
            for h in range(2):
                sp.dma_start(vr[0:124, P * (h + 1):P * (h + 2)], wd[124 * h:124 * h + 124]) \
                  .then_inc(m["vecs_loaded"], 16)
            ffn_up(0, 0)
            sp.dma_start(const[:, rest], ins["const"][:, rest]).then_inc(m["consts_loaded"], 16)
            pt = ins["page_table"]
            with nc.allow_non_contiguous_dma(reason="a table of 128 numbers"):
                for r in range(PAGE // CS):
                    sp.dma_start(ptab[r:P:PAGE // CS, :], pt.rearrange("b k -> k b")).then_inc(m["ptrow_loaded"], 16)
            sp.dma_start(ptrow[:, :], pt.rearrange("(a b) k -> a (b k)", a=1)).then_inc(m["ptrow_loaded"], 16)
            for h in range(2):
                sp.dma_start(hist[:, h, :], ins["state_conv"][0].rearrange("(h b) r d -> h (b r) d", h=2)[h]) \
                  .then_inc(m["hist_loaded"], 16)
            for c in range(2):
                sp.dma_start(w2[:, c, :], ins["w_cmp2"][c]).then_inc(m["misc_loaded"], 16)
            for g in range(NKV):
                sp.dma_start(b2v[0:1, g * HD:g * HD + HD], ins["b_cmp2"][1:2, :]).then_inc(m["misc_loaded"], 16)
            sp.dma_start(wg[:, :, :], ins["w_qg"][0][:, D:].rearrange("(k p) n -> p k n", p=P)) \
              .then_inc(m["misc_loaded"], 16)
            ffn_down(0, 0)
            wp = ins["w_pw1"][0].rearrange("(k p) (h n) -> p k h n", p=P, h=2)

            def pw1(i, u):
                for h in range(2):
                    sp.dma_start(Wgu[u][RAW][:, :, h, :], wp[:, :, h, bass.ds(i * 256 + u * P, P)]) \
                      .then_inc(slab_loaded[u], 16)
            slabs("pw1", pw1)
            sp.wait_ge(m["lo_ready"], PH["pw1"].end + CREDIT)
            for c in range(2):
                sp.dma_start(w1[:, c, :, :], ins["w_cmp1"][c].rearrange("(j s) d h -> (s d) j h", s=2)) \
                  .then_inc(m["w1_loaded"], 16)

            def wide(src):
                def load(i, u):
                    sp.dma_start(W256[u][RAW], src[:, :, bass.ds(i * 512 + u * 256, 256)]).then_inc(slab_loaded[u], 16)
                return load
            slabs("pw2", wide(ins["w_pw2"][0].rearrange("(k p) n -> p k n", p=P)),
                  first=[[(m["w1_low"], 2), (m["cst_ready"], 2)], [(m["kv_out"], 2 * NB)]])
            ffn(0, 1)
            slabs("kv", wide(ins["w_kv"].rearrange("(k p) n -> p k n", p=P)))
            ffn(1, 0)
            wq = ins["w_qg"][0].rearrange("(k p) n -> p k n", p=P)

            def queries(i, u):
                for h in range(2):
                    for g in range(2):
                        sp.dma_start(W256[u][RAW][:, :, h * P + g * HD:h * P + g * HD + HD],
                                     wq[:, :, bass.ds(i * 512 + (g * 256 + (2 * u + h) * HD), HD)]) \
                          .then_inc(slab_loaded[u], 16)
            slabs("q", queries)
            sp.wait_ge(m["kv_stored"], 16)
            sp.wait_ge(m["evac_done"], OUTS_DOWN10 + CREDIT)
            for u in range(2):
                src = outs[2][0].rearrange("(n s) c g d -> n s (c g d)", s=CS)[:, 8 * u:8 * u + 8, 0:512]
                sp.dma_start(STGp[u][0:NCP], src).then_inc(m["prow_loaded"], 16)
                sp.dma_start(w1p[:, u, :, :], ins["w_cmp1"][u].rearrange("(j s) d h -> (s d) j h", s=2)) \
                  .then_inc(m["w1p_loaded"], 16)
            sp.wait_ge(m["lo_ready"], PH["q"].end + CREDIT)
            sp.wait_ge(m["kv_out"], 2 * (NB + 1))
            sp.wait_ge(m["gate_logits"], 2)
            sp.dma_start(selb, ins["const"][:, const.shape[1]:]).then_inc(m["selb_loaded"], 16)
            sp.wait_ge(m["ptrow_loaded"], 16 * 9)

            def load_keys(i, off):
                b, u = i * 2 + off, off % 2
                load_pages(sp, b, 2, kpg, K_used, K_loaded)
                sp.wait_ge(win_used[u], i + (off // 2 + 1))
                sp.sem_inc(m["passed"], 1)
                sp.dma_start(W[:, u, :], ins["state_kv_win"].rearrange("b (p r) c g d -> b p (r c g d)", r=WR)
                             [bass.ds(b, 1)].rearrange("a p c -> p (a c)")).then_inc(win_loaded[u], 16)

            load_keys(0, 0)
            with sp.Fori(0, NB // 2 - 1) as i:
                for u in range(2):
                    load_keys(i, u + 1)
            load_keys(NB // 2 - 1, 1)
            wo = ins["w_o"][0].rearrange("(q g z d) n -> q g d z n", q=2, g=2, z=NZ)

            def out_proj(i, u):
                for q in range(2):
                    for g in range(2):
                        sp.dma_start(W256[u][RAW][g * HD:g * HD + HD, q * NZ:q * NZ + NZ, :],
                                     wo[q, g, :, :, bass.ds(i * 512 + u * 256, 256)]).then_inc(slab_loaded[u], 16)
            slabs("o", out_proj, first=[[(win_used[u], 1 + NB // 2)] for u in range(2)])
            ffn(1, 1)

        CREDIT_H = 1

        def pool_program(pool):
            pool.memset(eps[:, :], EPS).then_inc(m["pool_step"], 1)
            pool.memset(ones[:, :], 1.0).then_inc(m["pool_step"], 1)
            pool.memset(HF[:, 0:1], 0.0).then_inc(m["pool_step"], 1)
            pool.wait_ge(m["idx_ready"], 1)
            pool.wait_ge(m["evac_done"], OUTS_DOWN00 + CREDIT)
            pairs = cache.rearrange("n t (h c) g d -> (n t h) (c g d)", h=2)
            with pool.Fori(0, NB) as b:
                for u in range(2):
                    pool.wait_ge(half_used[u], b + 1)
                    pool.tensor_copy(cslot[:, 8 * u:8 * u + 8], cidx[:, bass.ds(b * CS + 8 * u, 8)]) \
                        .then_inc(m["slot_ready"], 1)
                    pool.wait_ge(m["slot_ready"], b * 2 + (u + 1))
                    pool.sem_inc(m["passed"], 1)
                    for s in range(8):
                        pool.indirect_dma_start(
                            out=STG[u][:, s, :], out_offset=None, in_=pairs,
                            in_offset=bass.IndirectOffsetOnAxis(ap=cslot[:, 8 * u + s:8 * u + s + 1], axis=0)) \
                            .then_inc(gathered[u], 16)
            pool.dma_start(outs[5].rearrange("b t c g d -> b (t c g d)")[:, 0:(WIN - NQ) * 512],
                           ins["state_kv_win"].rearrange("b t c g d -> b (t c g d)")[:, NQ * 512:]) \
                .then_inc(m["stored"], 16)
            pool.dma_start(outs[7][0, :, 0:HIST - NQ, :], ins["state_conv"][0, :, NQ:, :]).then_inc(m["stored"], 16)
            pool.wait_ge(m["conv_rows"], 4)
            pool.dma_start(outs[6][0, 0], convP).then_inc(m["conv_stored"], 16)
            for b in range(NB):
                pool.dma_start(outs[7][0, b, HIST - NQ:, :], convS[b * NQ:b * NQ + NQ, :]) \
                    .then_inc(m["conv_stored"], 16)
            pool.wait_ge(m["evac_done"], OUTS_KV + CREDIT)
            flat = [outs[2][0].rearrange("(t p) c g d -> p t (c g d)", p=P),
                    outs[4][0].rearrange("(t p) c g d -> p t (c g d)", p=P)]
            for o, (c, n), done in zip(flat, ((0, 4), (4, 2)), (m["kv_stored"], m["stored"])):
                pool.dma_start(o, rows[:, :, c:c + n, :].rearrange("p t c d -> p t (c d)")).then_inc(done, 16)
            pool.dma_start(outs[3].rearrange("b t c g d -> (b t) (c g d)"),
                           rowsS[:, 0:4, :].rearrange("p c d -> p (c d)")).then_inc(m["stored"], 16)
            for b in range(NB):
                pool.dma_start(outs[5].rearrange("b t c g d -> b t (c g d)")[b, WIN - NQ:, :],
                               rowsS[b * NQ:b * NQ + NQ, 4:6, :].rearrange("p c d -> p (c d)")) \
                    .then_inc(m["stored"], 16)
            pool.wait_ge(m["ptrow_loaded"], 16 * 9)
            pool.wait_ge(m["kv_out"], 2 * (NB + 1))
            with pool.Fori(0, NB) as b:
                load_pages(pool, b, 3, vpg, V_used, V_loaded)
            pool.wait_ge(m["y_out"], 6)
            pool.dma_start(outs[0][0].rearrange("(t p) d -> p t d", p=P), yout[:, 0:2, :]).then_inc(m["stored"], 16)
            pool.dma_start(outs[1].rearrange("b t d -> (b t) d"), yout[0:TS, 2, :]).then_inc(m["stored"], 16)
            pool.wait_ge(m["kv_stored"], 16)
            pool.wait_ge(m["conv_stored"], 16 * (NB + 1))
            pool.wait_ge(m["stored"], 16 * (2 + 2 + NB + 2))

        def pe_program(pe):
            seen = Seen()
            outs_ = [0]
            for s, n in ((m["slab_used"], CREDIT), (K_used, 1), (V_used, 1), (win_used[0], 1), (win_used[1], 1)):
                pe.sem_inc(s, n)

            def product(out, w, x, start, stop):
                pe.matmul(out, w[0], x[0], start=start, stop=False)
                pe.matmul(out, w[0], x[1], start=False, stop=False)
                return pe.matmul(out, w[1], x[0], start=False, stop=stop)

            def slabs(name, work, own_outs=True, first=None):
                ph, o = PH[name], outs_[0]

                def pair_of_slabs(i, first=None):
                    for u in range(2):
                        pe.wait_ge(m["lo_ready"], ph.upto(i, u) + CREDIT)
                        if own_outs:
                            pe.wait_ge(m["evac_done"], i * 2 + (o + u + 1))
                        work(i, u, first if u == 0 else None).then_inc(m["slab_used"], 1)
                pair_of_slabs(0, first)
                with pe.Fori(1, ph.n // 2) as i:
                    pair_of_slabs(i)
                outs_[0] += ph.n

            def gated(i, u, first):
                for k in range(KT):
                    if first:
                        first(k)
                    for h in range(2):
                        mm = product(PS[2 * u + h][:, 0:T], [Wgu[u][p][:, k, h, :] for p in (HI, LO)],
                                     [x[:, k, :] for x in hR], k == 0, k == KT - 1)
                return mm

            def pair(i, u, first):
                for k in range(KT):
                    if first:
                        first(k)
                    for h in range(2):
                        mm = product(PS[2 * u + h][:, 0:T], [W256[u][p][:, k, h * P:h * P + P] for p in (HI, LO)],
                                     [x[:, k, :] for x in hR], k == 0, k == KT - 1)
                return mm

            def down(name):
                ph, o = PH[name], outs_[0]

                def tile(i, u, gate_rows=None):
                    pe.wait_ge(m["evac_done"], i * 2 + (o + u + 1))
                    for h in range(2):
                        pe.wait_ge(m["lo_ready"], i * 4 + (ph.base + 2 * u + h + 1 + CREDIT))
                        if gate_rows and h:
                            pe.wait_ge(m["evac_done"], gate_rows)
                        for k in range(FT // 2):
                            kk = h * (FT // 2) + k
                            mm = product(PS[2 * u][:, 0:T], [Wdn[h][p][:, k, :] for p in (HI, LO)],
                                         [x[:, kk, :] for x in gR], kk == 0, kk == FT - 1)
                        mm.then_inc(m["slab_used"], 1)
                tile(0, 0, outs_[0] + CREDIT)
                tile(0, 1)
                with pe.Fori(1, KT // 2) as i:
                    for u in range(2):
                        tile(i, u)
                outs_[0] += KT

            def kv(i, u, first):
                for t, (at, n) in enumerate(TOK_TILES):
                    out = PS[2 * u][:, t * 256:t * 256 + 256] if t < 2 else PS[2 * u + 1][0:n, 0:256]
                    for k in range(KT):
                        if first and t == 0:
                            first(k)
                        mm = product(out, [x[:, k, at:at + n] for x in hR], [W256[u][p][:, k, :] for p in (HI, LO)],
                                     k == 0, k == KT - 1)
                return mm

            def channel_mean(ready, bank=4):
                seen.wait(pe, *ready)
                pe.matmul(PS[bank][:, 0:T], meanm, stat[:, 0, :], start=True, stop=True).then_inc(m["mean_ready"], 1)

            def rows_in():
                n = seen.add(m["h_ready"], KT) - KT
                return lambda k: pe.wait_ge(m["h_ready"], n + k + 1)

            def ffn(name, steps):
                if steps:
                    channel_mean((m["x_step"], steps))
                slabs("up" + name, gated, first=rows_in())
                down("down" + name)

            class Compression:

                def __init__(self, n, layer):
                    self.n, self.layer = n, layer

                def turn(self, b, t):
                    n, c = self.n, t % 2
                    pe.wait_ge(m["rt_ready"], b * 16 + (t + 1))
                    pe.wait_ge(m["rl_ready"], b * 16 + (t + 1))
                    for g in range(NKV):
                        tr = pe.transpose(PS[5 + c][:, g * n:g * n + n], RL[0:n, c, g * P:g * P + P], ident[0:n, 0:n])
                    tr.then_inc(m["rt_turned"], 1)

                def first_layer(self, b, t):
                    n, j, c = self.n, t // 2, t % 2
                    pe.wait_ge(m["rt_ready"], b * 16 + (t + 1 + CREDIT))
                    if t < 2:
                        if isinstance(b, int) and b == 0:
                            pe.wait_ge(m["w1_low"], 2)
                        else:
                            pe.wait_ge(m["gelu_ready"], b * 2 + (c - 1))
                    z = PS[(7, 4)[c]][:, 0:4 * n]
                    for h in range(2):
                        mm = self.layer(z, c, 8 * h + j, lambda x: x[:, j % 2, c, h:4 * n + h], t < 2 and h == 0,
                                        j == 7 and h == 1)
                    if t >= 14:
                        mm.then_inc(m["z_ready"], 1)

                def second_layer(self, b):
                    n = self.n
                    pe.wait_ge(m["gelu_ready"], b * 2 + 1)
                    h4 = hgel[:, 0, 0:4 * n].rearrange("p (q g n) -> p g q n", q=2, g=2)
                    for g in range(2):
                        mm = pe.matmul(PS[0][g * HD:g * HD + HD, 0:2 * n], w2[:, 0, :], h4[:, g, :, :],
                                       start=True, stop=True)
                    mm.then_inc(m["kv_ready"], 1)
                    pe.wait_ge(m["gelu_ready"], b * 2 + 2)
                    for g in range(NKV):
                        out = PS[1][0:n, g * HD:g * HD + HD]
                        pe.matmul(out, ones[0:1, 0:n], b2v[0:1, g * HD:g * HD + HD], start=True, stop=False)
                        mm = pe.matmul(out, hgel[:, 1, g * n:g * n + n], w2[:, 1, :], start=False, stop=True)
                    mm.then_inc(m["kv_ready"], 1)

                def batch(self, b, last=None, at12=None):
                    for t in range(16):
                        self.turn(b, t)
                        if t > 1:
                            self.first_layer(b, t - 2)
                        elif last is not None:
                            self.first_layer(last, 14 + t)
                        if t == 4 and last is not None:
                            self.second_layer(last)
                        if t == 12 and at12:
                            at12()

                def end(self, b):
                    self.first_layer(b, 14)
                    self.first_layer(b, 15)
                    self.second_layer(b)

            pe.wait_ge(m["consts_loaded"], 16)
            pe.wait_ge(m["x_loaded"], 32)
            for k in range(KT):
                for t, (at, n) in enumerate(TOK_TILES):
                    mm = pe.transpose(PS[k][:, at:at + n], xin[0:n, t, k * P:k * P + P], ident[0:n, 0:n])
                mm.then_inc(m["turned"], 1)
            pe.wait_ge(m["vecs_loaded"], 16 * 12)
            pe.wait_ge(m["turned_out"], 1)
            pe.transpose(PS[0][:, 0:V_ROWS], vr[0:V_ROWS, 0:P], ident[0:V_ROWS, 0:V_ROWS]).then_inc(m["turned"], 1)
            for h in range(2):
                pe.wait_ge(m["turned_out"], h + 2)
                pe.transpose(PS[h + 1][:, 0:124], vr[0:124, P * (h + 1):P * (h + 2)], ident[0:124, 0:124]) \
                    .then_inc(m["turned"], 1)
            pe.wait_ge(m["turned_out"], KT + 3)
            ffn("00", SQ)
            pe.wait_ge(m["hist_loaded"], 32)
            pe.wait_ge(m["consts_loaded"], 32)
            for h in range(2):
                for a in range(2):
                    for k in range(4):
                        kk = 4 * a + k
                        mm = pe.transpose(PS[4 + 2 * h + a][:, k * 120:k * 120 + 120],
                                          hist[:, h, kk * P:kk * P + P], ident[0:120, 0:120])
                    mm.then_inc(m["turned"], 1)
            pe.wait_ge(m["hist_out"], 1)
            channel_mean((m["x_step"], SQ))
            slabs("pw1", gated, first=rows_in())
            pe.wait_ge(m["vnew_ready"], 1)
            for k in range(KT):
                b, c = k // 4, (k % 4) * P
                pe.transpose(PS[b][0:TS, c:c + P], vnew[:, k, :], ident)
                mm = pe.transpose(PS[2 + b][0:HIST, c:c + P], full[:, k, PROMPT_W - HIST:PROMPT_W], ident)
            mm.then_inc(m["conv_turned"], 1)
            pe.wait_ge(m["conv_rows"], 4)
            pe.wait_ge(m["w1_loaded"], 32)
            for c in range(2):
                for j in range(16):
                    mm = pe.matmul(PS[3][:, c:c + 1], w1[:, c, j, :], vecs[:, V_PE + 16 * c + j:V_PE + 16 * c + j + 1],
                                   start=j == 0, stop=j == 15)
            mm.then_inc(m["turned"], 1)
            pe.wait_ge(m["cst_ready"], 2)
            pe.wait_ge(m["misc_loaded"], 16 * 7)
            cached = Compression(P, lambda z, c, j, rows_, start, stop: product(
                z, [w[:, c, j, :] for w in w1s], [rows_(x) for x in RTs], start, stop))
            cached.batch(0)
            with pe.Fori(0, NB - 2) as b:
                cached.batch(b + 1, b)
            cached.batch(NB - 1, NB - 2, lambda: channel_mean((m["ssum_ready"], 1), 3))
            cached.end(NB - 1)
            channel_mean((m["ln_step"], KT))
            slabs("pw2", pair, first=rows_in())
            ffn("01", SQ)
            channel_mean((m["x_step"], SQ))
            slabs("kv", kv, first=rows_in())
            pe.wait_ge(m["evac_done"], outs_[0] + CREDIT)
            for br in range(2):
                for q in range(2):
                    for t, (at, n) in enumerate(TOK_TILES):
                        src = rows[:, t, 2 + 2 * br, q * P:q * P + P] if t < 2 else rowsS[:, 2 + 2 * br, q * P:q * P + P]
                        mm = pe.transpose(PS[4 + 2 * br + q][:, at:at + n], src, ident[0:n, 0:n])
                    mm.then_inc(m["kT_turned"], 1)
            pe.wait_ge(m["kT_out"], 4)
            ffn("10", 0)
            channel_mean((m["x_step"], SQ))
            slabs("q", pair, first=rows_in())
            for t in range(2):
                for k in range(KT):
                    mm = product(PS[5][:, t * 48:t * 48 + 48], [x[:, k, t * P:t * P + P] for x in hR],
                                 [wgh[:, k, :], wgl[:, k, :]], k == 0, k == KT - 1)
            mm.then_inc(m["gate_logits"], 1)
            for r in range(3):
                for k in range(KT):
                    mm = product(PS[6][0:NH, r * TS:r * TS + TS], [w[:, k, r * NH:r * NH + NH] for w in (wgh, wgl)],
                                 [x[:, k, SEQ:] for x in hR], k == 0, k == KT - 1)
            mm.then_inc(m["gate_logits"], 1)
            pe.wait_ge(m["gate_sig"], 2)
            pe.matmul(PS[7][:, 0:3 * TS], cn("head_rows", NH), gsig[:, :], start=True, stop=True) \
                .then_inc(m["gate_spread"], 1)
            pe.wait_ge(m["evac_done"], outs_[0] + CREDIT)
            pe.wait_ge(m["gate_out"], 1)
            pe.wait_ge(m["w1p_loaded"], 32)
            prompt = Compression(NCP, lambda z, c, j, rows_, start, stop: pe.matmul(
                z, w1p[:, c, j, :], rows_(RTp), start=start, stop=stop))
            prompt.batch(NB)
            prompt.end(NB)
            pe.wait_ge(m["kv_out"], 2 * (NB + 1))

            for q in range(2):
                def unit(z, back, w):
                    return z * 4 + (16 * q + w + 1 - 4 * back)

                def scores(z, w):
                    g, t = w // 2, w % 2
                    n = P * (t + 1)
                    if w == 0:
                        pe.wait_ge(m["qsl_ready"], z + (4 * q + 1))
                    if q or w > 1 or not isinstance(z, int) or z:
                        pe.wait_ge(m["p_max"], unit(z, 0, w) - 2)
                    lhs = qsl[:, g, t * P:t * P + P]
                    X, Y = PS[2 * (w % 2)], PS[2 * (w % 2) + 1]
                    pe.matmul(X[:, 0:n], lhs, kT[:, 0, q, 0:n], start=True, stop=True)
                    pe.matmul(X[:, 256:256 + NCP], lhs, kcTp[:, q, :], start=True, stop=True)
                    pe.matmul(Y[:, 0:n], lhs, kT[:, 1, q, 0:n], start=True, stop=True) \
                        .then_inc(m["p_scores"], 1)

                def turn(z, back, w):
                    t = w % 2
                    pe.wait_ge(m["p_scaled"], unit(z, back, w))
                    if q or w or not isinstance(z, int) or z - back:
                        pe.wait_ge(m["p_PT"], unit(z, back, w) - 1)
                    for c in range(2 * (t + 1)):
                        br, k = c // (t + 1), c % (t + 1)
                        pe.transpose(PS[4][:, c * P:c * P + P], SP_[:, w, br * 256 + k * P:br * 256 + k * P + P], ident)
                    pe.transpose(PS[5][0:NCP, 0:P], SP_[:, w, 512:528], ident).then_inc(m["p_turned"], 1)

                def values(z, back, w):
                    g, t, v = w // 2, w % 2, w % 2
                    grp = 2 * q + g
                    pe.wait_ge(m["p_PT"], unit(z, back, w))
                    out = PS[6 + t][:, bass.ds(z * P + (g * HD - back * P), HD)]
                    for c in range(2 * (t + 1)):
                        br, k = c // (t + 1), c % (t + 1)
                        pe.matmul(out, PTp[:, v, c, :], rows[:, k, 3 + 2 * br, grp * HD:grp * HD + HD],
                                  start=c == 0, stop=False)
                    pe.matmul(out, PTp[0:NCP, v, 4, :], vcp[:, grp * HD:grp * HD + HD], start=False, stop=True) \
                        .then_inc(m["p_out"], 1)

                def step(z, w, first=False):
                    scores(z, w)
                    if w >= 2 or not first:
                        turn(z, w < 2, (w - 2) % 4)
                    if w >= 3 or not first:
                        values(z, w < 3, (w - 3) % 4)

                for w in range(4):
                    step(0, w, first=True)
                with pe.Fori(1, NZ) as z:
                    for w in range(4):
                        step(z, w)
                turn(NZ - 1, 0, 2)
                values(NZ - 1, 0, 1)
                turn(NZ - 1, 0, 3)
                values(NZ - 1, 0, 2)
                values(NZ - 1, 0, 3)
                pe.wait_ge(m["o_evac"], 2 * q + 2)
            for c in range(8):
                for t in range(2):
                    mm = pe.transpose(PS[c // 2][:, (c % 2) * 256 + t * P:(c % 2) * 256 + t * P + P],
                                      oP[:, t, c * P:c * P + P], ident)
                if c % 2:
                    mm.then_inc(m["oP_turned"], 1)
            pe.wait_ge(m["oP_out"], 4)
            pe.wait_ge(m["attn_in"], 1)

            prob_groups = [[(S_NEW, TS), (S_WNEW, TS), (S_CMP, P)], [(S_WIN + c * P, P) for c in range(4)]] + \
                [[(S_SEL + (4 * g + c) * P, P) for c in range(4)] for g in range(4)]

            def turn_probs(b, g):
                if g == 0:
                    pe.wait_ge(m["s_scaled"], b + 1)
                pe.wait_ge(m["pt_out"], b * 6 + (g + 1))
                pe.sem_inc(m["passed"], 1)
                for c, (at, n) in enumerate(prob_groups[g]):
                    mm = pe.transpose(PS[5 + g % 2][0:n, c * P:c * P + P], S[:, at:at + n], ident)
                mm.then_inc(m["pt_turned"], 1)

            def batch_scores(i, off, before):
                b, u = i * 2 + off, off % 2
                last = i * 2 + (off - 1)

                def chunk(c, mms):
                    pe.wait_ge(m["s_biased"], b * 6 + (c + 1))
                    bank = PS[2 + c % 2]
                    for at, n, keys in mms:
                        for q in range(2):
                            mm = pe.matmul(bank[:, at:at + n], qbd[:, q, :], keys(q), start=q == 0, stop=q == 1)
                    mm.then_inc(m["s_scores"], 1)

                def turn_keys(r, tiles):
                    pe.wait_ge((m["kt_out0"], m["kt_out1"])[r % 2], b * 5 + (r // 2 + 1))
                    for c, t in enumerate(tiles):
                        mm = pe.transpose(PS[r % 2][:, c * P:c * P + P], t, ident)
                        if r == 8 and c == 0:
                            mm.then_inc(K_used, 1)
                    mm.then_inc(m["kt_turned"], 1)

                def turn_before(g):
                    if before:
                        turn_probs(last, g)

                turn_before(0)
                turn_before(1)
                pe.wait_ge(m["qbd_ready"], b + 1)
                chunk(0, [(0, TS, lambda q: kT[:, 0, q, SEQ:]), (TS, TS, lambda q: kT[:, 1, q, SEQ:]),
                          (2 * TS, P, lambda q: kcT[:, bass.ds(b, 1), q, :].rearrange("p a n -> p (a n)"))])
                turn_before(2)
                pe.wait_ge(K_loaded, b * 256 + 256)
                for r in range(8):
                    turn_keys(r, [kpg[:, 4 * (r % 4) + c, (r // 4) * P:(r // 4) * P + P] for c in range(4)])
                    if r in (1, 3, 5):
                        turn_before(3 + r // 2)
                pe.wait_ge(win_loaded[u], i * 16 + (off // 2 * 16 + 16))
                for q in range(2):
                    turn_keys(8 + q, [wst[u][:, c, q * P:q * P + P] for c in range(4)])
                pe.wait_ge(m["c_scaled"], b + 1)
                pe.matmul(PS[4][:, 0:P], S[:, S_CMP:S_COLS], cn("zsum"), start=True, stop=True) \
                    .then_inc(m["imp_sum"], 1)
                for o in range(2):
                    pe.wait_ge((m["kt_out0"], m["kt_out1"])[o], b * 5 + 6)
                chunk(1, [(0, 512, lambda q: KTb[:, q, 0:512])])
                pe.wait_ge(m["imp_sumout"], b + 1)
                pe.matmul(PS[4][:, P:P + NSEL], ips, cn("overlap"), start=True, stop=True) \
                    .then_inc(m["imp_ready"], 1)
                for c in range(1, 4):
                    chunk(c + 1, [(0, 512, lambda q: KTb[:, q, c * 512:c * 512 + 512])])
                chunk(5, [(0, WIN, lambda q: KTw[:, q, :])])

            def batch_values(i, off):
                b, u = i * 2 + off, off % 2

                def value(c, n, v, first=False, last=False):
                    return pe.matmul(PS[7][:, 0:256], PT[0:n, c * P:c * P + P], v, start=first, stop=last)

                pe.wait_ge(V_loaded, b * 256 + 256)
                pe.wait_ge(m["o_copied"], b + 1)
                pe.wait_ge(m["pt_out"], b * 6 + (6 + CREDIT))
                value(0, TS, rowsS[:, 3, :], first=True)
                value(1, TS, rowsS[:, 5, :])
                value(2, P, vc[:, bass.ds(b, 1), :].rearrange("p a n -> p (a n)"))
                for c in range(4):
                    mm = value(3 + c, P, wst[u][:, c, 256:512])
                mm.then_inc(win_used[u], 1)
                for k in range(NPAGE):
                    mm = value(7 + k, P, vpg[:, k, :], last=k == NPAGE - 1)
                mm.then_inc(m["o_ready"], 1)
                pe.wait_ge(m["o_copied"], b + 2)
                pe.transpose(PS[4][:, 256:384], osb[:, 0:P], ident).then_inc(V_used, 1)
                pe.transpose(PS[4][:, 384:512], osb[:, P:256], ident).then_inc(m["o_turned"], 1)

            batch_scores(0, 0, False)
            with pe.Fori(0, NB // 2 - 1) as i:
                for u in range(2):
                    batch_scores(i, u + 1, True)
                    batch_values(i, u)
            batch_scores(NB // 2 - 1, 1, True)
            batch_values(NB // 2 - 1, 0)
            for g in range(6):
                turn_probs(NB - 1, g)
            pe.wait_ge(m["o_out"], 2 * (NB - 1))
            batch_values(NB // 2 - 1, 1)
            pe.wait_ge(m["o_out"], 2 * NB)
            slabs("o", pair, first=rows_in())
            ffn("11", SQ)
            channel_mean((m["x_step"], SQ))
            seen.wait(pe, m["h_ready"], 1)
            for g in range(6):
                t, h = g // 2, g % 2
                at, n = TOK_TILES[t]
                for k in range(4):
                    mm = pe.transpose(PS[g][0:n, k * P:k * P + P], oT[:, 4 * h + k, at:at + n], ident)
                mm.then_inc(m["y_turned"], 1)

        def act_program(act):
            seen = Seen()

            warmed = [0]

            def warm_up(func):
                act.activation(warm[:, warmed[0]:warmed[0] + 1], eps[:, :], func)
                warmed[0] += 1

            def split(ph, i, u, ahead=0):
                act.wait_ge(slab_loaded[u], ph.loaded(i, ahead))
                act.wait_ge(m["slab_used"], ph.upto(i, u, ahead))
                act.activation(flat_slab[u][HI][:, 0:ph.cols], flat_slab[u][RAW][:, 0:ph.cols], ACT.Copy) \
                    .then_inc(m["hi_ready"], 1)

            def slabs(name, after, work=None):
                ph = PH[name]
                with act.Fori(0, ph.n // 2 - 1) as i:
                    for u in range(2):
                        if work:
                            work(i, u)
                        split(ph, i, u, 1)
                for u in range(2):
                    if work:
                        work(ph.n // 2 - 1, u)
                    if after:
                        split(PH[after], 0, u)

            glus = [0]

            def glu(name, after, half, func):
                warm_up(func)

                def work(i, u):
                    act.wait_ge(m["slab_used"], PH[name].upto(i, u) + CREDIT)
                    act.activation(tmp[:, u, :], PS[2 * u + half][:, 0:T], func).then_inc(m["act_glu"], 1)
                slabs(name, after, work)

            def root():
                warm_up(ACT.Sqrt)
                seen.wait(act, m["mean_ready"])
                act.activation(stat[:, 1, :], PS[4][:, 0:T], ACT.Sqrt, bias=eps[:, 0:1]).then_inc(m["std_ready"], 1)

            def rows_hi():
                for k in range(KT):
                    seen.wait(act, m["h_raw"])
                    act.activation(hR[0][:, k, :], tmp[:, k % 4, :], ACT.Copy).then_inc(m["h_hi"], 1)

            def ffn(name, after):
                rows_hi()
                glu("up" + name, "down" + name, 0, ACT.Silu)
                slabs("down" + name, after)

            class Compression:

                def __init__(self, n, RT, out_sem, halves, loaded, kout, vout):
                    self.n, self.RT, self.out_sem, self.halves, self.loaded = n, RT, out_sem, halves, loaded
                    self.kout, self.vout = kout, vout

                def relay(self, b, t):
                    n, j, c = self.n, t // 2, t % 2
                    if t % 8 == 0:
                        self.loaded(b, t // 8)
                    src = self.halves[j // 4][0:n, 2 * (j % 4):2 * (j % 4) + 2, c * 256:c * 256 + 256]
                    act.activation(RL[0:n, c, :].rearrange("p (g s d) -> p s g d", g=NKV, s=2),
                                   src.rearrange("p s (g d) -> p s g d", g=NKV), ACT.Copy).then_inc(m["rl_ready"], 1)

                def turned_out(self, b, t):
                    n, j, c = self.n, t // 2, t % 2
                    act.wait_ge(m["rt_turned"], b * 16 + (t + 1))
                    act.activation(self.RT[:, j % 2, c, 0:4 * n], PS[5 + c][:, 0:4 * n], ACT.Copy) \
                        .then_inc(self.out_sem, 1)

                def gelus(self, b):
                    for c in range(2):
                        act.wait_ge(m["z_ready"], b * 2 + (c + 1))
                        act.activation(hgel[:, c, 0:4 * self.n], PS[(7, 4)[c]][:, 0:4 * self.n], ACT.Gelu_apprx_tanh,
                                       bias=cst[:, c:c + 1]).then_inc(m["gelu_ready"], 1)

                def results(self, b):
                    n = self.n
                    act.wait_ge(m["kv_ready"], b * 2 + 1)
                    act.activation(self.kout(b), PS[0][:, 0:2 * n].rearrange("p (q n) -> p q n", q=2), ACT.Identity,
                                   bias=vecs[:, V_B2:V_B2 + 1]).then_inc(m["kv_out"], 1)
                    act.wait_ge(m["kv_ready"], b * 2 + 2)
                    act.activation(self.vout(b), PS[1][0:n, 0:256], ACT.Copy).then_inc(m["kv_out"], 1)

                def batch(self, b, last=None, after=None):
                    for t in range(16):
                        self.turned_out(b, t)
                        if t < 14:
                            self.relay(b, t + 2)
                        elif after is not None:
                            self.relay(after, t - 14)
                        if t in (6, 14):
                            act.wait_ge(m["rl_ready"], b * 16 + (8 + 8 * (t // 14)))
                            act.sem_inc(half_used[t // 14], 1)
                        if t == 1 and last is not None:
                            self.gelus(last)
                        if t == 6 and last is not None:
                            self.results(last)

                def end(self, b):
                    self.gelus(b)
                    self.results(b)

            act.sem_inc(m["rt_ready"], CREDIT)
            for u in range(2):
                act.sem_inc(half_used[u], CREDIT_H)
            for k in range(KT):
                act.wait_ge(m["turned"], k + 1)
                act.activation(xT[:, k, :], PS[k][:, 0:T], ACT.Copy).then_inc(m["turned_out"], 1)
            for i, (dst, n) in enumerate(((vecs[:, :], V_ROWS), (wdw[:, 0:124], 124), (wdw[:, 124:248], 124))):
                act.wait_ge(m["turned"], KT + 1 + i)
                act.activation(dst, PS[i][:, 0:n], ACT.Copy).then_inc(m["turned_out"], 1)
            act.wait_ge(m["pool_step"], 3)
            split(PH["up00"], 0, 0)
            root()
            rows_hi()
            split(PH["up00"], 0, 1)
            glu("up00", "down00", 0, ACT.Silu)
            slabs("down00", "pw1")

            def history(i):
                h, a = i // 2, i % 2
                act.wait_ge(m["turned"], KT + 4 + i)
                act.activation(fullS[:, 4 * a:4 * a + 4, 4 * h:4 * h + 4, 0:HIST],
                               PS[4 + i][:, 0:480].rearrange("p (k b r) -> p k b r", k=4, b=4), ACT.Copy) \
                    .then_inc(m["hist_out"], 1)
            history(0)
            root()
            rows_hi()
            for i in range(1, 4):
                history(i)
            glu("pw1", None, 1, ACT.Sigmoid)
            act.wait_ge(m["conv_turned"], 1)
            for h in range(2):
                act.activation(convS[:, 512 * h:512 * h + 512], PS[h][0:TS, :], ACT.Copy).then_inc(m["conv_rows"], 1)
                act.activation(convP[:, 512 * h:512 * h + 512], PS[2 + h][0:HIST, :], ACT.Copy) \
                    .then_inc(m["conv_rows"], 1)
            act.wait_ge(m["misc_loaded"], 16 * 7)
            act.activation(wgh[:, :, :], wg[:, :, :], ACT.Copy).then_inc(m["wg_hi"], 1)
            act.wait_ge(m["w1_loaded"], 32)
            for c in (1, 0):
                act.activation(w1s[0][:, c, :, :], w1[:, c, :, :], ACT.Copy).then_inc(m["w1_high"], 1)
            act.wait_ge(m["turned"], KT + 8)
            for c in range(2):
                act.activation(cst[:, c:c + 1], PS[3][:, c:c + 1], ACT.Identity,
                               bias=vecs[:, V_B1 + c:V_B1 + c + 1]).then_inc(m["cst_ready"], 1)
            act.wait_ge(m["cst_ready"], 2)
            act.wait_ge(m["w1_low"], 1)
            warm_up(ACT.Gelu_apprx_tanh)
            cached = Compression(P, RTs[0], m["rt_high"], STG, lambda b, u: act.wait_ge(gathered[u], b * 128 + 128),
                                 lambda b: kcT[:, bass.ds(b, 1), :, :].rearrange("p a q n -> p (a q) n"),
                                 lambda b: vc[:, bass.ds(b, 1), :].rearrange("p a n -> p (a n)"))
            cached.relay(0, 0)
            cached.relay(0, 1)
            cached.batch(0, after=1)
            with act.Fori(0, NB - 2) as b:
                cached.batch(b + 1, b, b + 2)
            cached.batch(NB - 1, NB - 2)
            seen.wait(act, m["mean_ready"])
            cached.gelus(NB - 1)
            split(PH["pw2"], 0, 0)
            cached.results(NB - 1)
            for k in range(KT):
                seen.wait(act, m["cen_ready"])
                if k >= 4:
                    act.wait_ge(m["ln_step"], k - 3)
                act.activation(tmp[:, k % 4, :], csum[:, k, :], ACT.Square).then_inc(m["sq_ready"], 1)
            root()
            warm_up(ACT.Silu)

            def silu(k):
                seen.wait(act, m["cen_ready"])
                act.activation(csum[:, k, :], csum[:, k, :], ACT.Silu, scale=vecs[:, V_LNG + k:V_LNG + k + 1],
                               bias=vecs[:, V_LNB + k:V_LNB + k + 1]).then_inc(m["h_raw"], 1)
            silu(0)
            for k in range(KT):
                if k < KT - 1:
                    silu(k + 1)
                seen.wait(act, m["h_raw"])
                act.activation(hR[0][:, k, :], csum[:, k, :], ACT.Copy).then_inc(m["h_hi"], 1)
            split(PH["pw2"], 0, 1)
            slabs("pw2", "up01")
            root()
            ffn("01", "kv")
            root()
            rows_hi()
            slabs("kv", "up10")
            for i in range(4):
                act.wait_ge(m["kT_turned"], i + 1)
                act.activation(kT[:, i // 2, i % 2, :], PS[4 + i][:, 0:T], ACT.Copy).then_inc(m["kT_out"], 1)
            ffn("10", "q")
            root()
            rows_hi()
            slabs("q", None)
            act.wait_ge(m["gate_logits"], 1)
            act.activation(gateP[:, :, :], PS[5][:, 0:96].rearrange("p (t n) -> p t n", t=2), ACT.Sigmoid) \
                .then_inc(m["gate_sig"], 1)
            act.wait_ge(m["gate_logits"], 2)
            act.activation(gsig[:, :], PS[6][0:NH, 0:3 * TS], ACT.Sigmoid).then_inc(m["gate_sig"], 1)

            warm_up(ACT.Gelu_apprx_tanh)
            prompt = Compression(NCP, RTp, m["rt_ready"], STGp, lambda b, u: act.wait_ge(m["prow_loaded"], 32),
                                 lambda b: kcTp[:, :, :], lambda b: vcp[:, :])
            prompt.relay(NB, 0)
            prompt.relay(NB, 1)
            prompt.batch(NB)
            prompt.end(NB)

            for q in range(2):
                def exps(z, w):
                    n = P * (w % 2 + 1)
                    act.wait_ge(m["p_max"], z * 4 + (16 * q + w + 1))
                    for r in range(3):
                        x = SP_[:, w, 512:528] if r == 0 else SP_[:, w, 256 * (r - 1):256 * (r - 1) + n]
                        e = act.activation(x, x, ACT.Exp, bias=small[:, w, r:r + 1],
                                           accum_out=small[:, w, 4 + r:5 + r] if r else None)
                    e.then_inc(m["p_exp"], 1)

                def probs(z, back, w):
                    v, t = w % 2, w % 2
                    act.wait_ge(m["p_turned"], z * 4 + (16 * q + w + 1 - 4 * back))
                    act.activation(PTp[:, v, 0:2 * (t + 1), :].rearrange("p c n -> p (c n)"),
                                   PS[4][:, 0:256 * (t + 1)], ACT.Copy)
                    act.activation(PTp[0:NCP, v, 4, :], PS[5][0:NCP, 0:P], ACT.Copy).then_inc(m["p_PT"], 1)

                for w in range(4):
                    if w >= 2:
                        probs(0, 0, w - 2)
                    exps(0, w)
                with act.Fori(1, NZ) as z:
                    for w in range(4):
                        probs(z, w < 2, (w - 2) % 4)
                        exps(z, w)
                probs(NZ - 1, 0, 2)
                probs(NZ - 1, 0, 3)

            for s, n in ((m["kt_out0"], 1), (m["pt_out"], CREDIT), (m["o_copied"], 1)):
                act.sem_inc(s, n)

            def probs_out(b, g):
                act.wait_ge(m["pt_turned"], b * 6 + (g + 1))
                if g == 0:
                    act.activation(PT[0:TS, 0:256], PS[5][0:TS, 0:256], ACT.Copy)
                    act.activation(PT[:, 256:384], PS[5][:, 256:384], ACT.Copy).then_inc(m["pt_out"], 1)
                else:
                    at = (3 + 4 * (g - 1)) * P
                    act.activation(PT[:, at:at + 512], PS[5 + g % 2][:, :], ACT.Copy).then_inc(m["pt_out"], 1)

            def batch_scores(b, last):
                def keys(r):
                    act.wait_ge(m["kt_turned"], b * 10 + (r + 1))
                    dst = KTb[:, r // 4, (r % 4) * 512:(r % 4) * 512 + 512] if r < 8 else KTw[:, r - 8, :]
                    act.activation(dst, PS[r % 2][:, :], ACT.Copy).then_inc(m["kt_out0"], 1)

                def before(g):
                    if last is not None:
                        probs_out(last, g)
                for g in range(3):
                    before(g)
                keys(0)
                act.wait_ge(m["c_max"], b + 1)
                act.activation(S[:, S_CMP:S_COLS], S[:, S_CMP:S_COLS], ACT.Exp, bias=small[:, 0, 0:1],
                               accum_out=small[:, 0, 4:5]).then_inc(m["c_exp"], 1)
                for r in range(2, 10, 2):
                    if r < 8:
                        before(2 + r // 2)
                    keys(r)
                act.wait_ge(m["imp_sum"], b + 1)
                act.activation(ips, PS[4][:, 0:P], ACT.Copy).then_inc(m["imp_sumout"], 1)
                act.wait_ge(m["s_max"], b * 2 + 1)
                act.activation(S[:, S_WIN:S_CMP], S[:, S_WIN:S_CMP], ACT.Exp, bias=small[:, 0, 2:3],
                               accum_out=small[:, 0, 6:7]).then_inc(m["s_exp"], 1)
                act.wait_ge(m["s_max"], b * 2 + 2)
                act.activation(S[:, 0:S_WIN], S[:, 0:S_WIN], ACT.Exp, bias=small[:, 0, 1:2],
                               accum_out=small[:, 0, 5:6]).then_inc(m["s_exp"], 1)

            def batch_out(b):
                act.wait_ge(m["o_ready"], b + 1)
                act.activation(osb, PS[7][:, 0:256], ACT.Copy).then_inc(m["o_copied"], 1)

            batch_scores(0, None)
            with act.Fori(0, NB - 1) as b:
                batch_scores(b + 1, b)
                batch_out(b)
            for g in range(6):
                probs_out(NB - 1, g)
            act.wait_ge(m["pt_out"], 6 * NB + CREDIT)
            split(PH["o"], 0, 0)
            batch_out(NB - 1)
            act.wait_ge(m["o_out"], 2 * NB)
            act.wait_ge(m["oP_out"], 4)
            for k in range(KT):
                act.activation(hR[0][:, k, :], oT[:, k, :], ACT.Copy).then_inc(m["h_hi"], 1)
            split(PH["o"], 0, 1)
            slabs("o", "up11")
            root()
            ffn("11", None)
            root()

        def dve_program(dve):
            seen = Seen()
            steps = [0, 0]

            def did(ins):
                steps[1] += 1
                return ins.then_inc(m["dve_step"], 1)

            def settle():
                dve.wait_ge(m["dve_step"], steps[0] + steps[1])

            def low(u, upto, cols):
                dve.wait_ge(m["hi_ready"], upto)
                raw, hi, lo = [x[:, 0:cols] for x in flat_slab[u]]
                dve.tensor_tensor(lo, raw, hi, ALU.subtract).then_inc(m["lo_ready"], 1)

            def slabs(name, after, work):
                ph = PH[name]

                def one(i, u, nxt, ahead):
                    dve.wait_ge(m["slab_used"], ph.upto(i, u) + CREDIT)
                    work(i, u)
                    if nxt:
                        low(u, nxt.upto(i if ahead else 0, u, ahead), nxt.cols)
                with dve.Fori(0, ph.n // 2 - 1) as i:
                    for u in range(2):
                        one(i, u, ph, 1)
                for u in range(2):
                    one(ph.n // 2 - 1, u, PH[after] if after else None, 0)
                outs_[0] += ph.n

            outs_ = [0]
            x_steps = [0]

            def squares(x, slot, step):
                dve.tensor_tensor(tmp[:, 2 + slot, :], x, x, ALU.mult).then_inc(m["x_step"], 1)
                dve.wait_ge(m["x_step"], step + 1)
                dve.tensor_tensor(stat[:, 0, :], stat[:, 0, :], tmp[:, 2 + slot, :], ALU.add).then_inc(m["x_step"], 1)

            def down(name, after):
                ph, o, x0 = PH[name], outs_[0], x_steps[0]

                def tile(i, u, last=False):
                    nxt = PH[after] if last and after else ph
                    at = [nxt.base + h + 1 for h in range(2)] if last else \
                        [i * 4 + (ph.base + 2 * u + 2 + h + 1) for h in range(2)]
                    split = not last or after
                    if split:
                        low(0, at[0], nxt.cols)
                    dve.wait_ge(m["slab_used"], i * 4 + (ph.base + 2 * u + 2 + CREDIT))
                    x = xT[:, bass.ds(i * 2 + u, 1), :].rearrange("p a t -> p (a t)")
                    dve.scalar_tensor_tensor(x, PS[2 * u][:, 0:T], 0.5, x, ALU.mult, ALU.add).then_inc(m["evac_done"], 1)
                    dve.wait_ge(m["evac_done"], i * 2 + (o + u + 1 + CREDIT))
                    squares(x, u, i * 4 + (x0 + 2 * u))
                    if split:
                        low(1, at[1], nxt.cols)
                with dve.Fori(0, KT // 2 - 1) as i:
                    for u in range(2):
                        tile(i, u)
                tile(KT // 2 - 1, 0)
                tile(KT // 2 - 1, 1, last=True)
                outs_[0] += KT
                x_steps[0] += SQ

            glus, gates_ = [0], [0]

            def gate_rows(name):
                g0, a0 = gates_[0], glus[0]

                def work(i, u):
                    t, hi, lo = tmp[:, 2 + u, :], *[x[:, bass.ds(i * 2 + u, 1), :].rearrange("p a t -> p (a t)") for x in gR]
                    dve.wait_ge(m["act_glu"], i * 2 + (a0 + u + 1))
                    dve.tensor_tensor(t, PS[2 * u + 1][:, 0:T], tmp[:, u, :], ALU.mult).then_inc(m["gate_step"], 1)
                    dve.wait_ge(m["gate_step"], i * 4 + (g0 + 2 * u + 1))
                    dve.tensor_copy(hi, t).then_inc(m["gate_step"], 1)
                    dve.wait_ge(m["gate_step"], i * 4 + (g0 + 2 * u + 2))
                    dve.tensor_tensor(lo, t, hi, ALU.subtract).then_inc(m["evac_done"], 1)
                slabs("up" + name, "down" + name, work)
                gates_[0] += 2 * FT
                glus[0] += FT

            def residual_pair(name, after):
                o, x0 = outs_[0], x_steps[0]

                def work(i, u):
                    x = xT[:, bass.ds(i * 4 + 2 * u, 2), :]
                    dve.tensor_tensor(x, PSA[:, 2 * u:2 * u + 2, 0:T], x, ALU.add).then_inc(m["evac_done"], 1)
                    dve.wait_ge(m["evac_done"], i * 2 + (o + u + 1 + CREDIT))
                    for k in range(2):
                        squares(xT[:, bass.ds(i * 4 + (2 * u + k), 1), :].rearrange("p a t -> p (a t)"), k,
                                i * 8 + (x0 + 4 * u + 2 * k))
                slabs(name, after, work)
                x_steps[0] += SQ

            def root():
                seen.add(m["mean_ready"])
                seen.wait(dve, m["std_ready"])
                did(dve.reciprocal(stat[:, 2, :], stat[:, 1, :]))
                settle()

            def rows_lo(k, src):
                seen.wait(dve, m["h_hi"])
                dve.tensor_tensor(hR[1][:, k, :], src, hR[0][:, k, :], ALU.subtract).then_inc(m["h_ready"], 1)

            def norm(g):
                for k in range(KT + 1):
                    if k < KT:
                        dve.scalar_tensor_tensor(tmp[:, k % 4, :], xT[:, k, :], vecs[:, g + k:g + k + 1], stat[:, 2, :],
                                                 ALU.mult, ALU.mult).then_inc(m["h_raw"], 1)
                    if k == 0:
                        did(dve.memset(stat[:, 0, :], 0.0))
                    if k:
                        rows_lo(k - 1, tmp[:, (k - 1) % 4, :])
                settle()

            def ffn(name, g, after):
                norm(g)
                gate_rows(name)
                down("down" + name, after)

            for s, n in ((m["evac_done"], CREDIT), (m["lo_ready"], CREDIT)):
                dve.sem_inc(s, n)
            did(dve.memset(stat[:, 0, :], 0.0))
            settle()
            for k in range(KT):
                dve.wait_ge(m["turned_out"], k + 1)
                squares(xT[:, k, :], k % 2, 2 * k)
            x_steps[0] += SQ
            low(0, 1, PH["up00"].cols)
            root()
            dve.wait_ge(m["turned_out"], KT + 1)
            norm(V_NORM)
            low(1, 2, PH["up00"].cols)
            gate_rows("00")
            down("down00", "pw1")
            root()
            norm(V_NORM + 8)
            dve.memset(full[:, :, 0:HIST], 0.0)
            dve.wait_ge(m["ptrow_loaded"], 16 * 9)
            dve.wait_ge(m["consts_loaded"], 16)
            did(dve.tensor_scalar(ptabf[:, :], ptab[:, :], float(2 * PAGE), None, ALU.mult))
            settle()
            for b in range(NB):
                s = dve.tensor_scalar(cidx[:, b * CS:b * CS + CS], cn("token_row"), ptabf[:, b:b + 1], None, ALU.add)
            s.then_inc(m["idx_ready"], 1)

            def conv_rows_in(i, u):
                dve.wait_ge(m["act_glu"], i * 2 + (glus[0] + u + 1))
                k = bass.ds(i * 2 + u, 1)
                dve.tensor_tensor(full[:, k, HIST:PROMPT_W].rearrange("p a t -> p (a t)"),
                                  PS[2 * u][:, 0:SEQ], tmp[:, u, 0:SEQ], ALU.mult)
                dve.tensor_tensor(fullS[:, k, :, HIST:].rearrange("p a b r -> p (a b) r"),
                                  PS[2 * u][:, SEQ:T].rearrange("p (b r) -> p b r", b=NB),
                                  tmp[:, u, SEQ:].rearrange("p (b r) -> p b r", b=NB), ALU.mult) \
                    .then_inc(m["evac_done"], 1)
            slabs("pw1", None, conv_rows_in)
            glus[0] += KT
            for x in RTs:
                dve.memset(x[:, :, :, 4 * P:4 * P + 2].bitcast(F32), 0.0)
            dve.wait_ge(m["evac_done"], outs_[0] + CREDIT)
            dve.wait_ge(m["hist_out"], 4)
            dve.tensor_copy(vnew.rearrange("p k (b r) -> p k b r", b=NB), fullS[:, :, :, HIST:]) \
                .then_inc(m["vnew_ready"], 1)
            def conv_tiles(k):
                return (csum[:, k, 0:SEQ], lambda tap: full[:, k, bass.ds(tap, SEQ)],
                        csum[:, k, SEQ:].rearrange("p (b r) -> p b r", b=NB),
                        lambda tap: fullS[:, k, :, bass.ds(tap, NQ)])
            for k in range(KT):
                o1, i1, o2, i2 = conv_tiles(k)
                for o, x in ((o1, i1(0)), (o2, i2(0))):
                    dve.tensor_scalar(o, x, wdw[:, k:k + 1], vecs[:, V_BDW + k:V_BDW + k + 1], ALU.mult, ALU.add) \
                        .then_inc(m["conv_step"], 1)
            for i, c in enumerate((1, 0)):
                dve.wait_ge(m["w1_high"], i + 1)
                dve.tensor_tensor(w1s[1][:, c, :, :], w1[:, c, :, :], w1s[0][:, c, :, :], ALU.subtract) \
                    .then_inc(m["w1_low"], 1)

            TAPS_AT_ONCE = 4

            def compression_step(b, t):
                j, c = t // 2, t % 2
                dve.wait_ge(m["rt_high"], b * 16 + (t + 1))
                dve.tensor_tensor(RTs[1][:, j % 2, c, 0:4 * P], PS[5 + c][:, 0:4 * P], RTs[0][:, j % 2, c, 0:4 * P],
                                  ALU.subtract).then_inc(m["rt_ready"], 1)

            def convolution_step(b, t):
                a = t // 4
                for k in range(2 * (t % 4), 2 * (t % 4) + 2):
                    o1, i1, o2, i2 = conv_tiles(k)
                    for h, (o, x) in enumerate(((o1, i1), (o2, i2))):
                        dve.wait_ge(m["conv_step"], b * (16 * TAPS_AT_ONCE) + (16 * a + 2 * k + h + 1))
                        dve.scalar_tensor_tensor(o, x(b * TAPS_AT_ONCE + (a + 1)),
                                                 wdw[:, bass.ds(b * (TAPS_AT_ONCE * KT) + (a * KT + KT + k), 1)], o,
                                                 ALU.mult, ALU.add).then_inc(m["conv_step"], 1)

            with dve.Fori(0, NB - 1) as b:
                for t in range(16):
                    compression_step(b, t)
                    convolution_step(b, t)
            left = (TAPS - 1 - (NB - 1) * TAPS_AT_ONCE) * 4
            for t in range(16):
                compression_step(NB - 1, t)
                if t < left:
                    convolution_step(NB - 1, t)
                if t == left:
                    dve.wait_ge(m["conv_step"], 16 * TAPS)
                    dve.wait_ge(m["conv_turned"], 1)
                    dve.tensor_reduce(stat[:, 0, :], csum[:, :, :].rearrange("p k t -> p t k"), AX_X, ALU.add) \
                        .then_inc(m["ssum_ready"], 1)
            seen.wait(dve, m["mean_ready"])
            did(dve.memset(stat[:, 0, :], 0.0))
            settle()
            for k in range(KT + 1):
                if k < KT:
                    dve.tensor_tensor(csum[:, k, :], csum[:, k, :], PS[3][:, 0:T], ALU.subtract) \
                        .then_inc(m["cen_ready"], 1)
                if k:
                    seen.wait(dve, m["sq_ready"])
                    if k > 1:
                        dve.wait_ge(m["ln_step"], k - 1)
                    dve.tensor_tensor(stat[:, 0, :], stat[:, 0, :], tmp[:, (k - 1) % 4, :], ALU.add) \
                        .then_inc(m["ln_step"], 1)
            low(0, PH["pw2"].base + 1, PH["pw2"].cols)
            root()
            for k in range(KT):
                dve.tensor_tensor(csum[:, k, :], csum[:, k, :], stat[:, 2, :], ALU.mult).then_inc(m["cen_ready"], 1)
                if k == 0:
                    did(dve.memset(stat[:, 0, :], 0.0))
                if k > 1:
                    rows_lo(k - 2, csum[:, k - 2, :])
            rows_lo(KT - 2, csum[:, KT - 2, :])
            rows_lo(KT - 1, csum[:, KT - 1, :])
            low(1, PH["pw2"].base + 2, PH["pw2"].cols)
            dve.wait_ge(m["wg_hi"], 1)
            did(dve.tensor_tensor(wgl[:, :, :], wg[:, :, :], wgh[:, :, :], ALU.subtract))
            settle()
            residual_pair("pw2", "up01")
            root()
            dve.wait_ge(m["conv_stored"], 16 * (NB + 1))
            ffn("01", V_NORM + 16, "kv")
            root()
            norm(V_KV)

            def kv_rows(i, u):
                c = bass.ds(i * 2 + u, 1)
                dve.tensor_copy(rows[:, :, c, :].rearrange("p t a n -> p (t a) n"),
                                PS[2 * u][:, :].rearrange("p (t n) -> p t n", t=2))
                dve.tensor_copy(rowsS[:, c, :].rearrange("p a n -> p (a n)"), PS[2 * u + 1][0:TS, 0:256]) \
                    .then_inc(m["evac_done"], 1)
            slabs("kv", "up10", kv_rows)
            ffn("10", V_NORM + 24, "q")
            root()
            norm(V_NORM + 32)

            def queries(i, u):
                dve.tensor_scalar(qT[:, bass.ds(i * 4 + 2 * u, 2), :], PSA[:, 2 * u:2 * u + 2, 0:T], QSCALE, None,
                                  ALU.mult).then_inc(m["evac_done"], 1)
            slabs("q", None, queries)
            dve.wait_ge(m["evac_done"], outs_[0] + CREDIT)
            dve.wait_ge(m["gate_spread"], 1)
            dve.memset(RTp[:, :, :, 4 * NCP:4 * NCP + 2], 0.0)
            gm = tmp[:, 1, 0:3 * TS].rearrange("p (n q) -> p n q", q=NQ)
            own = cn("own_query").rearrange("p (a q) -> p a q", a=1).broadcast_to([P, 3 * NB, NQ])
            did(dve.tensor_tensor(gm, PS[7][:, 0:3 * TS].rearrange("p (n q) -> p n q", q=NQ), own, ALU.mult))
            settle()
            dve.tensor_reduce(gateS[:, :, :], gm, AX_X, ALU.add).then_inc(m["gate_out"], 1)
            dve.wait_ge(m["kv_out"], 2 * (NB + 1))
            did(dve.memset(qsl[:, :, :], 0.0))
            settle()

            PSTEPS = 20
            pbase = steps[1]

            def queries_of(z, ahead):
                for g in range(2):
                    s = dve.tensor_copy(qsl[g * HD:g * HD + HD, g, :],
                                        qT[g * HD:g * HD + HD, bass.ds(z + ahead, 1), 0:SEQ].rearrange("p a t -> p (a t)"))
                s.then_inc(m["qsl_ready"], 1)

            queries_of(0, 0)
            for q in range(2):
                def biased(z, w):
                    g, t = w // 2, w % 2
                    n = P * (t + 1)
                    slope = cn("neg_slope")[:, bass.ds(z + (2 * q + g) * NZ, 1)]
                    dve.wait_ge(m["p_scores"], z * 4 + (16 * q + w + 1))
                    if w == 3 and not (isinstance(z, int) and q and z == NZ - 1):
                        queries_of(z, q * NZ + 1)
                    full_ = SP_[:, w, 0:512].rearrange("p (r n) -> p r n", r=2)[:, :, 0:n]
                    dve.scalar_tensor_tensor(full_, dist_full[:, t:t + 1, 0:n].broadcast_to([P, 2, n]), slope,
                                             PSA[:, 2 * t:2 * t + 2, 0:n], ALU.mult, ALU.add)
                    did(dve.scalar_tensor_tensor(SP_[:, w, 512:528], dist_cmp[:, t, :], slope,
                                                 PS[2 * t][:, 256:256 + NCP], ALU.mult, ALU.add))
                    settle()
                    dve.tensor_reduce(small[:, w, 1:3], full_, AX_X, ALU.max, negate=True)
                    dve.tensor_reduce(small[:, w, 0:1], SP_[:, w, 512:528], AX_X, ALU.max, negate=True) \
                        .then_inc(m["p_max"], 1)

                def scaled(z, back, w):
                    g, t = w // 2, w % 2
                    n = P * (t + 1)
                    gates = gateP[:, t, :].rearrange("p (r h) -> p r h", r=3)[:, :, bass.ds(z + ((2 * q + g) * NZ - back), 1)] \
                        .rearrange("p r a -> p (r a)")
                    dve.wait_ge(m["p_exp"], z * 4 + (16 * q + w + 1 - 4 * back))
                    did(dve.scalar_tensor_tensor(SP_[:, w, 512:528], SP_[:, w, 512:528], 1.0, live_cmp[:, t, :],
                                                 ALU.mult, ALU.mult, accum_out=small[:, w, 4:5]))
                    settle()
                    did(dve.tensor_scalar(small[:, w, 8:11], small[:, w, 4:7], TINY, None, ALU.max))
                    settle()
                    did(dve.reciprocal(small[:, w, 8:11], small[:, w, 8:11]))
                    settle()
                    did(dve.tensor_tensor(small[:, w, 12:15], small[:, w, 8:11], gates, ALU.mult))
                    settle()
                    for r in range(3):
                        x = SP_[:, w, 512:528] if r == 0 else SP_[:, w, 256 * (r - 1):256 * (r - 1) + n]
                        s = dve.tensor_scalar(x, x, small[:, w, 12 + r:13 + r], None, ALU.mult)
                    s.then_inc(m["p_scaled"], 1)

                def step(z, w, first=False):
                    biased(z, w)
                    if w or not first:
                        scaled(z, w < 1, (w - 1) % 4)

                start = pbase + q * NZ * PSTEPS
                steps[0], steps[1] = 0, start
                for w in range(4):
                    step(0, w, first=True)
                peeled = steps[1] - start
                with dve.Fori(1, NZ - 1) as z:
                    steps[0], steps[1] = z * PSTEPS, start + peeled - PSTEPS
                    for w in range(4):
                        step(z, w)
                    assert steps[1] == start + peeled
                steps[0], steps[1] = 0, start + peeled + (NZ - 2) * PSTEPS
                for w in range(4):
                    step(NZ - 1, w)
                scaled(NZ - 1, 0, 3)
                assert steps[1] == start + NZ * PSTEPS
                for t in range(2):
                    dve.wait_ge(m["p_out"], 16 * (q + 1))
                    dve.tensor_copy(oP[:, t, 512 * q:512 * q + 512], PS[6 + t][:, :]).then_inc(m["o_evac"], 1)
            for c in range(4):
                dve.wait_ge(m["oP_turned"], c + 1)
                dve.tensor_copy(oT[:, 2 * c:2 * c + 2, 0:SEQ], PS[c][:, :].rearrange("p (k t) -> p k t", k=2)) \
                    .then_inc(m["oP_out"], 1)

            steps[0], steps[1] = 0, pbase + 2 * NZ * PSTEPS
            did(dve.memset(qbd[:, :, :], 0.0))
            did(dve.memset(imp[:, 0, :], FORCE))
            settle()
            dve.sem_inc(m["s_biased"], CREDIT)
            dve.sem_inc(m["kt_out1"], 1)
            dve.wait_ge(m["oP_turned"], 4)
            dve.drain().then_inc(m["attn_in"], 1)
            dve.wait_ge(m["selb_loaded"], 16)
            SSTEPS = 13
            sbase = steps[1]

            def batch_scores(b):
                steps[0], steps[1] = b * SSTEPS, sbase
                for q in range(2):
                    for g in range(2):
                        grp = 2 * q + g
                        s = dve.tensor_copy(
                            qbd[g * HD:g * HD + HD, q, grp * 32:grp * 32 + 32].rearrange("p (z r) -> p z r", z=NZ),
                            qT[g * HD:g * HD + HD, q * NZ:q * NZ + NZ, bass.ds(b * NQ + SEQ, NQ)])
                s.then_inc(m["qbd_ready"], 1)
                newb = cn("new_bias")[:, bass.ds(b * -NQ + 56, TS)]
                dve.wait_ge(m["s_scores"], b * 6 + 1)
                dve.tensor_tensor(S[:, S_NEW:S_WIN], PS[2][:, 0:TS], newb, ALU.add)
                dve.tensor_tensor(S[:, S_WNEW:S_CMP], PS[2][:, TS:2 * TS], newb, ALU.add)
                dve.tensor_tensor(S[:, S_CMP:S_COLS], PS[2][:, 2 * TS:2 * TS + P], cn("cmp_bias"), ALU.add) \
                    .then_inc(m["s_biased"], 1)
                dve.wait_ge(m["s_biased"], b * 6 + 1 + CREDIT)
                dve.tensor_reduce(small[:, 0, 0:1], S[:, S_CMP:S_COLS], AX_X, ALU.max, negate=True) \
                    .then_inc(m["c_max"], 1)

                def keys(r):
                    dve.wait_ge(m["kt_turned"], b * 10 + (r + 1))
                    dst = KTb[:, r // 4, (r % 4) * 512:(r % 4) * 512 + 512] if r < 8 else KTw[:, r - 8, :]
                    dve.tensor_copy(dst, PS[r % 2][:, :]).then_inc(m["kt_out1"], 1)

                def normalise(src, col):
                    did(dve.tensor_scalar(small[:, 0, 8 + col:8 + col + src], small[:, 0, 4 + col:4 + col + src], TINY,
                                          None, ALU.max))
                    settle()
                    did(dve.reciprocal(small[:, 0, 8 + col:8 + col + src], small[:, 0, 8 + col:8 + col + src]))
                    settle()

                keys(1)
                dve.wait_ge(m["c_exp"], b + 1)
                normalise(1, 0)
                dve.tensor_scalar(S[:, S_CMP:S_COLS], S[:, S_CMP:S_COLS], small[:, 0, 8:9], None, ALU.mult) \
                    .then_inc(m["c_scaled"], 1)
                for r in range(3, 10, 2):
                    keys(r)
                dve.wait_ge(m["imp_sum"], b + 1)
                dve.wait_ge(m["c_scaled"], b + 1)
                did(dve.tensor_scalar(S[:, S_CMP:S_COLS], S[:, S_CMP:S_COLS], gateS[:, 0, bass.ds(b, 1)], None,
                                      ALU.mult))

                def chunk(c):
                    dve.wait_ge(m["s_scores"], b * 6 + (c + 1))
                    at = 512 * (c - 1)
                    dst, bias = (S[:, at:at + 512], selb[:, at:at + 512]) if c < 5 else \
                        (S[:, S_WIN:S_WNEW], cn("win_bias"))
                    dve.tensor_tensor(dst, PS[2 + c % 2][:, :], bias, ALU.add).then_inc(m["s_biased"], 1)
                chunk(1)
                dve.wait_ge(m["imp_ready"], b + 1)
                did(dve.tensor_copy(imp[:, 0, 1:NSEL - 2], PS[4][:, P + 1:P + NSEL - 2]))
                settle()
                dve.sem_inc(m["passed"], 1)
                did(dve.max(out=top8[:, 0, :], in_=imp[:, 0, :]))
                settle()
                dve.sem_inc(m["passed"], 1)
                did(dve.match_replace(out=imp[:, 1, :], in_to_replace=top8[:, 0, :], in_values=imp[:, 0, :],
                                      imm_value=NEG))
                settle()
                dve.sem_inc(m["passed"], 1)
                did(dve.max(out=top8[:, 1, :], in_=imp[:, 1, :]))
                settle()
                dve.sem_inc(m["passed"], 1)
                did(dve.match_replace(out=imp[:, 2, :], in_to_replace=top8[:, 1, :], in_values=imp[:, 1, :],
                                      imm_value=NEG))
                settle()
                did(dve.tensor_scalar(imp[:, 3, :], imp[:, 2, :], NEG / 2, NEG, ALU.is_gt, ALU.mult))
                for c in range(2, 6):
                    chunk(c)
                dve.wait_ge(m["s_biased"], b * 6 + 6 + CREDIT)
                dve.tensor_reduce(small[:, 0, 2:3], S[:, S_WIN:S_CMP], AX_X, ALU.max, negate=True) \
                    .then_inc(m["s_max"], 1)
                settle()
                sblk = S[:, 0:PAST].rearrange("p (j l) -> p j l", l=SB)
                drop = imp[:, 3, 0:NSEL - 1].rearrange("p (j a) -> p j a", a=1).broadcast_to([P, NSEL - 1, SB])
                did(dve.tensor_tensor(sblk, sblk, drop, ALU.add))
                settle()
                dve.tensor_reduce(small[:, 0, 1:2], S[:, 0:S_WIN], AX_X, ALU.max, negate=True) \
                    .then_inc(m["s_max"], 1)
                dve.wait_ge(m["s_exp"], b * 2 + 2)
                normalise(2, 1)
                did(dve.tensor_tensor(small[:, 0, 12:14], small[:, 0, 9:11], gateS[:, 1:3, bass.ds(b, 1)]
                                      .rearrange("p r a -> p (r a)"), ALU.mult))
                settle()
                dve.tensor_scalar(S[:, S_WIN:S_CMP], S[:, S_WIN:S_CMP], small[:, 0, 13:14], None, ALU.mult)
                dve.tensor_scalar(S[:, 0:S_WIN], S[:, 0:S_WIN], small[:, 0, 12:13], None, ALU.mult) \
                    .then_inc(m["s_scaled"], 1)
                assert steps[1] - sbase == SSTEPS

            def batch_out(b):
                dve.wait_ge(m["o_turned"], b + 1)
                ob = PS[4][:, 256:512]
                for q in range(2):
                    for g in range(2):
                        grp = 2 * q + g
                        s = dve.tensor_copy(
                            oT[g * HD:g * HD + HD, q * NZ:q * NZ + NZ, bass.ds(b * NQ + SEQ, NQ)],
                            ob[g * HD:g * HD + HD, q * P + grp * 32:q * P + grp * 32 + 32].rearrange("p (z r) -> p z r", z=NZ))
                        if q:
                            s.then_inc(m["o_out"], 1)
            batch_scores(0)
            with dve.Fori(0, NB - 1) as b:
                batch_scores(b + 1)
                batch_out(b)
            low(0, PH["o"].base + 1, PH["o"].cols)
            batch_out(NB - 1)
            steps[0], steps[1] = 0, sbase + NB * SSTEPS
            for k in range(KT):
                rows_lo(k, oT[:, k, :])
            did(dve.memset(stat[:, 0, :], 0.0))
            settle()
            low(1, PH["o"].base + 2, PH["o"].cols)
            residual_pair("o", "up11")
            root()
            ffn("11", V_NORM + 40, None)
            root()
            for k in range(KT):
                s = dve.scalar_tensor_tensor(oT[:, k, :], xT[:, k, :], vecs[:, V_FINAL + k:V_FINAL + k + 1],
                                             stat[:, 2, :], ALU.mult, ALU.mult)
            s.then_inc(m["h_ready"], 1)
            for g in range(6):
                t, h = g // 2, g % 2
                at, n = TOK_TILES[t]
                dve.wait_ge(m["y_turned"], g + 1)
                dve.tensor_copy(yout[0:n, t, h * 512:h * 512 + 512], PS[g][0:n, :]).then_inc(m["y_out"], 1)


        with nc.Block() as block:
            @block.sync
            def _(sp):
                sp_program(sp)

            @block.gpsimd
            def _(pool):
                pool_program(pool)

            @block.scalar
            def _(act):
                act_program(act)

            @block.vector
            def _(dve):
                dve_program(dve)

            @block.tensor
            def _(pe):
                pe_program(pe)


_OUTS = [((1, SEQ, D), "y_prompt"), ((NB, NQ, D), "y_sample"), ((1, SEQ, 4, NKV, HD), "kv_prompt"),
         ((NB, NQ, 4, NKV, HD), "kv_sample"), ((1, SEQ, 2, NKV, HD), "win_prompt"),
         ((NB, WIN, 2, NKV, HD), "win_sample"), ((1, 1, HIST, D), "conv_prompt"), ((1, NB, HIST, D), "conv_sample")]


def kernel(**inputs):
    import concourse.bacc as bacc
    from concourse.bass_utils import run_bass_kernel_spmd

    nc = bacc.Bacc("TRN2", target_bir_lowering=False, num_devices=1)
    table, where = host_constants()
    arrays, ins = {}, {}
    for name, a in {**inputs, "const": table}.items():
        a = np.ascontiguousarray(a)
        arrays[f"in_{name}"] = a
        ins[name] = nc.dram_tensor(f"in_{name}", a.shape, mybir.dt.from_np(a.dtype), kind="ExternalInput").ap()
    outs = [nc.dram_tensor(f"out_{name}", list(shape), F32, kind="ExternalOutput").ap() for shape, name in _OUTS]
    program(nc, ins, outs, where)
    r = run_bass_kernel_spmd(nc, [arrays], core_ids=[0])
    return tuple(r.results[0][f"out_{name}"] for _, name in _OUTS)
```

```python
from contextlib import ExitStack

import numpy as np

import concourse.bass as bass
from concourse import mybir
from concourse.alu_op_type import AluOpType as ALU

ACT = mybir.ActivationFunctionType
F32 = mybir.dt.float32
F32R = mybir.dt.float32r
I32 = mybir.dt.int32
AX_X = mybir.AxisListType.X

P = 128
D = 1024
KT = D // P
SEQ = 256
NB = 8
NQ = 8
TS = NB * NQ
T = SEQ + TS
FF = 2816
FT = FF // P
TAPS = 31
HIST = TAPS - 1
NKV = 4
NZ = 4
NH = NKV * NZ
HD = 64
PAGE = 128
NPAGE = 16
PAST = NPAGE * PAGE
NPOOL = 160
CS = 16
NCP = SEQ // CS
SB = 64
NSEL = 33
WIN = 512
WR = WIN // P
EPS = 1e-6
NEG = -1e30
FORCE = 1e9
FAR = 1e33
TINY = 1e-30
QSCALE = HD ** -0.5

PROMPT_W = HIST + SEQ
SAMPLE_W = HIST + NQ
FULL_W = PROMPT_W + NB * SAMPLE_W
TOK_TILES = ((0, P), (P, P), (SEQ, TS))

V_NORM, V_KV, V_FINAL, V_BDW, V_LNG, V_LNB = 0, 48, 56, 64, 72, 80
V_B1, V_B2, V_PE, V_ROWS = 88, 90, 91, 123

S_SEL, S_NEW, S_WIN, S_WNEW, S_CMP = 0, PAST, PAST + TS, PAST + TS + WIN, PAST + 2 * TS + WIN
S_COLS = S_CMP + P
CREDIT = 2


def host_constants():
    f = np.float32
    p = np.arange(P)
    slope = np.exp2(f(-8.0) * (np.arange(NH, dtype=f) + f(1)) / f(NH)).astype(f)
    g, z, q = p // 32, p // 8 % 4, p % 8
    sl = slope[g * NZ + z][:, None]
    qpos = (PAST + q)[:, None]
    n = np.arange(P)[None]
    cmp_bias = -(sl * (qpos - (n * CS + 31)).astype(f))
    cmp_bias[:, P - 1] = NEG
    sel_bias = -(sl * (qpos - np.arange(PAST)[None]).astype(f))
    r, pp = np.divmod(np.arange(WIN), P)
    dist = qpos - (PAST - WIN + pp * WR + r)[None]
    win_bias = np.where(dist < WIN, -(sl * dist.astype(f)), f(NEG))
    k = np.arange(120)[None] - 56
    dist = q[:, None] - k
    new_bias = np.where((k >= 0) & (k < NQ) & (dist >= 0), -(sl * dist.astype(f)), f(NEG))
    cs, ss = np.arange(P)[:, None] * CS, np.arange(NSEL)[None] * SB
    overlap = np.clip(np.minimum(cs + 32, ss + SB) - np.maximum(cs, ss), 0, 32).astype(f) / f(32)
    overlap[P - 1] = 0
    t = np.arange(SEQ).reshape(2, P)
    dist = t[:, :, None] - np.arange(SEQ)
    dist_full = np.where(dist >= 0, dist, FAR).transpose(1, 0, 2)
    dist = t[:, :, None] - (np.arange(NCP) * CS + 31)
    live = (dist >= 0) & (np.arange(NCP) < NCP - 1)
    dist_cmp = np.where(live, dist, FAR).transpose(1, 0, 2)
    live_cmp = live.transpose(1, 0, 2)
    parts = [
        ("ident", np.eye(P)), ("mean", np.full((P, P), 1 / D)),
        ("zsum", (g[:, None] == g[None]) & (q[:, None] == q[None])),
        ("overlap", overlap),
        ("head_rows", np.arange(P)[:, None] == (p // 8)[None]),
        ("own_query", q[:, None] == np.arange(NQ)[None]),
        ("token_row", (p % 8)[:, None] * 32 + np.arange(CS)[None] * 2),
        ("neg_slope", np.broadcast_to(-slope, (P, NH))),
        ("cmp_bias", cmp_bias), ("new_bias", new_bias), ("win_bias", win_bias),
        ("dist_full", dist_full.reshape(P, -1)), ("dist_cmp", dist_cmp.reshape(P, -1)),
        ("live_cmp", live_cmp.reshape(P, -1)), ("sel_bias", sel_bias),
    ]
    where, at = {}, 0
    for name, a in parts:
        where[name] = (at, a.shape[1])
        at += a.shape[1]
    return np.concatenate([a.astype(f) for _, a in parts], axis=1), where


class Phase:

    def __init__(self, n, dmas, cols, before):
        self.n, self.dmas, self.cols = n, dmas, cols
        self.base = before.end if before else 0
        self.loaded0 = before.loaded0 + 16 * before.dmas * before.n // 2 if before else 0
        self.end = self.base + n

    def upto(self, i, u, ahead=0):
        return i * 2 + (self.base + 2 * ahead + u + 1)

    def loaded(self, i, ahead=0):
        return i * (16 * self.dmas) + (self.loaded0 + 16 * self.dmas * (ahead + 1))


def slab_phases():
    up, down = (FT, 2, 2 * D), (2 * KT, 1, FT // 2 * P)
    wide = 2 * D
    order = [("up00", up), ("down00", down), ("pw1", (KT, 2, wide)), ("pw2", (4, 1, wide)), ("up01", up),
             ("down01", down), ("kv", (6, 1, wide)), ("up10", up), ("down10", down), ("q", (4, 4, wide)),
             ("o", (4, 4, wide)), ("up11", up), ("down11", down)]
    phases, last = {}, None
    for name, shape in order:
        last = phases[name] = Phase(*shape, last)
    return phases


class Seen:

    def __init__(self):
        self.n = {}

    def __getitem__(self, sem):
        return self.n.get(sem.name, 0)

    def add(self, sem, k=1):
        self.n[sem.name] = self[sem] + k
        return self[sem]

    def wait(self, eng, sem, k=1):
        eng.wait_ge(sem, self.add(sem, k))


def program(nc, ins, outs, where):
    with ExitStack() as ctx:
        def sb(name, *shape, dt=F32):
            return ctx.enter_context(nc.sbuf_tensor(name, list(shape), dt))

        def both(name, n):
            with nc.sbuf_tensor(name + "_f32", [P, n], F32) as f:
                pass
            return f, sb(name + "_f32r", P, n, dt=F32R)

        def sem(name):
            return ctx.enter_context(nc.semaphore(name))

        const = sb("const", P, where["sel_bias"][0])
        xT = sb("xT", P, KT, T)
        W = sb("W", P, 2, 2 * D)
        SF, SR = both("S", 8 * D)
        HF, HR = both("H", 2 * KT * T)
        GF, GR = both("G", 14968)
        kcT = sb("kcT", P, NB, 2, P)
        vc = sb("vc", P, NB, 256)
        kcTp = sb("kcTp", P, 2, NCP)
        vcp = sb("vcp", NCP, 256)
        rows = sb("rows", P, 2, 6, 256)
        rowsS = sb("rowsS", TS, 6, 256)
        kT = sb("kT", P, 2, 2, T)
        w2 = sb("w2", P, 2, HD)
        b2v = sb("b2v", 1, 256)
        ones = sb("ones", 1, P)
        wg = sb("wg", P, KT, 48)
        wgh, wgl = sb("wgh", P, KT, 48, dt=F32R), sb("wgl", P, KT, 48, dt=F32R)
        vecs = sb("vecs", P, V_ROWS)
        wdw = sb("wdw", P, TAPS * KT)
        cst, cst_part = sb("cst", P, 2), sb("cst_part", P, 2)
        eps = sb("eps", P, 1)
        warm = sb("warm", P, 32)
        stat = sb("stat", P, 3, T)
        tmp = sb("tmp", P, 4, T)
        ptab = sb("ptab", P, NB, dt=I32)
        ptabf = sb("ptabf", P, NB)
        ptrow = sb("ptrow", 1, P, dt=I32)
        cidx = sb("cidx", P, NB * CS, dt=I32)
        cslot = sb("cslot", P, CS, dt=I32)
        gateP = sb("gateP", P, 2, 48)
        rtok = sb("rtok", P, 2, 3)
        gateS = sb("gateS", P, 3, NB)
        gsig = sb("gsig", NH, 3 * TS)
        small = sb("small", P, 4, 16)
        imp = sb("imp", P, 4, NSEL)
        top8 = sb("top8", P, 2, 8)
        PSA = ctx.enter_context(nc.psum_tensor("PSA", [P, 8, 512], F32))
        PS = [PSA[:, i, :] for i in range(8)]

        def cn(name, n=P):
            a, w = where[name]
            return const[0:n, a:a + w]

        ident, meanm = cn("ident"), cn("mean")
        dist_full = cn("dist_full").rearrange("p (q k) -> p q k", q=2)
        dist_cmp = cn("dist_cmp").rearrange("p (q k) -> p q k", q=2)
        live_cmp = cn("live_cmp").rearrange("p (q k) -> p q k", q=2)
        def area(a, at, *shape):
            n = int(np.prod(shape))
            names = "abcd"[:len(shape)]
            return a[:, at:at + n].rearrange(f"p ({' '.join(names)}) -> p {' '.join(names)}",
                                             **dict(zip(names, shape))) if len(shape) > 1 else a[:, at:at + n]

        def slab_views(*shape):
            n = int(np.prod(shape))
            names = "abc"[:len(shape)]
            pat = f"p ({' '.join(names)}) -> p {' '.join(names)}"
            kw = dict(zip(names, shape))
            return [[a[:, 0:n].rearrange(pat, **kw) for a in (W[:, u, :], SR[:, u * 2 * D:u * 2 * D + 2 * D],
                                                              SR[:, (u + 2) * 2 * D:(u + 3) * 2 * D])] for u in range(2)]
        flat_slab = [[W[:, u, :], SR[:, u * 2 * D:u * 2 * D + 2 * D], SR[:, (u + 2) * 2 * D:(u + 3) * 2 * D]]
                     for u in range(2)]
        Wgu = slab_views(KT, 2, P)
        Wdn = slab_views(FT // 2, P)
        W256 = slab_views(KT, 256)
        RAW, HI, LO = range(3)
        hR = [area(HR, p * KT * T, KT, T) for p in range(2)]
        gR = [area(GR, p * FT * T, FT, T) for p in range(2)]
        oT = area(HF, KT * T, KT, T)
        csum = oT
        xin = area(GF, 0, 3, D)
        full = area(GF, 0, KT, FULL_W)
        fullS = full[:, :, PROMPT_W:].rearrange("p k (b r) -> p k b r", b=NB)
        rowsf = rows[:, :, :, :].rearrange("p t c d -> p (t c d)")
        convS = rowsf[0:TS, 0:D]
        convP = rowsf[0:HIST, D:2 * D]
        hist = rowsf[0:120, 0:2 * D].rearrange("p (h d) -> p h d", h=2)
        vr = rowsf[:, 2 * D:2 * D + 3 * P]
        STG = [area(GF, 4720 + u * 4096, 8, 512) for u in range(2)]
        w1 = W[:, :, :].rearrange("p c (j h) -> p c j h", h=P)
        w1s = [area(SR, part * 4096, 2, 16, P) for part in range(2)]
        RTs = area(HR, 0, 2, 2, 514), area(GR, 12912, 2, 2, 514)
        RTp = area(HF, 0, 2, 2, 66)
        hgel = area(W[:, 1, :], 0, 2, 512)
        RL = area(W[:, 1, :], 1024, 2, 512)
        vnew = stat[:, :, :].rearrange("p a t -> p (a t)")[:, 0:KT * TS].rearrange("p (k t) -> p k t", k=KT)
        pages = [area(GF, u * 4096, NPAGE, 256) for u in range(2)]
        kpg, vpg = pages
        STGp = [area(GF, u * 4096, 8, 512) for u in range(2)]
        qT = area(GF, 8192, KT, T)
        w1p = area(GF, 8192 + KT * T, 2, 16, P)
        PT = area(GF, 8192 + KT * T, 23 * P)
        qbd = area(GF, 8192 + KT * T + 23 * P, 2, P)
        selb = area(HF, 0, PAST)
        KTb = area(SF, 0, 2, PAST)
        S = area(SF, 4096, S_COLS)
        KTw = area(SF, 4096 + S_COLS, 2, WIN)
        osb = tmp[:, 0, 0:256]
        ips = tmp[:, 1, 0:P]
        wst = [W[:, u, :].rearrange("p (r c) -> p r c", r=WR) for u in range(2)]
        oP = area(SF, 0, 2, 1024)
        SP_ = area(SF, 4104, 4, 528)
        PTp = area(SF, 4104 + 4 * 528, 2, 5, P)
        qsl = area(SF, 4104 + 4 * 528 + 1280, 2, 256)
        yout = area(SF, 0, 3, D)
        PH = slab_phases()

        names = """hi_ready lo_ready x_step gate_step h_raw h_hi w1_loaded w1p_loaded w1_high w1_low rt_high wg_hi
            cst_ready passed kv_stored conv_stored consts_loaded vecs_loaded x_loaded misc_loaded hist_loaded
            slab_used evac_done act_glu turned turned_out sq_ready ssum_ready mean_ready std_ready h_ready
            conv_step ln_step hist_out cen_ready idx_ready slot_ready rt_turned rt_ready rl_ready vnew_ready
            z_ready gelu_ready kv_ready kv_out conv_turned conv_rows stored kT_turned kT_out prow_loaded
            gate_logits gate_scaled scaled gate_sig gate_spread gate_out dve_step qsl_ready p_scores p_max p_exp
            p_weights p_scaled p_turned p_PT p_out o_evac oP_turned oP_out attn_in kt_turned kt_out0 kt_out1
            s_scores s_biased c_max c_exp c_scaled imp_sum imp_sumout imp_ready s_max s_exp s_scaled pt_turned
            pt_out o_ready o_copied o_turned o_out qbd_ready selb_loaded ptrow_loaded y_turned y_out pool_step""".split()
        m = {n: sem(n) for n in names}
        slab_loaded = [sem("slab_loaded0"), sem("slab_loaded1")]
        gathered = [sem("gathered0"), sem("gathered1")]
        half_used = [sem("half_used0"), sem("half_used1")]
        K_loaded, V_loaded, K_used, V_used = map(sem, ("K_loaded", "V_loaded", "K_used", "V_used"))
        V_last_loaded = sem("V_last_loaded")
        win_loaded = [sem("win_loaded0"), sem("win_loaded1")]
        win_used = [sem("win_used0"), sem("win_used1")]

        SQ = 2 * KT
        OUTS_DOWN00 = FT + KT
        OUTS_KV = 2 * (FT + KT) + KT + 4 + 6
        OUTS_DOWN10 = OUTS_KV + FT + KT

        cache = ins["cache_kv"]

        def load_pages(eng, b, c, page, used, count, loaded):
            eng.wait_ge(used, count)
            eng.sem_inc(m["passed"], 1)
            for k in range(NPAGE):
                n = eng.value_load(ptrow[0:1, bass.ds(b * NPAGE + k, 1)], min_val=0, max_val=NPOOL - 1)
                src = cache[bass.ds(n, 1), :, c, :, :].rearrange("a t g d -> t (a g d)")
                eng.dma_start(page[:, k, :], src).then_inc(loaded, 16)

        def sp_program(sp):
            def slabs(name, load, first=None):
                ph = PH[name]
                if first:
                    for u in range(2):
                        for sem_, n in first[u]:
                            sp.wait_ge(sem_, n)
                        load(0, u)
                with sp.Fori(1 if first else 0, ph.n // 2) as i:
                    for u in range(2):
                        sp.wait_ge(m["lo_ready"], ph.upto(i, u))
                        load(i, u)

            def ffn_up(layer, j):
                wi = ins["w_ff_in"][layer, j].rearrange("(k p) (h n) -> p k h n", p=P, h=2)

                def up(i, u):
                    for h in range(2):
                        sp.dma_start(Wgu[u][RAW][:, :, h, :], wi[:, :, h, bass.ds(i * 256 + u * P, P)]) \
                          .then_inc(slab_loaded[u], 16)

                slabs(f"up{layer}{j}", up)

            def ffn_down(layer, j):
                wo = ins["w_ff_out"][layer, j].rearrange("(k p) n -> p k n", p=P)

                def down(i, u):
                    sp.dma_start(Wdn[u][RAW], wo[:, u * (FT // 2):(u + 1) * (FT // 2), bass.ds(i * P, P)]) \
                      .then_inc(slab_loaded[u], 16)
                slabs(f"down{layer}{j}", down)

            def ffn(layer, j):
                ffn_up(layer, j)
                ffn_down(layer, j)

            first, rest = slice(0, 2 * P), slice(2 * P, const.shape[1])
            sp.dma_start(const[:, first], ins["const"][:, first]).then_inc(m["consts_loaded"], 16)
            sp.dma_start(xin[:, 0:2, :], ins["x_prompt"][0].rearrange("(t p) d -> p t d", p=P)) \
              .then_inc(m["x_loaded"], 16)
            sp.dma_start(xin[0:TS, 2, :], ins["x_sample"].rearrange("b t d -> (b t) d")).then_inc(m["x_loaded"], 16)

            def vload(row, n, src):
                sp.dma_start(vr[row:row + n, 0:P], src).then_inc(m["vecs_loaded"], 16)
            vload(V_NORM, 48, ins["norm_g"].rearrange("l j (k p) -> (l j k) p", p=P))
            vload(V_KV, 8, ins["g_kv"].rearrange("(k p) -> k p", p=P))
            vload(V_FINAL, 8, ins["g_final"].rearrange("(k p) -> k p", p=P))
            for r, name in ((V_BDW, "b_dw"), (V_LNG, "ln_g"), (V_LNB, "ln_b")):
                vload(r, 8, ins[name][0].rearrange("(k p) -> k p", p=P))
            vload(V_B1, 2, ins["b_cmp1"])
            for h in range(2):
                sp.dma_start(vr[V_B2:V_B2 + 1, h * HD:h * HD + HD], ins["b_cmp2"][0:1, :]).then_inc(m["vecs_loaded"], 16)
            vload(V_PE, 32, ins["pe_cmp"].rearrange("c (j s) d -> (c j) (s d)", s=2))
            wd = ins["w_dw"][0].rearrange("w (k p) -> (w k) p", p=P)
            for h in range(2):
                sp.dma_start(vr[0:124, P * (h + 1):P * (h + 2)], wd[124 * h:124 * h + 124]) \
                  .then_inc(m["vecs_loaded"], 16)
            ffn_up(0, 0)
            sp.dma_start(const[:, rest], ins["const"][:, rest]).then_inc(m["consts_loaded"], 16)
            pt = ins["page_table"]
            with nc.allow_non_contiguous_dma(reason="a table of 128 numbers"):
                for r in range(PAGE // CS):
                    sp.dma_start(ptab[r:P:PAGE // CS, :], pt.rearrange("b k -> k b")).then_inc(m["ptrow_loaded"], 16)
            sp.dma_start(ptrow[:, :], pt.rearrange("(a b) k -> a (b k)", a=1)).then_inc(m["ptrow_loaded"], 16)
            for h in range(2):
                sp.dma_start(hist[:, h, :], ins["state_conv"][0].rearrange("(h b) r d -> h (b r) d", h=2)[h]) \
                  .then_inc(m["hist_loaded"], 16)
            for c in range(2):
                sp.dma_start(w2[:, c, :], ins["w_cmp2"][c]).then_inc(m["misc_loaded"], 16)
            for g in range(NKV):
                sp.dma_start(b2v[0:1, g * HD:g * HD + HD], ins["b_cmp2"][1:2, :]).then_inc(m["misc_loaded"], 16)
            sp.dma_start(wg[:, :, :], ins["w_qg"][0][:, D:].rearrange("(k p) n -> p k n", p=P)) \
              .then_inc(m["misc_loaded"], 16)
            ffn_down(0, 0)
            wp = ins["w_pw1"][0].rearrange("(k p) (h n) -> p k h n", p=P, h=2)

            def pw1(i, u):
                for h in range(2):
                    sp.dma_start(Wgu[u][RAW][:, :, h, :], wp[:, :, h, bass.ds(i * 256 + u * P, P)]) \
                      .then_inc(slab_loaded[u], 16)
            slabs("pw1", pw1)
            sp.wait_ge(m["lo_ready"], PH["pw1"].end + CREDIT)
            for c in range(2):
                sp.dma_start(w1[:, c, :, :], ins["w_cmp1"][c].rearrange("(j s) d h -> (s d) j h", s=2)) \
                  .then_inc(m["w1_loaded"], 16)

            def wide(src):
                def load(i, u):
                    sp.dma_start(W256[u][RAW], src[:, :, bass.ds(i * 512 + u * 256, 256)]).then_inc(slab_loaded[u], 16)
                return load
            slabs("pw2", wide(ins["w_pw2"][0].rearrange("(k p) n -> p k n", p=P)),
                  first=[[(m["w1_low"], 2), (m["cst_ready"], 2)], [(m["kv_out"], 2 * NB)]])
            ffn(0, 1)
            slabs("kv", wide(ins["w_kv"].rearrange("(k p) n -> p k n", p=P)))
            ffn(1, 0)
            wq = ins["w_qg"][0].rearrange("(k p) n -> p k n", p=P)

            def queries(i, u):
                for h in range(2):
                    for g in range(2):
                        sp.dma_start(W256[u][RAW][:, :, h * P + g * HD:h * P + g * HD + HD],
                                     wq[:, :, bass.ds(i * 512 + (g * 256 + (2 * u + h) * HD), HD)]) \
                          .then_inc(slab_loaded[u], 16)
            slabs("q", queries)
            sp.wait_ge(m["kv_stored"], 16)
            sp.wait_ge(m["evac_done"], OUTS_DOWN10 + CREDIT)
            for u in range(2):
                src = outs[2][0].rearrange("(n s) c g d -> n s (c g d)", s=CS)[:, 8 * u:8 * u + 8, 0:512]
                sp.dma_start(STGp[u][0:NCP], src).then_inc(m["prow_loaded"], 16)
                sp.dma_start(w1p[:, u, :, :], ins["w_cmp1"][u].rearrange("(j s) d h -> (s d) j h", s=2)) \
                  .then_inc(m["w1p_loaded"], 16)
            sp.wait_ge(m["lo_ready"], PH["q"].end + CREDIT)
            sp.wait_ge(m["kv_out"], 2 * (NB + 1))
            sp.wait_ge(m["gate_logits"], 2)
            sp.dma_start(selb, ins["const"][:, const.shape[1]:]).then_inc(m["selb_loaded"], 16)
            sp.wait_ge(m["ptrow_loaded"], 16 * 9)

            def load_keys(i, off):
                b, u = i * 2 + off, off % 2
                load_pages(sp, b, 2, kpg, K_used, b + 1, K_loaded)
                sp.wait_ge(win_used[u], i + (off // 2 + 1))
                sp.sem_inc(m["passed"], 1)
                sp.dma_start(W[:, u, :], ins["state_kv_win"].rearrange("b (p r) c g d -> b p (r c g d)", r=WR)
                             [bass.ds(b, 1)].rearrange("a p c -> p (a c)")).then_inc(win_loaded[u], 16)

            load_keys(0, 0)
            with sp.Fori(0, NB // 2 - 1) as i:
                for u in range(2):
                    load_keys(i, u + 1)
            load_keys(NB // 2 - 1, 1)
            load_pages(sp, NB - 1, 3, kpg, K_used, NB + 1, V_last_loaded)
            wo = ins["w_o"][0].rearrange("(q g z d) n -> q g d z n", q=2, g=2, z=NZ)

            def out_proj(i, u):
                for q in range(2):
                    for g in range(2):
                        sp.dma_start(W256[u][RAW][g * HD:g * HD + HD, q * NZ:q * NZ + NZ, :],
                                     wo[q, g, :, :, bass.ds(i * 512 + u * 256, 256)]).then_inc(slab_loaded[u], 16)
            slabs("o", out_proj, first=[[(win_used[u], 1 + NB // 2)] for u in range(2)])
            ffn(1, 1)

        CREDIT_H = 1

        def pool_program(pool):
            pool.memset(eps[:, :], EPS).then_inc(m["pool_step"], 1)
            pool.memset(ones[:, :], 1.0).then_inc(m["pool_step"], 1)
            pool.memset(HF[:, 0:1], 0.0).then_inc(m["pool_step"], 1)
            pool.wait_ge(m["idx_ready"], 1)
            pool.wait_ge(m["evac_done"], OUTS_DOWN00 + CREDIT)
            pairs = cache.rearrange("n t (h c) g d -> (n t h) (c g d)", h=2)
            with pool.Fori(0, NB) as b:
                for u in range(2):
                    pool.wait_ge(half_used[u], b + 1)
                    pool.tensor_copy(cslot[:, 8 * u:8 * u + 8], cidx[:, bass.ds(b * CS + 8 * u, 8)]) \
                        .then_inc(m["slot_ready"], 1)
                    pool.wait_ge(m["slot_ready"], b * 2 + (u + 1))
                    pool.sem_inc(m["passed"], 1)
                    for s in range(8):
                        pool.indirect_dma_start(
                            out=STG[u][:, s, :], out_offset=None, in_=pairs,
                            in_offset=bass.IndirectOffsetOnAxis(ap=cslot[:, 8 * u + s:8 * u + s + 1], axis=0)) \
                            .then_inc(gathered[u], 16)
            pool.dma_start(outs[5].rearrange("b t c g d -> b (t c g d)")[:, 0:(WIN - NQ) * 512],
                           ins["state_kv_win"].rearrange("b t c g d -> b (t c g d)")[:, NQ * 512:]) \
                .then_inc(m["stored"], 16)
            pool.dma_start(outs[7][0, :, 0:HIST - NQ, :], ins["state_conv"][0, :, NQ:, :]).then_inc(m["stored"], 16)
            pool.wait_ge(m["conv_rows"], 4)
            pool.dma_start(outs[6][0, 0], convP).then_inc(m["conv_stored"], 16)
            for b in range(NB):
                pool.dma_start(outs[7][0, b, HIST - NQ:, :], convS[b * NQ:b * NQ + NQ, :]) \
                    .then_inc(m["conv_stored"], 16)
            pool.wait_ge(m["evac_done"], OUTS_KV + CREDIT)
            flat = [outs[2][0].rearrange("(t p) c g d -> p t (c g d)", p=P),
                    outs[4][0].rearrange("(t p) c g d -> p t (c g d)", p=P)]
            for o, (c, n), done in zip(flat, ((0, 4), (4, 2)), (m["kv_stored"], m["stored"])):
                pool.dma_start(o, rows[:, :, c:c + n, :].rearrange("p t c d -> p t (c d)")).then_inc(done, 16)
            pool.dma_start(outs[3].rearrange("b t c g d -> (b t) (c g d)"),
                           rowsS[:, 0:4, :].rearrange("p c d -> p (c d)")).then_inc(m["stored"], 16)
            for b in range(NB):
                pool.dma_start(outs[5].rearrange("b t c g d -> b t (c g d)")[b, WIN - NQ:, :],
                               rowsS[b * NQ:b * NQ + NQ, 4:6, :].rearrange("p c d -> p (c d)")) \
                    .then_inc(m["stored"], 16)
            pool.wait_ge(m["ptrow_loaded"], 16 * 9)
            pool.wait_ge(m["kv_out"], 2 * (NB + 1))
            with pool.Fori(0, NB - 1) as b:
                load_pages(pool, b, 3, vpg, V_used, b + 1, V_loaded)
            pool.wait_ge(m["y_out"], 6)
            pool.dma_start(outs[0][0].rearrange("(t p) d -> p t d", p=P), yout[:, 0:2, :]).then_inc(m["stored"], 16)
            pool.dma_start(outs[1].rearrange("b t d -> (b t) d"), yout[0:TS, 2, :]).then_inc(m["stored"], 16)
            pool.wait_ge(m["kv_stored"], 16)
            pool.wait_ge(m["conv_stored"], 16 * (NB + 1))
            pool.wait_ge(m["stored"], 16 * (2 + 2 + NB + 2))

        def pe_program(pe):
            seen = Seen()
            outs_ = [0]
            for s, n in ((m["slab_used"], CREDIT), (K_used, 1), (V_used, 1), (win_used[0], 1), (win_used[1], 1)):
                pe.sem_inc(s, n)

            def product(out, w, x, start, stop):
                pe.matmul(out, w[0], x[0], start=start, stop=False)
                pe.matmul(out, w[0], x[1], start=False, stop=False)
                return pe.matmul(out, w[1], x[0], start=False, stop=stop)

            def slabs(name, work, first=None):
                ph, o = PH[name], outs_[0]

                def pair_of_slabs(i, first=None):
                    for u in range(2):
                        pe.wait_ge(m["lo_ready"], ph.upto(i, u) + CREDIT)
                        pe.wait_ge(m["evac_done"], i * 2 + (o + u + 1))
                        work(i, u, first if u == 0 else None).then_inc(m["slab_used"], 1)
                pair_of_slabs(0, first)
                with pe.Fori(1, ph.n // 2) as i:
                    pair_of_slabs(i)
                outs_[0] += ph.n

            def gated(i, u, first):
                for k in range(KT):
                    if first:
                        first(k)
                    for h in range(2):
                        mm = product(PS[2 * u + h][:, 0:T], [Wgu[u][p][:, k, h, :] for p in (HI, LO)],
                                     [x[:, k, :] for x in hR], k == 0, k == KT - 1)
                return mm

            def pair(i, u, first):
                for k in range(KT):
                    if first:
                        first(k)
                    for h in range(2):
                        mm = product(PS[2 * u + h][:, 0:T], [W256[u][p][:, k, h * P:h * P + P] for p in (HI, LO)],
                                     [x[:, k, :] for x in hR], k == 0, k == KT - 1)
                return mm

            def down(name):
                ph, o = PH[name], outs_[0]

                def tile(i, u, gate_rows=None):
                    pe.wait_ge(m["evac_done"], i * 2 + (o + u + 1))
                    for h in range(2):
                        pe.wait_ge(m["lo_ready"], i * 4 + (ph.base + 2 * u + h + 1 + CREDIT))
                        if gate_rows and h:
                            pe.wait_ge(m["evac_done"], gate_rows)
                        for k in range(FT // 2):
                            kk = h * (FT // 2) + k
                            mm = product(PS[2 * u][:, 0:T], [Wdn[h][p][:, k, :] for p in (HI, LO)],
                                         [x[:, kk, :] for x in gR], kk == 0, kk == FT - 1)
                        mm.then_inc(m["slab_used"], 1)
                tile(0, 0, outs_[0] + CREDIT)
                tile(0, 1)
                with pe.Fori(1, KT // 2) as i:
                    for u in range(2):
                        tile(i, u)
                outs_[0] += KT

            def kv(i, u, first):
                for t, (at, n) in enumerate(TOK_TILES):
                    out = PS[2 * u][:, t * 256:t * 256 + 256] if t < 2 else PS[2 * u + 1][0:n, 0:256]
                    for k in range(KT):
                        if first and t == 0:
                            first(k)
                        mm = product(out, [x[:, k, at:at + n] for x in hR], [W256[u][p][:, k, :] for p in (HI, LO)],
                                     k == 0, k == KT - 1)
                return mm

            def channel_mean(ready, bank=4, tokens=False):
                seen.wait(pe, *ready)
                if tokens:
                    for t, (at, n) in enumerate(TOK_TILES):
                        pe.matmul(PS[bank][0:n, 384 + t:385 + t], stat[:, 0, at:at + n], meanm[:, 0:1],
                                  start=True, stop=True)
                pe.matmul(PS[bank][:, 0:T], meanm, stat[:, 0, :], start=True, stop=True).then_inc(m["mean_ready"], 1)

            def row_mean(tokens=False):
                channel_mean((m["x_step"], SQ), tokens=tokens)

            def rows_in(mean=None, at=KT // 2):
                n = seen.add(m["h_ready"], KT) - KT

                def wait(k):
                    if mean and k == at:
                        mean()
                    pe.wait_ge(m["h_ready"], n + k + 1)
                return wait

            def ffn(name, mean=True):
                slabs("up" + name, gated, first=rows_in(row_mean if mean else None))
                down("down" + name)

            class Compression:

                def __init__(self, n, layer):
                    self.n, self.layer = n, layer

                def turn(self, b, t):
                    n, c = self.n, t % 2
                    pe.wait_ge(m["rt_ready"], b * 16 + (t + 1))
                    pe.wait_ge(m["rl_ready"], b * 16 + (t + 1))
                    for g in range(NKV):
                        tr = pe.transpose(PS[5 + c][:, g * n:g * n + n], RL[0:n, c, g * P:g * P + P], ident[0:n, 0:n])
                    tr.then_inc(m["rt_turned"], 1)

                def first_layer(self, b, t):
                    n, j, c = self.n, t // 2, t % 2
                    pe.wait_ge(m["rt_ready"], b * 16 + (t + 1 + CREDIT))
                    if t < 2:
                        if isinstance(b, int) and b == 0:
                            pe.wait_ge(m["w1_low"], 2)
                        else:
                            pe.wait_ge(m["gelu_ready"], b * 2 + (c - 1))
                    z = PS[(7, 4)[c]][:, 0:4 * n]
                    for h in range(2):
                        mm = self.layer(z, c, 8 * h + j, lambda x: x[:, j % 2, c, h:4 * n + h], t < 2 and h == 0,
                                        j == 7 and h == 1)
                    if t >= 14:
                        mm.then_inc(m["z_ready"], 1)

                def second_layer(self, b):
                    n = self.n
                    pe.wait_ge(m["gelu_ready"], b * 2 + 1)
                    h4 = hgel[:, 0, 0:4 * n].rearrange("p (q g n) -> p g q n", q=2, g=2)
                    for g in range(2):
                        mm = pe.matmul(PS[0][g * HD:g * HD + HD, 0:2 * n], w2[:, 0, :], h4[:, g, :, :],
                                       start=True, stop=True)
                    mm.then_inc(m["kv_ready"], 1)
                    pe.wait_ge(m["gelu_ready"], b * 2 + 2)
                    for g in range(NKV):
                        out = PS[1][0:n, g * HD:g * HD + HD]
                        pe.matmul(out, ones[0:1, 0:n], b2v[0:1, g * HD:g * HD + HD], start=True, stop=False)
                        mm = pe.matmul(out, hgel[:, 1, g * n:g * n + n], w2[:, 1, :], start=False, stop=True)
                    mm.then_inc(m["kv_ready"], 1)

                def batch(self, b, last=None, at12=None):
                    for t in range(16):
                        self.turn(b, t)
                        if t > 1:
                            self.first_layer(b, t - 2)
                        elif last is not None:
                            self.first_layer(last, 14 + t)
                        if t == 4 and last is not None:
                            self.second_layer(last)
                        if t == 12 and at12:
                            at12()

                def end(self, b):
                    self.first_layer(b, 14)
                    self.first_layer(b, 15)
                    self.second_layer(b)

            pe.wait_ge(m["consts_loaded"], 16)
            pe.wait_ge(m["x_loaded"], 32)
            for k in range(KT):
                for t, (at, n) in enumerate(TOK_TILES):
                    mm = pe.transpose(PS[k][:, at:at + n], xin[0:n, t, k * P:k * P + P], ident[0:n, 0:n])
                mm.then_inc(m["turned"], 1)
            pe.wait_ge(m["vecs_loaded"], 16 * 12)
            pe.wait_ge(m["turned_out"], 1)
            pe.transpose(PS[0][:, 0:V_ROWS], vr[0:V_ROWS, 0:P], ident[0:V_ROWS, 0:V_ROWS]).then_inc(m["turned"], 1)
            for h in range(2):
                pe.wait_ge(m["turned_out"], h + 2)
                pe.transpose(PS[h + 1][:, 0:124], vr[0:124, P * (h + 1):P * (h + 2)], ident[0:124, 0:124]) \
                    .then_inc(m["turned"], 1)
            pe.wait_ge(m["turned_out"], KT + 3)
            ffn("00")
            pe.wait_ge(m["hist_loaded"], 32)
            pe.wait_ge(m["consts_loaded"], 32)
            for h in range(2):
                for a in range(2):
                    for k in range(4):
                        kk = 4 * a + k
                        mm = pe.transpose(PS[4 + 2 * h + a][:, k * 120:k * 120 + 120],
                                          hist[:, h, kk * P:kk * P + P], ident[0:120, 0:120])
                    mm.then_inc(m["turned"], 1)

            def pw1_mean():
                pe.wait_ge(m["hist_out"], 1)
                row_mean()
            slabs("pw1", gated, first=rows_in(pw1_mean))
            pe.wait_ge(m["vnew_ready"], 1)
            for k in range(KT):
                b, c = k // 4, (k % 4) * P
                pe.transpose(PS[b][0:TS, c:c + P], vnew[:, k, :], ident)
                mm = pe.transpose(PS[2 + b][0:HIST, c:c + P], full[:, k, PROMPT_W - HIST:PROMPT_W], ident)
            mm.then_inc(m["conv_turned"], 1)
            pe.wait_ge(m["conv_rows"], 4)
            pe.wait_ge(m["w1_loaded"], 32)
            for c in range(2):
                for j in range(16):
                    mm = pe.matmul(PS[3][:, c:c + 1], w1[:, c, j, :], vecs[:, V_PE + 16 * c + j:V_PE + 16 * c + j + 1],
                                   start=j == 0, stop=j == 15)
            mm.then_inc(m["turned"], 1)
            pe.wait_ge(m["cst_ready"], 2)
            pe.wait_ge(m["misc_loaded"], 16 * 7)
            cached = Compression(P, lambda z, c, j, rows_, start, stop: product(
                z, [w[:, c, j, :] for w in w1s], [rows_(x) for x in RTs], start, stop))
            cached.batch(0)
            with pe.Fori(0, NB - 2) as b:
                cached.batch(b + 1, b)
            cached.batch(NB - 1, NB - 2, lambda: channel_mean((m["ssum_ready"], 1), 3))
            cached.end(NB - 1)
            channel_mean((m["ln_step"], KT))
            slabs("pw2", pair, first=rows_in())
            ffn("01")
            slabs("kv", kv, first=rows_in(lambda: row_mean(tokens=True), KT - 1))
            pe.wait_ge(m["evac_done"], outs_[0] + CREDIT)
            for br in range(2):
                for q in range(2):
                    for t, (at, n) in enumerate(TOK_TILES):
                        src = rows[:, t, 2 + 2 * br, q * P:q * P + P] if t < 2 else rowsS[:, 2 + 2 * br, q * P:q * P + P]
                        mm = pe.transpose(PS[4 + 2 * br + q][:, at:at + n], src, ident[0:n, 0:n])
                    mm.then_inc(m["kT_turned"], 1)
            pe.wait_ge(m["kT_out"], 4)
            ffn("10", mean=False)
            slabs("q", pair, first=rows_in(lambda: row_mean(tokens=True)))
            for t in range(2):
                for k in range(KT):
                    mm = product(PS[5][:, t * 48:t * 48 + 48], [x[:, k, t * P:t * P + P] for x in hR],
                                 [wgh[:, k, :], wgl[:, k, :]], k == 0, k == KT - 1)
            mm.then_inc(m["gate_logits"], 1)
            for r in range(3):
                for k in range(KT):
                    mm = product(PS[6][0:NH, r * TS:r * TS + TS], [w[:, k, r * NH:r * NH + NH] for w in (wgh, wgl)],
                                 [x[:, k, SEQ:] for x in hR], k == 0, k == KT - 1)
            mm.then_inc(m["gate_logits"], 1)
            pe.wait_ge(m["gate_sig"], 2)
            pe.matmul(PS[7][:, 0:3 * TS], cn("head_rows", NH), gsig[:, :], start=True, stop=True) \
                .then_inc(m["gate_spread"], 1)
            pe.wait_ge(m["evac_done"], outs_[0] + CREDIT)
            pe.wait_ge(m["gate_out"], 1)
            pe.wait_ge(m["w1p_loaded"], 32)
            prompt = Compression(NCP, lambda z, c, j, rows_, start, stop: pe.matmul(
                z, w1p[:, c, j, :], rows_(RTp), start=start, stop=stop))
            prompt.batch(NB)
            prompt.end(NB)
            pe.wait_ge(m["kv_out"], 2 * (NB + 1))

            for q in range(2):
                def unit(z, back, w):
                    return z * 4 + (16 * q + w + 1 - 4 * back)

                def scores(z, w):
                    g, t = w // 2, w % 2
                    n = P * (t + 1)
                    if w == 0:
                        pe.wait_ge(m["qsl_ready"], z + (4 * q + 1))
                    if q or w > 1 or not isinstance(z, int) or z:
                        pe.wait_ge(m["p_max"], unit(z, 0, w) - 2)
                    lhs = qsl[:, g, t * P:t * P + P]
                    X, Y = PS[2 * (w % 2)], PS[2 * (w % 2) + 1]
                    pe.matmul(X[:, 0:n], lhs, kT[:, 0, q, 0:n], start=True, stop=True)
                    pe.matmul(X[:, 256:256 + NCP], lhs, kcTp[:, q, :], start=True, stop=True)
                    pe.matmul(Y[:, 0:n], lhs, kT[:, 1, q, 0:n], start=True, stop=True) \
                        .then_inc(m["p_scores"], 1)

                def turn(z, back, w):
                    t = w % 2
                    pe.wait_ge(m["p_scaled"], unit(z, back, w))
                    if q or w or not isinstance(z, int) or z - back:
                        pe.wait_ge(m["p_PT"], unit(z, back, w) - 1)
                    for c in range(2 * (t + 1)):
                        br, k = c // (t + 1), c % (t + 1)
                        pe.transpose(PS[4][:, c * P:c * P + P], SP_[:, w, br * 256 + k * P:br * 256 + k * P + P], ident)
                    pe.transpose(PS[5][0:NCP, 0:P], SP_[:, w, 512:528], ident).then_inc(m["p_turned"], 1)

                def values(z, back, w):
                    g, t, v = w // 2, w % 2, w % 2
                    grp = 2 * q + g
                    pe.wait_ge(m["p_PT"], unit(z, back, w))
                    out = PS[6 + t][:, bass.ds(z * P + (g * HD - back * P), HD)]
                    for c in range(2 * (t + 1)):
                        br, k = c // (t + 1), c % (t + 1)
                        pe.matmul(out, PTp[:, v, c, :], rows[:, k, 3 + 2 * br, grp * HD:grp * HD + HD],
                                  start=c == 0, stop=False)
                    pe.matmul(out, PTp[0:NCP, v, 4, :], vcp[:, grp * HD:grp * HD + HD], start=False, stop=True) \
                        .then_inc(m["p_out"], 1)

                def step(z, w, first=False):
                    scores(z, w)
                    if w >= 3 or not first:
                        turn(z, w < 3, (w - 3) % 4)
                    if not first:
                        values(z, 1, w)

                for w in range(4):
                    step(0, w, first=True)
                with pe.Fori(1, NZ) as z:
                    for w in range(4):
                        step(z, w)
                for w in range(4):
                    if w:
                        turn(NZ - 1, 0, w)
                    values(NZ - 1, 0, w)
                pe.wait_ge(m["o_evac"], 2 * q + 2)
            for c in range(8):
                for t in range(2):
                    mm = pe.transpose(PS[c // 2][:, (c % 2) * 256 + t * P:(c % 2) * 256 + t * P + P],
                                      oP[:, t, c * P:c * P + P], ident)
                if c % 2:
                    mm.then_inc(m["oP_turned"], 1)
            pe.wait_ge(m["oP_out"], 4)
            pe.wait_ge(m["attn_in"], 1)

            prob_groups = [[(S_NEW, TS), (S_WNEW, TS), (S_CMP, P)], [(S_WIN + c * P, P) for c in range(4)]] + \
                [[(S_SEL + (4 * g + c) * P, P) for c in range(4)] for g in range(4)]

            def turn_probs(b, g):
                if g == 0:
                    pe.wait_ge(m["s_scaled"], b + 1)
                pe.wait_ge(m["pt_out"], b * 6 + (g + 1))
                pe.sem_inc(m["passed"], 1)
                for c, (at, n) in enumerate(prob_groups[g]):
                    mm = pe.transpose(PS[5 + g % 2][0:n, c * P:c * P + P], S[:, at:at + n], ident)
                mm.then_inc(m["pt_turned"], 1)

            def batch_scores(i, off, before):
                b, u = i * 2 + off, off % 2
                last = i * 2 + (off - 1)

                def chunk(c, mms):
                    pe.wait_ge(m["s_biased"], b * 6 + (c + 1))
                    bank = PS[2 + c % 2]
                    for at, n, keys in mms:
                        for q in range(2):
                            mm = pe.matmul(bank[:, at:at + n], qbd[:, q, :], keys(q), start=q == 0, stop=q == 1)
                    mm.then_inc(m["s_scores"], 1)

                def turn_keys(r, tiles):
                    pe.wait_ge((m["kt_out0"], m["kt_out1"])[r % 2], b * 5 + (r // 2 + 1))
                    for c, t in enumerate(tiles):
                        mm = pe.transpose(PS[r % 2][:, c * P:c * P + P], t, ident)
                        if r == 8 and c == 0:
                            mm.then_inc(K_used, 1)
                    mm.then_inc(m["kt_turned"], 1)

                def turn_before(g):
                    if before:
                        turn_probs(last, g)

                turn_before(0)
                turn_before(1)
                pe.wait_ge(m["qbd_ready"], b + 1)
                chunk(0, [(0, TS, lambda q: kT[:, 0, q, SEQ:]), (TS, TS, lambda q: kT[:, 1, q, SEQ:]),
                          (2 * TS, P, lambda q: kcT[:, bass.ds(b, 1), q, :].rearrange("p a n -> p (a n)"))])
                turn_before(2)
                pe.wait_ge(K_loaded, b * 256 + 256)
                for r in range(8):
                    turn_keys(r, [kpg[:, 4 * (r % 4) + c, (r // 4) * P:(r // 4) * P + P] for c in range(4)])
                    if r in (1, 3, 5):
                        turn_before(3 + r // 2)
                pe.wait_ge(win_loaded[u], i * 16 + (off // 2 * 16 + 16))
                for q in range(2):
                    turn_keys(8 + q, [wst[u][:, c, q * P:q * P + P] for c in range(4)])
                pe.wait_ge(m["c_scaled"], b + 1)
                pe.matmul(PS[4][:, 0:P], S[:, S_CMP:S_COLS], cn("zsum"), start=True, stop=True) \
                    .then_inc(m["imp_sum"], 1)
                for o in range(2):
                    pe.wait_ge((m["kt_out0"], m["kt_out1"])[o], b * 5 + 6)
                chunk(1, [(0, 512, lambda q: KTb[:, q, 0:512])])
                pe.wait_ge(m["imp_sumout"], b + 1)
                pe.matmul(PS[4][:, P:P + NSEL], ips, cn("overlap"), start=True, stop=True) \
                    .then_inc(m["imp_ready"], 1)
                for c in range(1, 4):
                    chunk(c + 1, [(0, 512, lambda q: KTb[:, q, c * 512:c * 512 + 512])])
                chunk(5, [(0, WIN, lambda q: KTw[:, q, :])])

            def batch_values(i, off, page=vpg, loaded=None):
                b, u = i * 2 + off, off % 2

                def value(c, n, v, first=False, last=False):
                    return pe.matmul(PS[7][:, 0:256], PT[0:n, c * P:c * P + P], v, start=first, stop=last)

                pe.wait_ge(*(loaded or (V_loaded, b * 256 + 256)))
                pe.wait_ge(m["o_copied"], b + 1)
                pe.wait_ge(m["pt_out"], b * 6 + (6 + CREDIT))
                value(0, TS, rowsS[:, 3, :], first=True)
                value(1, TS, rowsS[:, 5, :])
                value(2, P, vc[:, bass.ds(b, 1), :].rearrange("p a n -> p (a n)"))
                for c in range(4):
                    mm = value(3 + c, P, wst[u][:, c, 256:512])
                mm.then_inc(win_used[u], 1)
                for k in range(NPAGE):
                    mm = value(7 + k, P, page[:, k, :], last=k == NPAGE - 1)
                mm.then_inc(m["o_ready"], 1)
                pe.wait_ge(m["o_copied"], b + 2)
                pe.transpose(PS[4][:, 256:384], osb[:, 0:P], ident).then_inc(V_used, 1)
                pe.transpose(PS[4][:, 384:512], osb[:, P:256], ident).then_inc(m["o_turned"], 1)

            batch_scores(0, 0, False)
            with pe.Fori(0, NB // 2 - 1) as i:
                for u in range(2):
                    batch_scores(i, u + 1, True)
                    batch_values(i, u)
            batch_scores(NB // 2 - 1, 1, True)
            batch_values(NB // 2 - 1, 0)
            for g in range(6):
                turn_probs(NB - 1, g)
            pe.wait_ge(m["o_out"], 2 * (NB - 1))
            batch_values(NB // 2 - 1, 1, kpg, (V_last_loaded, 16 * NPAGE))
            pe.wait_ge(m["o_out"], 2 * NB)
            slabs("o", pair, first=rows_in())
            ffn("11")
            row_mean()
            seen.wait(pe, m["h_ready"], 1)
            for g in range(6):
                t, h = g // 2, g % 2
                at, n = TOK_TILES[t]
                for k in range(4):
                    mm = pe.transpose(PS[g][0:n, k * P:k * P + P], oT[:, 4 * h + k, at:at + n], ident)
                mm.then_inc(m["y_turned"], 1)

        def act_program(act):
            seen = Seen()

            warmed = [0]

            def warm_up(func):
                act.activation(warm[:, warmed[0]:warmed[0] + 1], eps[:, :], func)
                warmed[0] += 1

            def split(ph, i, u, ahead=0):
                act.wait_ge(slab_loaded[u], ph.loaded(i, ahead))
                act.wait_ge(m["slab_used"], ph.upto(i, u, ahead))
                act.activation(flat_slab[u][HI][:, 0:ph.cols], flat_slab[u][RAW][:, 0:ph.cols], ACT.Copy) \
                    .then_inc(m["hi_ready"], 1)

            def slabs(name, after, work=None, split_first=False, closing=None):
                ph = PH[name]
                with act.Fori(0, ph.n // 2 - 1) as i:
                    for u in range(2):
                        if split_first:
                            split(ph, i, u, 1)
                        if work:
                            work(i, u)
                        if not split_first:
                            split(ph, i, u, 1)
                for u in range(2):
                    if work:
                        work(ph.n // 2 - 1, u)
                    if closing and u:
                        closing()
                    if after:
                        split(PH[after], 0, u)

            glus = [0]

            def glu(name, after, func):
                warm_up(func)

                g0 = glus[0]

                def work(i, u):
                    act.wait_ge(m["scaled"], i * 2 + (g0 + u + 1))
                    act.activation(tmp[:, u, :], tmp[:, u, :], func).then_inc(m["act_glu"], 1)
                glus[0] += PH[name].n
                slabs(name, after, work)

            def root(tokens=False):
                warm_up(ACT.Sqrt)
                seen.wait(act, m["mean_ready"])
                if tokens:
                    act.activation(rtok[:, 0, 0:2], PS[4][:, 384:386], ACT.Sqrt, bias=eps[:, 0:1])
                    act.activation(rtok[0:TS, 0, 2:3], PS[4][0:TS, 386:387], ACT.Sqrt, bias=eps[0:TS, 0:1])
                act.activation(stat[:, 1, :], PS[4][:, 0:T], ACT.Sqrt, bias=eps[:, 0:1]).then_inc(m["std_ready"], 1)

            def rows_hi():
                for k in range(KT):
                    seen.wait(act, m["h_raw"])
                    act.activation(hR[0][:, k, :], tmp[:, k % 4, :], ACT.Copy).then_inc(m["h_hi"], 1)

            def down(name, after):
                h0 = seen[m["h_raw"]]

                def work(i, u):
                    if u:
                        act.wait_ge(m["h_raw"], i + (h0 + 1))
                        act.activation(hR[0][:, bass.ds(i, 1), :].rearrange("p a t -> p (a t)"), tmp[:, 0, :], ACT.Copy) \
                            .then_inc(m["h_hi"], 1)
                slabs(name, after, work if after else None, split_first=True)
                if after:
                    seen.add(m["h_raw"], KT)

            def ffn(name, after, mean=True):
                if mean:
                    root()
                glu("up" + name, "down" + name, ACT.Silu)
                down("down" + name, after)

            class Compression:

                def __init__(self, n, RT, out_sem, halves, loaded, kout, vout):
                    self.n, self.RT, self.out_sem, self.halves, self.loaded = n, RT, out_sem, halves, loaded
                    self.kout, self.vout = kout, vout

                def relay(self, b, t):
                    n, j, c = self.n, t // 2, t % 2
                    if t % 8 == 0:
                        self.loaded(b, t // 8)
                    src = self.halves[j // 4][0:n, 2 * (j % 4):2 * (j % 4) + 2, c * 256:c * 256 + 256]
                    act.activation(RL[0:n, c, :].rearrange("p (g s d) -> p s g d", g=NKV, s=2),
                                   src.rearrange("p s (g d) -> p s g d", g=NKV), ACT.Copy).then_inc(m["rl_ready"], 1)

                def turned_out(self, b, t):
                    n, j, c = self.n, t // 2, t % 2
                    act.wait_ge(m["rt_turned"], b * 16 + (t + 1))
                    act.activation(self.RT[:, j % 2, c, 0:4 * n], PS[5 + c][:, 0:4 * n], ACT.Copy) \
                        .then_inc(self.out_sem, 1)

                def gelus(self, b):
                    for c in range(2):
                        act.wait_ge(m["z_ready"], b * 2 + (c + 1))
                        act.activation(hgel[:, c, 0:4 * self.n], PS[(7, 4)[c]][:, 0:4 * self.n], ACT.Gelu_apprx_tanh,
                                       bias=cst[:, c:c + 1]).then_inc(m["gelu_ready"], 1)

                def results(self, b):
                    n = self.n
                    act.wait_ge(m["kv_ready"], b * 2 + 1)
                    act.activation(self.kout(b), PS[0][:, 0:2 * n].rearrange("p (q n) -> p q n", q=2), ACT.Identity,
                                   bias=vecs[:, V_B2:V_B2 + 1]).then_inc(m["kv_out"], 1)
                    act.wait_ge(m["kv_ready"], b * 2 + 2)
                    act.activation(self.vout(b), PS[1][0:n, 0:256], ACT.Copy).then_inc(m["kv_out"], 1)

                def batch(self, b, last=None, after=None):
                    for t in range(16):
                        self.turned_out(b, t)
                        if t < 14:
                            self.relay(b, t + 2)
                        elif after is not None:
                            self.relay(after, t - 14)
                        if t in (6, 14):
                            act.wait_ge(m["rl_ready"], b * 16 + (8 + 8 * (t // 14)))
                            act.sem_inc(half_used[t // 14], 1)
                        if t == 1 and last is not None:
                            self.gelus(last)
                        if t == 6 and last is not None:
                            self.results(last)

                def end(self, b):
                    self.gelus(b)
                    self.results(b)

            act.sem_inc(m["rt_ready"], CREDIT)
            for u in range(2):
                act.sem_inc(half_used[u], CREDIT_H)
            for k in range(KT):
                act.wait_ge(m["turned"], k + 1)
                act.activation(xT[:, k, :], PS[k][:, 0:T], ACT.Copy).then_inc(m["turned_out"], 1)
            for i, (dst, n) in enumerate(((vecs[:, :], V_ROWS), (wdw[:, 0:124], 124), (wdw[:, 124:248], 124))):
                act.wait_ge(m["turned"], KT + 1 + i)
                act.activation(dst, PS[i][:, 0:n], ACT.Copy).then_inc(m["turned_out"], 1)
            act.wait_ge(m["pool_step"], 3)
            split(PH["up00"], 0, 0)
            rows_hi()
            split(PH["up00"], 0, 1)
            root()
            glu("up00", "down00", ACT.Silu)
            down("down00", "pw1")

            def history(i):
                h, a = i // 2, i % 2
                act.wait_ge(m["turned"], KT + 4 + i)
                act.activation(fullS[:, 4 * a:4 * a + 4, 4 * h:4 * h + 4, 0:HIST],
                               PS[4 + i][:, 0:480].rearrange("p (k b r) -> p k b r", k=4, b=4), ACT.Copy) \
                    .then_inc(m["hist_out"], 1)
            for i in range(4):
                history(i)
            root()
            glu("pw1", None, ACT.Sigmoid)
            act.wait_ge(m["conv_turned"], 1)
            for h in range(2):
                act.activation(convS[:, 512 * h:512 * h + 512], PS[h][0:TS, :], ACT.Copy).then_inc(m["conv_rows"], 1)
                act.activation(convP[:, 512 * h:512 * h + 512], PS[2 + h][0:HIST, :], ACT.Copy) \
                    .then_inc(m["conv_rows"], 1)
            act.wait_ge(m["misc_loaded"], 16 * 7)
            act.activation(wgh[:, :, :], wg[:, :, :], ACT.Copy).then_inc(m["wg_hi"], 1)
            act.wait_ge(m["w1_loaded"], 32)
            for c in (1, 0):
                act.activation(w1s[0][:, c, :, :], w1[:, c, :, :], ACT.Copy).then_inc(m["w1_high"], 1)
            act.wait_ge(m["turned"], KT + 8)
            for c in range(2):
                act.activation(cst[:, c:c + 1], PS[3][:, c:c + 1], ACT.Identity,
                               bias=vecs[:, V_B1 + c:V_B1 + c + 1]).then_inc(m["cst_ready"], 1)
            act.wait_ge(m["cst_ready"], 2)
            act.wait_ge(m["w1_low"], 1)
            warm_up(ACT.Gelu_apprx_tanh)
            cached = Compression(P, RTs[0], m["rt_high"], STG, lambda b, u: act.wait_ge(gathered[u], b * 128 + 128),
                                 lambda b: kcT[:, bass.ds(b, 1), :, :].rearrange("p a q n -> p (a q) n"),
                                 lambda b: vc[:, bass.ds(b, 1), :].rearrange("p a n -> p (a n)"))
            cached.relay(0, 0)
            cached.relay(0, 1)
            cached.batch(0, after=1)
            with act.Fori(0, NB - 2) as b:
                cached.batch(b + 1, b, b + 2)
            cached.batch(NB - 1, NB - 2)
            seen.wait(act, m["mean_ready"])
            cached.gelus(NB - 1)
            split(PH["pw2"], 0, 0)
            cached.results(NB - 1)
            for k in range(KT):
                seen.wait(act, m["cen_ready"])
                if k >= 4:
                    act.wait_ge(m["ln_step"], k - 3)
                act.activation(tmp[:, k % 4, :], csum[:, k, :], ACT.Square).then_inc(m["sq_ready"], 1)
            root()
            warm_up(ACT.Silu)

            def silu(k):
                seen.wait(act, m["cen_ready"])
                act.activation(csum[:, k, :], csum[:, k, :], ACT.Silu, scale=vecs[:, V_LNG + k:V_LNG + k + 1],
                               bias=vecs[:, V_LNB + k:V_LNB + k + 1]).then_inc(m["h_raw"], 1)
            silu(0)
            for k in range(KT):
                if k < KT - 1:
                    silu(k + 1)
                seen.wait(act, m["h_raw"])
                act.activation(hR[0][:, k, :], csum[:, k, :], ACT.Copy).then_inc(m["h_hi"], 1)
            split(PH["pw2"], 0, 1)
            slabs("pw2", "up01", closing=rows_hi)
            ffn("01", "kv")
            root(tokens=True)
            slabs("kv", "up10")
            for i in range(4):
                act.wait_ge(m["kT_turned"], i + 1)
                act.activation(kT[:, i // 2, i % 2, :], PS[4 + i][:, 0:T], ACT.Copy).then_inc(m["kT_out"], 1)
            rows_hi()
            ffn("10", "q", mean=False)
            root(tokens=True)
            slabs("q", None)
            act.wait_ge(m["gate_logits"], 1)
            for t in range(2):
                a = act.activation(gateP[:, t, :], PS[5][:, t * 48:t * 48 + 48], ACT.Sigmoid, scale=rtok[:, 1, t:t + 1])
            a.then_inc(m["gate_sig"], 1)
            act.wait_ge(m["gate_scaled"], 1)
            act.activation(gsig[:, :], gsig[:, :], ACT.Sigmoid).then_inc(m["gate_sig"], 1)

            warm_up(ACT.Gelu_apprx_tanh)
            prompt = Compression(NCP, RTp, m["rt_ready"], STGp, lambda b, u: act.wait_ge(m["prow_loaded"], 32),
                                 lambda b: kcTp[:, :, :], lambda b: vcp[:, :])
            prompt.relay(NB, 0)
            prompt.relay(NB, 1)
            prompt.batch(NB)
            prompt.end(NB)

            for q in range(2):
                def exps(z, w):
                    n = P * (w % 2 + 1)
                    act.wait_ge(m["p_max"], z * 4 + (16 * q + w + 1))
                    for r in range(3):
                        x = SP_[:, w, 512:528] if r == 0 else SP_[:, w, 256 * (r - 1):256 * (r - 1) + n]
                        e = act.activation(x, x, ACT.Exp, bias=small[:, w, r:r + 1],
                                           accum_out=small[:, w, 4 + r:5 + r] if r else None)
                    e.then_inc(m["p_exp"], 1)

                def scaled(z, back, w):
                    n = P * (w % 2 + 1)
                    act.wait_ge(m["p_weights"], z * 4 + (16 * q + w + 1 - 4 * back))
                    for r in range(3):
                        x = SP_[:, w, 512:528] if r == 0 else SP_[:, w, 256 * (r - 1):256 * (r - 1) + n]
                        e = act.activation(x, x, ACT.Copy, scale=small[:, w, 12 + r:13 + r])
                    e.then_inc(m["p_scaled"], 1)

                def probs(z, back, w):
                    v, t = w % 2, w % 2
                    act.wait_ge(m["p_turned"], z * 4 + (16 * q + w + 1 - 4 * back))
                    act.activation(PTp[:, v, 0:2 * (t + 1), :].rearrange("p c n -> p (c n)"),
                                   PS[4][:, 0:256 * (t + 1)], ACT.Copy)
                    act.activation(PTp[0:NCP, v, 4, :], PS[5][0:NCP, 0:P], ACT.Copy).then_inc(m["p_PT"], 1)

                for w in range(4):
                    if w >= 3:
                        probs(0, 0, w - 3)
                    exps(0, w)
                    if w:
                        scaled(0, 0, w - 1)
                with act.Fori(1, NZ) as z:
                    for w in range(4):
                        probs(z, w < 3, (w - 3) % 4)
                        exps(z, w)
                        scaled(z, w < 1, (w - 1) % 4)
                scaled(NZ - 1, 0, 3)
                for w in range(1, 4):
                    probs(NZ - 1, 0, w)

            for s, n in ((m["kt_out0"], 1), (m["pt_out"], CREDIT), (m["o_copied"], 1)):
                act.sem_inc(s, n)

            def probs_out(b, g):
                act.wait_ge(m["pt_turned"], b * 6 + (g + 1))
                if g == 0:
                    act.activation(PT[0:TS, 0:256], PS[5][0:TS, 0:256], ACT.Copy)
                    act.activation(PT[:, 256:384], PS[5][:, 256:384], ACT.Copy).then_inc(m["pt_out"], 1)
                else:
                    at = (3 + 4 * (g - 1)) * P
                    act.activation(PT[:, at:at + 512], PS[5 + g % 2][:, :], ACT.Copy).then_inc(m["pt_out"], 1)

            def batch_scores(b, last):
                def keys(r):
                    act.wait_ge(m["kt_turned"], b * 10 + (r + 1))
                    dst = KTb[:, r // 4, (r % 4) * 512:(r % 4) * 512 + 512] if r < 8 else KTw[:, r - 8, :]
                    act.activation(dst, PS[r % 2][:, :], ACT.Copy).then_inc(m["kt_out0"], 1)

                def before(g):
                    if last is not None:
                        probs_out(last, g)
                for g in range(3):
                    before(g)
                keys(0)
                act.wait_ge(m["c_max"], b + 1)
                act.activation(S[:, S_CMP:S_COLS], S[:, S_CMP:S_COLS], ACT.Exp, bias=small[:, 0, 0:1],
                               accum_out=small[:, 0, 4:5]).then_inc(m["c_exp"], 1)
                for r in range(2, 10, 2):
                    if r < 8:
                        before(2 + r // 2)
                    keys(r)
                act.wait_ge(m["imp_sum"], b + 1)
                act.activation(ips, PS[4][:, 0:P], ACT.Copy).then_inc(m["imp_sumout"], 1)
                act.wait_ge(m["s_max"], b * 2 + 1)
                act.activation(S[:, S_WIN:S_CMP], S[:, S_WIN:S_CMP], ACT.Exp, bias=small[:, 0, 2:3],
                               accum_out=small[:, 0, 6:7]).then_inc(m["s_exp"], 1)
                act.wait_ge(m["s_max"], b * 2 + 2)
                act.activation(S[:, 0:S_WIN], S[:, 0:S_WIN], ACT.Exp, bias=small[:, 0, 1:2],
                               accum_out=small[:, 0, 5:6]).then_inc(m["s_exp"], 1)

            def batch_out(b):
                act.wait_ge(m["o_ready"], b + 1)
                act.activation(osb, PS[7][:, 0:256], ACT.Copy).then_inc(m["o_copied"], 1)

            batch_scores(0, None)
            with act.Fori(0, NB - 1) as b:
                batch_scores(b + 1, b)
                batch_out(b)
            for g in range(6):
                probs_out(NB - 1, g)
            act.wait_ge(m["pt_out"], 6 * NB + CREDIT)
            split(PH["o"], 0, 0)
            batch_out(NB - 1)
            act.wait_ge(m["o_out"], 2 * NB)
            act.wait_ge(m["oP_out"], 4)
            for k in range(KT):
                act.activation(hR[0][:, k, :], oT[:, k, :], ACT.Copy).then_inc(m["h_hi"], 1)
            split(PH["o"], 0, 1)
            slabs("o", "up11", closing=rows_hi)
            ffn("11", None)
            root()

        def dve_program(dve):
            seen = Seen()
            steps = [0, 0]

            def did(ins):
                steps[1] += 1
                return ins.then_inc(m["dve_step"], 1)

            def settle():
                dve.wait_ge(m["dve_step"], steps[0] + steps[1])

            def low(u, upto, cols):
                dve.wait_ge(m["hi_ready"], upto)
                raw, hi, lo = [x[:, 0:cols] for x in flat_slab[u]]
                dve.tensor_tensor(lo, raw, hi, ALU.subtract).then_inc(m["lo_ready"], 1)

            def slabs(name, after, work, closing=None):
                ph = PH[name]

                def one(i, u, nxt, ahead):
                    dve.wait_ge(m["slab_used"], ph.upto(i, u) + CREDIT)
                    (closing if closing and nxt is not ph and u else work)(i, u)
                    if nxt:
                        low(u, nxt.upto(i if ahead else 0, u, ahead), nxt.cols)
                with dve.Fori(0, ph.n // 2 - 1) as i:
                    for u in range(2):
                        one(i, u, ph, 1)
                for u in range(2):
                    one(ph.n // 2 - 1, u, PH[after] if after else None, 0)
                outs_[0] += ph.n

            outs_ = [0]
            x_steps = [0]

            def squares(x, slot, step):
                dve.tensor_tensor(tmp[:, 2 + slot, :], x, x, ALU.mult).then_inc(m["x_step"], 1)
                dve.wait_ge(m["x_step"], step + 1)
                dve.tensor_tensor(stat[:, 0, :], stat[:, 0, :], tmp[:, 2 + slot, :], ALU.add).then_inc(m["x_step"], 1)

            def down(name, after, gain=None):
                ph, o, x0, h0 = PH[name], outs_[0], x_steps[0], seen[m["h_hi"]]

                def tile(i, u, last=False):
                    nxt = PH[after] if last and after else ph
                    at = [nxt.base + h + 1 for h in range(2)] if last else \
                        [i * 4 + (ph.base + 2 * u + 2 + h + 1) for h in range(2)]
                    split = not last or after
                    if split:
                        low(0, at[0], nxt.cols)
                    dve.wait_ge(m["slab_used"], i * 4 + (ph.base + 2 * u + 2 + CREDIT))
                    x = xT[:, bass.ds(i * 2 + u, 1), :].rearrange("p a t -> p (a t)")
                    dve.scalar_tensor_tensor(x, PS[2 * u][:, 0:T], 0.5, x, ALU.mult, ALU.add).then_inc(m["evac_done"], 1)
                    dve.wait_ge(m["evac_done"], i * 2 + (o + u + 1 + CREDIT))
                    if gain is not None:
                        dve.tensor_scalar(tmp[:, 0, :], x, vecs[:, bass.ds(i * 2 + (gain + u), 1)], None, ALU.mult) \
                            .then_inc(m["h_raw"], 1)
                    squares(x, u, i * 4 + (x0 + 2 * u))
                    if split and not last:
                        low(1, at[1], nxt.cols)
                    if gain is not None:
                        hi, lo = [y[:, bass.ds(i * 2 + u, 1), :].rearrange("p a t -> p (a t)") for y in hR]
                        dve.wait_ge(m["h_hi"], i * 2 + (h0 + u + 1))
                        dve.tensor_tensor(lo, tmp[:, 0, :], hi, ALU.subtract).then_inc(m["h_ready"], 1)
                    if split and last:
                        low(1, at[1], nxt.cols)
                with dve.Fori(0, KT // 2 - 1) as i:
                    for u in range(2):
                        tile(i, u)
                tile(KT // 2 - 1, 0)
                tile(KT // 2 - 1, 1, last=True)
                outs_[0] += KT
                x_steps[0] += SQ
                if gain is not None:
                    seen.add(m["h_hi"], KT)

            glus, gates_ = [0], [0]

            def scale_sums(u, gate):
                dve.tensor_tensor(tmp[:, u, :], PS[2 * u + gate][:, 0:T], stat[:, 2, :], ALU.mult) \
                    .then_inc(m["scaled"], 1)
                dve.tensor_tensor(tmp[:, 2 + u, :], PS[2 * u + 1 - gate][:, 0:T], stat[:, 2, :], ALU.mult) \
                    .then_inc(m["gate_step"], 1)

            def gate_rows(name):
                g0, a0 = gates_[0], glus[0]

                def work(i, u):
                    t, hi, lo = tmp[:, 2 + u, :], *[x[:, bass.ds(i * 2 + u, 1), :].rearrange("p a t -> p (a t)") for x in gR]
                    step = i * 6 + (g0 + 3 * u)
                    scale_sums(u, 0)
                    dve.wait_ge(m["act_glu"], i * 2 + (a0 + u + 1))
                    dve.wait_ge(m["gate_step"], step + 1)
                    dve.tensor_tensor(t, t, tmp[:, u, :], ALU.mult).then_inc(m["gate_step"], 1)
                    dve.wait_ge(m["gate_step"], step + 2)
                    dve.tensor_copy(hi, t).then_inc(m["gate_step"], 1)
                    dve.wait_ge(m["gate_step"], step + 3)
                    dve.tensor_tensor(lo, t, hi, ALU.subtract).then_inc(m["evac_done"], 1)
                slabs("up" + name, "down" + name, work)
                gates_[0] += 3 * FT
                glus[0] += FT

            def residual_pair(name, after, gain):
                o, x0 = outs_[0], x_steps[0]

                def add(i, u):
                    x = xT[:, bass.ds(i * 4 + 2 * u, 2), :]
                    dve.tensor_tensor(x, PSA[:, 2 * u:2 * u + 2, 0:T], x, ALU.add).then_inc(m["evac_done"], 1)
                    dve.wait_ge(m["evac_done"], i * 2 + (o + u + 1 + CREDIT))

                def pair_squares(i, u):
                    for k in range(2):
                        squares(xT[:, bass.ds(i * 4 + (2 * u + k), 1), :].rearrange("p a t -> p (a t)"), k,
                                i * 8 + (x0 + 4 * u + 2 * k))

                def work(i, u):
                    add(i, u)
                    pair_squares(i, u)

                def closing(i, u):
                    def last_squares():
                        pair_squares(i, u)
                        dve.wait_ge(m["x_step"], x0 + SQ)
                    add(i, u)
                    gained(gain, last_squares)
                slabs(name, after, work, closing)
                x_steps[0] += SQ

            def root(tokens=False):
                seen.add(m["mean_ready"])
                seen.wait(dve, m["std_ready"])
                if tokens:
                    dve.reciprocal(rtok[:, 1, 0:2], rtok[:, 0, 0:2])
                    did(dve.reciprocal(rtok[0:TS, 1, 2:3], rtok[0:TS, 0, 2:3]))
                did(dve.reciprocal(stat[:, 2, :], stat[:, 1, :]))
                did(dve.memset(stat[:, 0, :], 0.0))
                settle()

            def rows_lo(k, src):
                seen.wait(dve, m["h_hi"])
                dve.tensor_tensor(hR[1][:, k, :], src, hR[0][:, k, :], ALU.subtract).then_inc(m["h_ready"], 1)

            def gained(g, behind_first=None):
                for k in range(KT + 1):
                    if k < KT:
                        dve.tensor_scalar(tmp[:, k % 4, :], xT[:, k, :], vecs[:, g + k:g + k + 1], None, ALU.mult) \
                            .then_inc(m["h_raw"], 1)
                    if k:
                        rows_lo(k - 1, tmp[:, (k - 1) % 4, :])
                    if k == 1 and behind_first:
                        behind_first()

            def ffn(name, after, gain=None, mean=True):
                if mean:
                    root()
                gate_rows(name)
                down("down" + name, after, gain)

            for s, n in ((m["evac_done"], CREDIT), (m["lo_ready"], CREDIT)):
                dve.sem_inc(s, n)
            did(dve.memset(stat[:, 0, :], 0.0))
            settle()
            def first_squares(ks):
                for k in ks:
                    dve.wait_ge(m["turned_out"], k + 1)
                    squares(xT[:, k, :], k % 2, 2 * k)
            first_squares(range(KT - 2))
            x_steps[0] += SQ
            low(0, 1, PH["up00"].cols)
            dve.wait_ge(m["turned_out"], KT + 1)

            def last_squares():
                first_squares(range(KT - 2, KT))
                dve.wait_ge(m["x_step"], SQ)
            gained(V_NORM, last_squares)
            low(1, 2, PH["up00"].cols)
            root()
            gate_rows("00")
            down("down00", "pw1", V_NORM + 8)
            dve.memset(full[:, :, 0:HIST], 0.0)
            dve.wait_ge(m["ptrow_loaded"], 16 * 9)
            dve.wait_ge(m["consts_loaded"], 16)
            did(dve.tensor_scalar(ptabf[:, :], ptab[:, :], float(2 * PAGE), None, ALU.mult))
            settle()
            for b in range(NB):
                s = dve.tensor_scalar(cidx[:, b * CS:b * CS + CS], cn("token_row"), ptabf[:, b:b + 1], None, ALU.add)
            s.then_inc(m["idx_ready"], 1)

            root()
            a0, g0 = glus[0], gates_[0]

            def conv_rows_in(i, u):
                scale_sums(u, 1)
                dve.wait_ge(m["act_glu"], i * 2 + (a0 + u + 1))
                dve.wait_ge(m["gate_step"], i * 2 + (g0 + u + 1))
                k = bass.ds(i * 2 + u, 1)
                dve.tensor_tensor(full[:, k, HIST:PROMPT_W].rearrange("p a t -> p (a t)"),
                                  tmp[:, 2 + u, 0:SEQ], tmp[:, u, 0:SEQ], ALU.mult)
                dve.tensor_tensor(fullS[:, k, :, HIST:].rearrange("p a b r -> p (a b) r"),
                                  tmp[:, 2 + u, SEQ:].rearrange("p (b r) -> p b r", b=NB),
                                  tmp[:, u, SEQ:].rearrange("p (b r) -> p b r", b=NB), ALU.mult) \
                    .then_inc(m["evac_done"], 1)
            slabs("pw1", None, conv_rows_in)
            gates_[0] += KT
            glus[0] += KT
            for x in RTs:
                dve.memset(x[:, :, :, 4 * P:4 * P + 2].bitcast(F32), 0.0)
            dve.wait_ge(m["evac_done"], outs_[0] + CREDIT)
            dve.wait_ge(m["hist_out"], 4)
            dve.tensor_copy(vnew.rearrange("p k (b r) -> p k b r", b=NB), fullS[:, :, :, HIST:]) \
                .then_inc(m["vnew_ready"], 1)
            def conv_tiles(k):
                return (csum[:, k, 0:SEQ], lambda tap: full[:, k, bass.ds(tap, SEQ)],
                        csum[:, k, SEQ:].rearrange("p (b r) -> p b r", b=NB),
                        lambda tap: fullS[:, k, :, bass.ds(tap, NQ)])
            for k in range(KT):
                o1, i1, o2, i2 = conv_tiles(k)
                for o, x in ((o1, i1(0)), (o2, i2(0))):
                    dve.tensor_scalar(o, x, wdw[:, k:k + 1], vecs[:, V_BDW + k:V_BDW + k + 1], ALU.mult, ALU.add) \
                        .then_inc(m["conv_step"], 1)
            for i, c in enumerate((1, 0)):
                dve.wait_ge(m["w1_high"], i + 1)
                dve.tensor_tensor(w1s[1][:, c, :, :], w1[:, c, :, :], w1s[0][:, c, :, :], ALU.subtract) \
                    .then_inc(m["w1_low"], 1)

            TAPS_AT_ONCE = 4

            def compression_step(b, t):
                j, c = t // 2, t % 2
                dve.wait_ge(m["rt_high"], b * 16 + (t + 1))
                dve.tensor_tensor(RTs[1][:, j % 2, c, 0:4 * P], PS[5 + c][:, 0:4 * P], RTs[0][:, j % 2, c, 0:4 * P],
                                  ALU.subtract).then_inc(m["rt_ready"], 1)

            def convolution_step(b, t):
                a = t // 4
                for k in range(2 * (t % 4), 2 * (t % 4) + 2):
                    o1, i1, o2, i2 = conv_tiles(k)
                    for h, (o, x) in enumerate(((o1, i1), (o2, i2))):
                        dve.wait_ge(m["conv_step"], b * (16 * TAPS_AT_ONCE) + (16 * a + 2 * k + h + 1))
                        dve.scalar_tensor_tensor(o, x(b * TAPS_AT_ONCE + (a + 1)),
                                                 wdw[:, bass.ds(b * (TAPS_AT_ONCE * KT) + (a * KT + KT + k), 1)], o,
                                                 ALU.mult, ALU.add).then_inc(m["conv_step"], 1)

            with dve.Fori(0, NB - 1) as b:
                for t in range(16):
                    compression_step(b, t)
                    convolution_step(b, t)
            left = (TAPS - 1 - (NB - 1) * TAPS_AT_ONCE) * 4
            for t in range(16):
                compression_step(NB - 1, t)
                if t < left:
                    convolution_step(NB - 1, t)
                if t == left:
                    dve.wait_ge(m["conv_step"], 16 * TAPS)
                    dve.wait_ge(m["conv_turned"], 1)
                    dve.tensor_reduce(stat[:, 0, :], csum[:, :, :].rearrange("p k t -> p t k"), AX_X, ALU.add) \
                        .then_inc(m["ssum_ready"], 1)
            seen.wait(dve, m["mean_ready"])
            did(dve.memset(stat[:, 0, :], 0.0))
            settle()
            for k in range(KT + 1):
                if k < KT:
                    dve.tensor_tensor(csum[:, k, :], csum[:, k, :], PS[3][:, 0:T], ALU.subtract) \
                        .then_inc(m["cen_ready"], 1)
                if k:
                    seen.wait(dve, m["sq_ready"])
                    if k > 1:
                        dve.wait_ge(m["ln_step"], k - 1)
                    dve.tensor_tensor(stat[:, 0, :], stat[:, 0, :], tmp[:, (k - 1) % 4, :], ALU.add) \
                        .then_inc(m["ln_step"], 1)
            low(0, PH["pw2"].base + 1, PH["pw2"].cols)
            root()
            for k in range(KT):
                dve.tensor_tensor(csum[:, k, :], csum[:, k, :], stat[:, 2, :], ALU.mult).then_inc(m["cen_ready"], 1)
                if k > 1:
                    rows_lo(k - 2, csum[:, k - 2, :])
            rows_lo(KT - 2, csum[:, KT - 2, :])
            rows_lo(KT - 1, csum[:, KT - 1, :])
            low(1, PH["pw2"].base + 2, PH["pw2"].cols)
            dve.wait_ge(m["wg_hi"], 1)
            did(dve.tensor_tensor(wgl[:, :, :], wg[:, :, :], wgh[:, :, :], ALU.subtract))
            settle()
            residual_pair("pw2", "up01", V_NORM + 16)
            dve.wait_ge(m["conv_stored"], 16 * (NB + 1))
            ffn("01", "kv", V_KV)
            root(tokens=True)

            def kv_rows(i, u):
                c = bass.ds(i * 2 + u, 1)
                for t in range(2):
                    dve.tensor_scalar(rows[:, t, c, :].rearrange("p a n -> p (a n)"),
                                      PS[2 * u][:, t * 256:t * 256 + 256], rtok[:, 1, t:t + 1], None, ALU.mult)
                dve.tensor_scalar(rowsS[:, c, :].rearrange("p a n -> p (a n)"), PS[2 * u + 1][0:TS, 0:256],
                                  rtok[0:TS, 1, 2:3], None, ALU.mult).then_inc(m["evac_done"], 1)
            slabs("kv", "up10", kv_rows)
            gained(V_NORM + 24)
            ffn("10", "q", V_NORM + 32, mean=False)
            root(tokens=True)

            def queries(i, u):
                dve.scalar_tensor_tensor(qT[:, bass.ds(i * 4 + 2 * u, 2), :], PSA[:, 2 * u:2 * u + 2, 0:T], QSCALE,
                                         stat[:, 2:3, :].broadcast_to([P, 2, T]), ALU.mult, ALU.mult) \
                    .then_inc(m["evac_done"], 1)
            slabs("q", None, queries)
            dve.wait_ge(m["evac_done"], outs_[0] + CREDIT)
            dve.wait_ge(m["gate_logits"], 2)
            dve.tensor_tensor(gsig[:, :].rearrange("p (r t) -> p r t", r=3),
                              PS[6][0:NH, 0:3 * TS].rearrange("p (r t) -> p r t", r=3),
                              stat[0:NH, 2:3, SEQ:].broadcast_to([NH, 3, TS]), ALU.mult).then_inc(m["gate_scaled"], 1)
            dve.wait_ge(m["gate_spread"], 1)
            dve.memset(RTp[:, :, :, 4 * NCP:4 * NCP + 2], 0.0)
            gm = tmp[:, 1, 0:3 * TS].rearrange("p (n q) -> p n q", q=NQ)
            own = cn("own_query").rearrange("p (a q) -> p a q", a=1).broadcast_to([P, 3 * NB, NQ])
            did(dve.tensor_tensor(gm, PS[7][:, 0:3 * TS].rearrange("p (n q) -> p n q", q=NQ), own, ALU.mult))
            settle()
            dve.tensor_reduce(gateS[:, :, :], gm, AX_X, ALU.add).then_inc(m["gate_out"], 1)
            dve.wait_ge(m["kv_out"], 2 * (NB + 1))
            did(dve.memset(qsl[:, :, :], 0.0))
            settle()

            PSTEPS = 16
            pbase = steps[1]

            def queries_of(z, ahead):
                for g in range(2):
                    s = dve.tensor_copy(qsl[g * HD:g * HD + HD, g, :],
                                        qT[g * HD:g * HD + HD, bass.ds(z + ahead, 1), 0:SEQ].rearrange("p a t -> p (a t)"))
                s.then_inc(m["qsl_ready"], 1)

            queries_of(0, 0)
            for q in range(2):
                def biased(z, w):
                    g, t = w // 2, w % 2
                    n = P * (t + 1)
                    slope = cn("neg_slope")[:, bass.ds(z + (2 * q + g) * NZ, 1)]
                    dve.wait_ge(m["p_scores"], z * 4 + (16 * q + w + 1))
                    if w == 3 and not (isinstance(z, int) and q and z == NZ - 1):
                        queries_of(z, q * NZ + 1)
                    full_ = SP_[:, w, 0:512].rearrange("p (r n) -> p r n", r=2)[:, :, 0:n]
                    dve.scalar_tensor_tensor(full_, dist_full[:, t:t + 1, 0:n].broadcast_to([P, 2, n]), slope,
                                             PSA[:, 2 * t:2 * t + 2, 0:n], ALU.mult, ALU.add)
                    did(dve.scalar_tensor_tensor(SP_[:, w, 512:528], dist_cmp[:, t, :], slope,
                                                 PS[2 * t][:, 256:256 + NCP], ALU.mult, ALU.add))
                    settle()
                    dve.tensor_reduce(small[:, w, 1:3], full_, AX_X, ALU.max, negate=True)
                    dve.tensor_reduce(small[:, w, 0:1], SP_[:, w, 512:528], AX_X, ALU.max, negate=True) \
                        .then_inc(m["p_max"], 1)

                def weights(z, back, w):
                    g, t = w // 2, w % 2
                    gates = gateP[:, t, :].rearrange("p (r h) -> p r h", r=3)[:, :, bass.ds(z + ((2 * q + g) * NZ - back), 1)] \
                        .rearrange("p r a -> p (r a)")
                    dve.wait_ge(m["p_exp"], z * 4 + (16 * q + w + 1 - 4 * back))
                    did(dve.scalar_tensor_tensor(SP_[:, w, 512:528], SP_[:, w, 512:528], 1.0, live_cmp[:, t, :],
                                                 ALU.mult, ALU.mult, accum_out=small[:, w, 4:5]))
                    settle()
                    did(dve.tensor_scalar(small[:, w, 8:11], small[:, w, 4:7], TINY, None, ALU.max))
                    settle()
                    did(dve.reciprocal(small[:, w, 8:11], small[:, w, 8:11]))
                    settle()
                    dve.tensor_tensor(small[:, w, 12:15], small[:, w, 8:11], gates, ALU.mult).then_inc(m["p_weights"], 1)

                def step(z, w, first=False):
                    biased(z, w)
                    if w or not first:
                        weights(z, w < 1, (w - 1) % 4)

                start = pbase + q * NZ * PSTEPS
                steps[0], steps[1] = 0, start
                for w in range(4):
                    step(0, w, first=True)
                peeled = steps[1] - start
                with dve.Fori(1, NZ - 1) as z:
                    steps[0], steps[1] = z * PSTEPS, start + peeled - PSTEPS
                    for w in range(4):
                        step(z, w)
                    assert steps[1] == start + peeled
                steps[0], steps[1] = 0, start + peeled + (NZ - 2) * PSTEPS
                for w in range(4):
                    step(NZ - 1, w)
                weights(NZ - 1, 0, 3)
                assert steps[1] == start + NZ * PSTEPS
                for t in range(2):
                    dve.wait_ge(m["p_out"], 16 * (q + 1))
                    dve.tensor_copy(oP[:, t, 512 * q:512 * q + 512], PS[6 + t][:, :]).then_inc(m["o_evac"], 1)
            for c in range(4):
                dve.wait_ge(m["oP_turned"], c + 1)
                dve.tensor_copy(oT[:, 2 * c:2 * c + 2, 0:SEQ], PS[c][:, :].rearrange("p (k t) -> p k t", k=2)) \
                    .then_inc(m["oP_out"], 1)

            steps[0], steps[1] = 0, pbase + 2 * NZ * PSTEPS
            did(dve.memset(qbd[:, :, :], 0.0))
            did(dve.memset(imp[:, 0, :], FORCE))
            settle()
            dve.sem_inc(m["s_biased"], CREDIT)
            dve.sem_inc(m["kt_out1"], 1)
            dve.wait_ge(m["oP_turned"], 4)
            dve.drain().then_inc(m["attn_in"], 1)
            dve.wait_ge(m["selb_loaded"], 16)
            SSTEPS = 13
            sbase = steps[1]

            def batch_scores(b):
                steps[0], steps[1] = b * SSTEPS, sbase
                for q in range(2):
                    for g in range(2):
                        grp = 2 * q + g
                        s = dve.tensor_copy(
                            qbd[g * HD:g * HD + HD, q, grp * 32:grp * 32 + 32].rearrange("p (z r) -> p z r", z=NZ),
                            qT[g * HD:g * HD + HD, q * NZ:q * NZ + NZ, bass.ds(b * NQ + SEQ, NQ)])
                s.then_inc(m["qbd_ready"], 1)
                newb = cn("new_bias")[:, bass.ds(b * -NQ + 56, TS)]
                dve.wait_ge(m["s_scores"], b * 6 + 1)
                dve.tensor_tensor(S[:, S_NEW:S_WIN], PS[2][:, 0:TS], newb, ALU.add)
                dve.tensor_tensor(S[:, S_WNEW:S_CMP], PS[2][:, TS:2 * TS], newb, ALU.add)
                dve.tensor_tensor(S[:, S_CMP:S_COLS], PS[2][:, 2 * TS:2 * TS + P], cn("cmp_bias"), ALU.add) \
                    .then_inc(m["s_biased"], 1)
                dve.wait_ge(m["s_biased"], b * 6 + 1 + CREDIT)
                dve.tensor_reduce(small[:, 0, 0:1], S[:, S_CMP:S_COLS], AX_X, ALU.max, negate=True) \
                    .then_inc(m["c_max"], 1)

                def keys(r):
                    dve.wait_ge(m["kt_turned"], b * 10 + (r + 1))
                    dst = KTb[:, r // 4, (r % 4) * 512:(r % 4) * 512 + 512] if r < 8 else KTw[:, r - 8, :]
                    dve.tensor_copy(dst, PS[r % 2][:, :]).then_inc(m["kt_out1"], 1)

                def normalise(src, col):
                    did(dve.tensor_scalar(small[:, 0, 8 + col:8 + col + src], small[:, 0, 4 + col:4 + col + src], TINY,
                                          None, ALU.max))
                    settle()
                    did(dve.reciprocal(small[:, 0, 8 + col:8 + col + src], small[:, 0, 8 + col:8 + col + src]))
                    settle()

                keys(1)
                dve.wait_ge(m["c_exp"], b + 1)
                normalise(1, 0)
                dve.tensor_scalar(S[:, S_CMP:S_COLS], S[:, S_CMP:S_COLS], small[:, 0, 8:9], None, ALU.mult) \
                    .then_inc(m["c_scaled"], 1)
                for r in range(3, 10, 2):
                    keys(r)
                dve.wait_ge(m["imp_sum"], b + 1)
                dve.wait_ge(m["c_scaled"], b + 1)
                did(dve.tensor_scalar(S[:, S_CMP:S_COLS], S[:, S_CMP:S_COLS], gateS[:, 0, bass.ds(b, 1)], None,
                                      ALU.mult))

                def chunk(c):
                    dve.wait_ge(m["s_scores"], b * 6 + (c + 1))
                    at = 512 * (c - 1)
                    dst, bias = (S[:, at:at + 512], selb[:, at:at + 512]) if c < 5 else \
                        (S[:, S_WIN:S_WNEW], cn("win_bias"))
                    dve.tensor_tensor(dst, PS[2 + c % 2][:, :], bias, ALU.add).then_inc(m["s_biased"], 1)
                chunk(1)
                dve.wait_ge(m["imp_ready"], b + 1)
                did(dve.tensor_copy(imp[:, 0, 1:NSEL - 2], PS[4][:, P + 1:P + NSEL - 2]))
                settle()
                dve.sem_inc(m["passed"], 1)
                did(dve.max(out=top8[:, 0, :], in_=imp[:, 0, :]))
                settle()
                dve.sem_inc(m["passed"], 1)
                did(dve.match_replace(out=imp[:, 1, :], in_to_replace=top8[:, 0, :], in_values=imp[:, 0, :],
                                      imm_value=NEG))
                settle()
                dve.sem_inc(m["passed"], 1)
                did(dve.max(out=top8[:, 1, :], in_=imp[:, 1, :]))
                settle()
                dve.sem_inc(m["passed"], 1)
                did(dve.match_replace(out=imp[:, 2, :], in_to_replace=top8[:, 1, :], in_values=imp[:, 1, :],
                                      imm_value=NEG))
                settle()
                did(dve.tensor_scalar(imp[:, 3, :], imp[:, 2, :], NEG / 2, NEG, ALU.is_gt, ALU.mult))
                for c in range(2, 6):
                    chunk(c)
                dve.wait_ge(m["s_biased"], b * 6 + 6 + CREDIT)
                dve.tensor_reduce(small[:, 0, 2:3], S[:, S_WIN:S_CMP], AX_X, ALU.max, negate=True) \
                    .then_inc(m["s_max"], 1)
                settle()
                sblk = S[:, 0:PAST].rearrange("p (j l) -> p j l", l=SB)
                drop = imp[:, 3, 0:NSEL - 1].rearrange("p (j a) -> p j a", a=1).broadcast_to([P, NSEL - 1, SB])
                did(dve.tensor_tensor(sblk, sblk, drop, ALU.add))
                settle()
                dve.tensor_reduce(small[:, 0, 1:2], S[:, 0:S_WIN], AX_X, ALU.max, negate=True) \
                    .then_inc(m["s_max"], 1)
                dve.wait_ge(m["s_exp"], b * 2 + 2)
                normalise(2, 1)
                did(dve.tensor_tensor(small[:, 0, 12:14], small[:, 0, 9:11], gateS[:, 1:3, bass.ds(b, 1)]
                                      .rearrange("p r a -> p (r a)"), ALU.mult))
                settle()
                dve.tensor_scalar(S[:, S_WIN:S_CMP], S[:, S_WIN:S_CMP], small[:, 0, 13:14], None, ALU.mult)
                dve.tensor_scalar(S[:, 0:S_WIN], S[:, 0:S_WIN], small[:, 0, 12:13], None, ALU.mult) \
                    .then_inc(m["s_scaled"], 1)
                assert steps[1] - sbase == SSTEPS

            def batch_out(b):
                dve.wait_ge(m["o_turned"], b + 1)
                ob = PS[4][:, 256:512]
                for q in range(2):
                    for g in range(2):
                        grp = 2 * q + g
                        s = dve.tensor_copy(
                            oT[g * HD:g * HD + HD, q * NZ:q * NZ + NZ, bass.ds(b * NQ + SEQ, NQ)],
                            ob[g * HD:g * HD + HD, q * P + grp * 32:q * P + grp * 32 + 32].rearrange("p (z r) -> p z r", z=NZ))
                        if q:
                            s.then_inc(m["o_out"], 1)
            batch_scores(0)
            with dve.Fori(0, NB - 1) as b:
                batch_scores(b + 1)
                batch_out(b)
            low(0, PH["o"].base + 1, PH["o"].cols)
            batch_out(NB - 1)
            steps[0], steps[1] = 0, sbase + NB * SSTEPS
            for k in range(KT):
                rows_lo(k, oT[:, k, :])
            did(dve.memset(stat[:, 0, :], 0.0))
            settle()
            low(1, PH["o"].base + 2, PH["o"].cols)
            residual_pair("o", "up11", V_NORM + 40)
            ffn("11", None)
            root()
            for k in range(KT):
                s = dve.scalar_tensor_tensor(oT[:, k, :], xT[:, k, :], vecs[:, V_FINAL + k:V_FINAL + k + 1],
                                             stat[:, 2, :], ALU.mult, ALU.mult)
            s.then_inc(m["h_ready"], 1)
            for g in range(6):
                t, h = g // 2, g % 2
                at, n = TOK_TILES[t]
                dve.wait_ge(m["y_turned"], g + 1)
                dve.tensor_copy(yout[0:n, t, h * 512:h * 512 + 512], PS[g][0:n, :]).then_inc(m["y_out"], 1)


        with nc.Block() as block:
            @block.sync
            def _(sp):
                sp_program(sp)

            @block.gpsimd
            def _(pool):
                pool_program(pool)

            @block.scalar
            def _(act):
                act_program(act)

            @block.vector
            def _(dve):
                dve_program(dve)

            @block.tensor
            def _(pe):
                pe_program(pe)


_OUTS = [((1, SEQ, D), "y_prompt"), ((NB, NQ, D), "y_sample"), ((1, SEQ, 4, NKV, HD), "kv_prompt"),
         ((NB, NQ, 4, NKV, HD), "kv_sample"), ((1, SEQ, 2, NKV, HD), "win_prompt"),
         ((NB, WIN, 2, NKV, HD), "win_sample"), ((1, 1, HIST, D), "conv_prompt"), ((1, NB, HIST, D), "conv_sample")]


def kernel(**inputs):
    import concourse.bacc as bacc
    from concourse.bass_utils import run_bass_kernel_spmd

    nc = bacc.Bacc("TRN2", target_bir_lowering=False, num_devices=1)
    table, where = host_constants()
    arrays, ins = {}, {}
    for name, a in {**inputs, "const": table}.items():
        a = np.ascontiguousarray(a)
        arrays[f"in_{name}"] = a
        ins[name] = nc.dram_tensor(f"in_{name}", a.shape, mybir.dt.from_np(a.dtype), kind="ExternalInput").ap()
    outs = [nc.dram_tensor(f"out_{name}", list(shape), F32, kind="ExternalOutput").ap() for shape, name in _OUTS]
    program(nc, ins, outs, where)
    r = run_bass_kernel_spmd(nc, [arrays], core_ids=[0])
    return tuple(r.results[0][f"out_{name}"] for _, name in _OUTS)
```
